# Optimizing a Trainium2 kernel written in Bass

```python
import math
import jax, jax.numpy as jnp
from jax import lax
import numpy as np
import jax
import jax.numpy as jnp

D_MODEL = 1024
BATCH = 1
SEQ = 256
DEPTH = 4

N_MIXERS = 3
D_INNER = D_MODEL
PLE_DIM = 256
CONV_WIDTH = 3
SSM_GROUP = 16
SSM_STATE = 64
SSM_GROUPS = D_INNER // SSM_GROUP
DT_MIN = 1e-3
DT_MAX = 1e-1
RWKV_HEAD = 64
RWKV_HEADS = D_INNER // RWKV_HEAD
DECAY_LORA = 64
ICLR_LORA = 64
RWKV_GN_EPS = 64e-5
LN_EPS = 1e-5
DN_ALPHA = (2 * DEPTH) ** 0.25
DN_BETA = (8 * DEPTH) ** -0.25
N_CONV = (DEPTH + 2) // 3
N_SSM = (DEPTH + 1) // 3
N_RWKV = DEPTH // 3


def layer_norm(h, g, b, eps=LN_EPS):
    h32 = h.astype(jnp.float32)
    mu = h32.mean(-1, keepdims=True)
    var = jnp.square(h32 - mu).mean(-1, keepdims=True)
    return ((h32 - mu) * lax.rsqrt(var + eps) * g.astype(jnp.float32) + b.astype(jnp.float32)).astype(h.dtype)

def token_shift(x):
    return jnp.pad(x, ((0, 0), (1, 0), (0, 0)))[:, :-1]

def short_conv_mixer(x, w_in, conv_k, w_out):
    bg, cg, h, z = jnp.split(x @ w_in, 4, axis=-1)
    u = cg * h
    conv = lax.conv_general_dilated(
        u, conv_k[:, None, :].astype(u.dtype), window_strides=(1,),
        padding=[(CONV_WIDTH - 1, 0)], dimension_numbers=("NWC", "WIO", "NWC"),
        feature_group_count=D_INNER)
    return (bg * conv * jax.nn.silu(z)) @ w_out

def _ssm_combine(left, right):
    a_l, b_l = left
    a_r, b_r = right
    return a_r * a_l, a_r * b_l + b_r

def s5_mixer(x, w_in, lam_re, lam_im, log_dt, b_re, b_im, c_re, c_im, d_skip, w_glu, b_glu, w_out):
    f32 = jnp.float32
    u, z = jnp.split(x @ w_in, 2, axis=-1)
    bsz, seqlen, _ = u.shape
    ug = u.astype(f32).reshape(bsz, seqlen, SSM_GROUPS, SSM_GROUP)
    lam = lax.complex(lam_re.astype(f32), lam_im.astype(f32))
    dt = jnp.exp(log_dt.astype(f32))[:, None]
    a_bar = jnp.exp(lam * dt)
    b_mat = lax.complex(b_re.astype(f32), b_im.astype(f32))
    b_bar = ((a_bar - 1.0) / lam)[..., None] * b_mat
    c_mat = lax.complex(c_re.astype(f32), c_im.astype(f32))
    bu = jnp.einsum("blgh,gph->blgp", ug, b_bar)
    a_seq = jnp.broadcast_to(a_bar, bu.shape)
    states = lax.associative_scan(_ssm_combine, (a_seq, bu), axis=1)[1]
    y = jnp.einsum("blgp,ghp->blgh", states, c_mat).real + d_skip.astype(f32).reshape(SSM_GROUPS, SSM_GROUP) * ug
    y = jax.nn.gelu(y.reshape(bsz, seqlen, D_INNER).astype(x.dtype))
    y = y * jax.nn.sigmoid(y @ w_glu + b_glu)
    return (y * jax.nn.silu(z)) @ w_out

def _rwkv_step(state, inp):
    r_t, w_t, k_t, v_t, kk_t, a_t = inp
    sa = jnp.einsum("bhvk,bhk->bhv", state, -kk_t)
    state = (state * w_t[:, :, None, :] + sa[..., None] * (kk_t * a_t)[:, :, None, :]
             + v_t[..., None] * k_t[:, :, None, :])
    out = jnp.einsum("bhvk,bhk->bhv", state, r_t)
    return state, out

def rwkv7_mixer(x, mu, w_rkvz, w0, w1, w2, a0, a1, a2, k_k, k_a, r_k, lnx_g, lnx_b, w_out):
    f32 = jnp.float32
    bsz, seqlen, _ = x.shape
    dx = token_shift(x) - x
    xs = x[None] + dx[None] * mu[:, None, None, :]
    r, k, v, z = jnp.einsum("nbld,nde->nble", xs[:4], w_rkvz)
    xw, xa = xs[4], xs[5]
    w_log = -jax.nn.softplus(-(w0 + jnp.tanh(xw @ w1) @ w2)) - 0.5
    decay = jnp.exp(-jnp.exp(w_log.astype(f32)))
    a = jax.nn.sigmoid(a0 + (xa @ a1) @ a2).astype(f32)
    heads = lambda t: t.astype(f32).reshape(bsz, seqlen, RWKV_HEADS, RWKV_HEAD)
    kk = heads(k * k_k)
    kk = kk / jnp.maximum(jnp.linalg.norm(kk, axis=-1, keepdims=True), 1e-12)
    k = heads(k * (1.0 + (a.astype(k.dtype) - 1.0) * k_a))
    r, v, decay, a = heads(r), heads(v), heads(decay), heads(a)
    seq_first = lambda t: jnp.moveaxis(t, 1, 0)
    s0 = jnp.zeros((bsz, RWKV_HEADS, RWKV_HEAD, RWKV_HEAD), f32)
    _, out = lax.scan(_rwkv_step, s0, tuple(seq_first(t) for t in (r, decay, k, v, kk, a)))
    out = jnp.moveaxis(out, 0, 1)
    mu_o = out.mean(-1, keepdims=True)
    var_o = jnp.square(out - mu_o).mean(-1, keepdims=True)
    out = ((out - mu_o) * lax.rsqrt(var_o + RWKV_GN_EPS)).reshape(bsz, seqlen, D_INNER)
    out = out * lnx_g.astype(f32) + lnx_b.astype(f32)
    bonus = jnp.sum(r * k * r_k.astype(f32), axis=-1, keepdims=True) * v
    out = (out + bonus.reshape(bsz, seqlen, D_INNER)).astype(x.dtype)
    return (out * jax.nn.silu(z)) @ w_out

def first_inputs(seed: int = 0) -> dict:
    key = jax.random.key(seed)
    ks = iter(jax.random.split(key, 48))
    nrm = lambda shape, s: jax.random.normal(next(ks), shape, jnp.float32) * s
    D, E, G, P, H, N = D_MODEL, D_INNER, SSM_GROUPS, SSM_STATE, RWKV_HEADS, RWKV_HEAD
    ramp = jnp.linspace(0.0, 1.0, E, dtype=jnp.float32) ** 0.85
    inp = {}
    inp["x"] = nrm((BATCH, SEQ, D), 1.0)
    inp["p"] = nrm((DEPTH, BATCH, SEQ, PLE_DIM), 1.0)
    inp["conv_w_in"] = nrm((N_CONV, D, 4 * E), D ** -0.5)
    inp["conv_k"] = nrm((N_CONV, CONV_WIDTH, E), CONV_WIDTH ** -0.5)
    inp["conv_w_out"] = nrm((N_CONV, E, D), E ** -0.5 * DN_BETA)
    inp["ssm_w_in"] = nrm((N_SSM, D, 2 * E), D ** -0.5)
    inp["ssm_lam_re"] = -0.5 + nrm((N_SSM, G, P), 0.01)
    inp["ssm_lam_im"] = math.pi * jnp.arange(P, dtype=jnp.float32) + nrm((N_SSM, G, P), 0.01)
    inp["ssm_log_dt"] = jax.random.uniform(next(ks), (N_SSM, G), jnp.float32, math.log(DT_MIN), math.log(DT_MAX))
    inp["ssm_b_re"] = nrm((N_SSM, G, P, SSM_GROUP), (2 * SSM_GROUP) ** -0.5)
    inp["ssm_b_im"] = nrm((N_SSM, G, P, SSM_GROUP), (2 * SSM_GROUP) ** -0.5)
    inp["ssm_c_re"] = nrm((N_SSM, G, SSM_GROUP, P), (2 * P) ** -0.5)
    inp["ssm_c_im"] = nrm((N_SSM, G, SSM_GROUP, P), (2 * P) ** -0.5)
    inp["ssm_d"] = nrm((N_SSM, E), 1.0)
    inp["ssm_w_glu"] = nrm((N_SSM, E, E), E ** -0.5)
    inp["ssm_b_glu"] = nrm((N_SSM, E), 0.01)
    inp["ssm_w_out"] = nrm((N_SSM, E, D), E ** -0.5 * DN_BETA)
    inp["rwkv_mu"] = jax.random.uniform(next(ks), (N_RWKV, 6, D), jnp.float32)
    inp["rwkv_w_rkvz"] = nrm((N_RWKV, 4, D, E), D ** -0.5)
    inp["rwkv_w0"] = -6.0 + 5.0 * ramp + nrm((N_RWKV, E), 0.1)
    inp["rwkv_w1"] = nrm((N_RWKV, D, DECAY_LORA), D ** -0.5)
    inp["rwkv_w2"] = nrm((N_RWKV, DECAY_LORA, E), 0.1 * DECAY_LORA ** -0.5)
    inp["rwkv_a0"] = nrm((N_RWKV, E), 0.1)
    inp["rwkv_a1"] = nrm((N_RWKV, D, ICLR_LORA), D ** -0.5)
    inp["rwkv_a2"] = nrm((N_RWKV, ICLR_LORA, E), 0.1 * ICLR_LORA ** -0.5)
    inp["rwkv_k_k"] = 0.85 + nrm((N_RWKV, E), 0.05)
    inp["rwkv_k_a"] = 1.0 + nrm((N_RWKV, E), 0.05)
    inp["rwkv_r_k"] = nrm((N_RWKV, H, N), 0.1)
    inp["rwkv_lnx_g"] = 1.0 + nrm((N_RWKV, E), 0.05)
    inp["rwkv_lnx_b"] = nrm((N_RWKV, E), 0.01)
    inp["rwkv_w_out"] = nrm((N_RWKV, E, D), E ** -0.5 * DN_BETA)
    inp["ple_proj"] = nrm((DEPTH, PLE_DIM, D), PLE_DIM ** -0.5)
    inp["ple_gate"] = nrm((DEPTH, D, D), D ** -0.5)
    inp["ln_g"] = 1.0 + nrm((DEPTH, D), 0.05)
    inp["ln_b"] = nrm((DEPTH, D), 0.01)
    return inp

def first_block(x, p, conv_w_in, conv_k, conv_w_out,
              ssm_w_in, ssm_lam_re, ssm_lam_im, ssm_log_dt, ssm_b_re, ssm_b_im, ssm_c_re, ssm_c_im,
              ssm_d, ssm_w_glu, ssm_b_glu, ssm_w_out,
              rwkv_mu, rwkv_w_rkvz, rwkv_w0, rwkv_w1, rwkv_w2, rwkv_a0, rwkv_a1, rwkv_a2,
              rwkv_k_k, rwkv_k_a, rwkv_r_k, rwkv_lnx_g, rwkv_lnx_b, rwkv_w_out,
              ple_proj, ple_gate, ln_g, ln_b):
    for i in range(DEPTH):
        kind, j = i % N_MIXERS, i // N_MIXERS
        if kind == 0:
            y = short_conv_mixer(x, conv_w_in[j], conv_k[j], conv_w_out[j])
        elif kind == 1:
            y = s5_mixer(x, ssm_w_in[j], ssm_lam_re[j], ssm_lam_im[j], ssm_log_dt[j],
                         ssm_b_re[j], ssm_b_im[j], ssm_c_re[j], ssm_c_im[j], ssm_d[j],
                         ssm_w_glu[j], ssm_b_glu[j], ssm_w_out[j])
        else:
            y = rwkv7_mixer(x, rwkv_mu[j], rwkv_w_rkvz[j], rwkv_w0[j], rwkv_w1[j], rwkv_w2[j],
                            rwkv_a0[j], rwkv_a1[j], rwkv_a2[j], rwkv_k_k[j], rwkv_k_a[j],
                            rwkv_r_k[j], rwkv_lnx_g[j], rwkv_lnx_b[j], rwkv_w_out[j])
        r = DN_ALPHA * x + y
        r = r + (p[i] @ ple_proj[i]) * jax.nn.sigmoid(r @ ple_gate[i])
        x = layer_norm(r, ln_g[i], ln_b[i])
    return x


DEPTH_2 = 2

GRID_W = 64
CTX_LEN = 256
HEAD_DIM = 64
Q_BLOCK = 128
EPS = 1e-6
ROPE_THETA = 10000.0
D_FF = 2816
ADA_STD = 0.02
N_MOD = 9

A_HEADS = 8
A_KV_HEADS = 2
B_HEADS = 8
B_NOPE = 64
B_ROPE = 32
B_VDIM = 64
B_KV_RANK = 256
B_QK = B_NOPE + B_ROPE
C_HEADS = 8
C_DK = 64
C_DV = 64
C_CHUNK = 64
D_HEADS = 8
D_WIN_H = 8
D_WIN_W = 16

N_EVEN = (DEPTH_2 + 1) // 2
N_ODD = DEPTH_2 // 2

A_QW = A_HEADS * HEAD_DIM
A_KVW = A_KV_HEADS * HEAD_DIM
B_QW = B_HEADS * B_QK
AB_IN = A_QW + 2 * A_KVW + B_QW + B_KV_RANK + B_ROPE
AB_SPLITS = (A_QW, A_QW + A_KVW, A_QW + 2 * A_KVW, A_QW + 2 * A_KVW + B_QW, A_QW + 2 * A_KVW + B_QW + B_KV_RANK)
AB_OUT = A_QW + B_HEADS * B_VDIM

C_W = C_HEADS * C_DK
C_VW = C_HEADS * C_DV
D_W = D_HEADS * HEAD_DIM
CD_IN = 3 * C_W + 2 * C_VW + 3 * D_W
CD_SPLITS = (C_W, 2 * C_W, 3 * C_W, 3 * C_W + C_VW, 3 * C_W + 2 * C_VW, 3 * C_W + 2 * C_VW + D_W, 3 * C_W + 2 * C_VW + 2 * D_W)
CD_OUT = C_VW + D_W


def rms_norm(x, g):
    xf = x.astype(jnp.float32)
    y = xf * lax.rsqrt(jnp.mean(xf * xf, axis=-1, keepdims=True) + EPS)
    return (y * g.astype(jnp.float32)).astype(x.dtype)

def modulate(h, shift, scale):
    return h * (1 + scale[:, None, :]) + shift[:, None, :]

def swiglu(h, w1, w3, w2):
    return (jax.nn.silu(h @ w1) * (h @ w3)) @ w2

def half_ffn(h, g, shift, scale, gate, w1, w3, w2):
    return h + 0.5 * gate[:, None, :] * swiglu(modulate(rms_norm(h, g), shift, scale), w1, w3, w2)

def rope_1d(pos, dim):
    inv = ROPE_THETA ** (-jnp.arange(0, dim, 2, dtype=jnp.float32) / dim)
    ang = pos.astype(jnp.float32)[:, None] * inv[None, :]
    ang = jnp.concatenate([ang, ang], axis=-1)
    return jnp.cos(ang), jnp.sin(ang)

def axial_rope_tables(n_tok, dim):
    t = jnp.arange(n_tok, dtype=jnp.int32)
    cos_r, sin_r = rope_1d(t // GRID_W, dim // 2)
    cos_c, sin_c = rope_1d(t % GRID_W, dim // 2)
    return jnp.concatenate([cos_r, cos_c], axis=-1), jnp.concatenate([sin_r, sin_c], axis=-1)

def _rotate_half(u):
    u1, u2 = jnp.split(u, 2, axis=-1)
    return jnp.concatenate([-u2, u1], axis=-1)

def apply_axial_rope(x, cos, sin):
    h = x.shape[-1] // 2
    rot = jnp.concatenate([_rotate_half(x[..., :h]), _rotate_half(x[..., h:])], axis=-1)
    return x * cos[None, :, None, :].astype(x.dtype) + rot * sin[None, :, None, :].astype(x.dtype)

def blocked_attention(q, k, v, scale):
    b, s, hkv, g, d = q.shape
    nb = s // Q_BLOCK
    qb = jnp.moveaxis(q.reshape(b, nb, Q_BLOCK, hkv, g, d), 1, 0)

    def one_block(qi):
        sc = jnp.einsum('bqhgd,bkhd->bhgqk', qi, k, preferred_element_type=jnp.float32) * scale
        p = jax.nn.softmax(sc, axis=-1).astype(v.dtype)
        return jnp.einsum('bhgqk,bkhd->bqhgd', p, v)

    out = lax.map(one_block, qb)
    return jnp.moveaxis(out, 0, 1).reshape(b, s, hkv * g * v.shape[-1])

def mixer_ab(hx, hc, w_in, a_qn, a_kn, b_qn, b_kn, b_kvn, b_wukv, w_out, with_ctx):
    b, s, _ = hx.shape
    grp = A_HEADS // A_KV_HEADS
    cos_a, sin_a = axial_rope_tables(s, HEAD_DIM)
    cos_b, sin_b = axial_rope_tables(s, B_ROPE)

    def project(h, rotary):
        n = h.shape[1]
        aq, ak, av, bq, bkv, bkr = jnp.split(h @ w_in, AB_SPLITS, axis=-1)
        aq = rms_norm(aq.reshape(b, n, A_HEADS, HEAD_DIM), a_qn)
        ak = rms_norm(ak.reshape(b, n, A_KV_HEADS, HEAD_DIM), a_kn)
        av = av.reshape(b, n, A_KV_HEADS, HEAD_DIM)
        kv = (rms_norm(bkv, b_kvn) @ b_wukv).reshape(b, n, B_HEADS, B_NOPE + B_VDIM)
        bk_rope = jnp.broadcast_to(bkr[:, :, None, :], (b, n, B_HEADS, B_ROPE))
        bq = rms_norm(bq.reshape(b, n, B_HEADS, B_QK), b_qn)
        bk = rms_norm(jnp.concatenate([kv[..., :B_NOPE], bk_rope], axis=-1), b_kn)
        bv = kv[..., B_NOPE:]
        if rotary:
            aq = apply_axial_rope(aq, cos_a, sin_a)
            ak = apply_axial_rope(ak, cos_a, sin_a)
            bq = jnp.concatenate([bq[..., :B_NOPE], apply_axial_rope(bq[..., B_NOPE:], cos_b, sin_b)], axis=-1)
            bk = jnp.concatenate([bk[..., :B_NOPE], apply_axial_rope(bk[..., B_NOPE:], cos_b, sin_b)], axis=-1)
        return aq.reshape(b, n, A_KV_HEADS, grp, HEAD_DIM), ak, av, bq[:, :, :, None, :], bk, bv

    qa, ka, va, qb, kb, vb = project(hx, True)
    qa_c, ka_c, va_c, qb_c, kb_c, vb_c = project(hc, False)
    y_x = jnp.concatenate([
        blocked_attention(qa, jnp.concatenate([ka, ka_c], axis=1), jnp.concatenate([va, va_c], axis=1), HEAD_DIM ** -0.5),
        blocked_attention(qb, jnp.concatenate([kb, kb_c], axis=1), jnp.concatenate([vb, vb_c], axis=1), B_QK ** -0.5),
    ], axis=-1) @ w_out
    if not with_ctx:
        return y_x, None
    y_c = jnp.concatenate([
        blocked_attention(qa_c, ka_c, va_c, HEAD_DIM ** -0.5),
        blocked_attention(qb_c, kb_c, vb_c, B_QK ** -0.5),
    ], axis=-1) @ w_out
    return y_x, y_c

def hgrn_chunk_scan(q, k, v, g, s0, with_output):
    b, h, n, dk = q.shape
    nc = n // C_CHUNK

    def chunks(t):
        return jnp.moveaxis(t.reshape(b, h, nc, C_CHUNK, t.shape[-1]), 2, 0)

    tri = jnp.tril(jnp.ones((C_CHUNK, C_CHUNK), dtype=bool))[:, :, None]

    def step(state, inp):
        qi, ki, vi, gi = inp
        gcum = jnp.cumsum(gi, axis=2)
        glast = gcum[:, :, -1, :]
        new_state = jnp.exp(glast)[..., None] * state + jnp.einsum('bhck,bhcv->bhkv', ki * jnp.exp(glast[:, :, None, :] - gcum), vi)
        if not with_output:
            return new_state, None
        o_inter = jnp.einsum('bhtk,bhkv->bhtv', qi * jnp.exp(gcum), state)
        decay = jnp.exp(jnp.where(tri, gcum[:, :, :, None, :] - gcum[:, :, None, :, :], -jnp.inf))
        attn = jnp.einsum('bhtk,bhsk,bhtsk->bhts', qi, ki, decay)
        return new_state, o_inter + jnp.einsum('bhts,bhsv->bhtv', attn, vi)

    s_fin, o = lax.scan(step, s0, (chunks(q), chunks(k), chunks(v), chunks(g)))
    if with_output:
        o = jnp.moveaxis(o, 0, 2).reshape(b, h, n, v.shape[-1])
    return s_fin, o

def neighbourhood_attention(q, k, v, k_ctx, v_ctx, rpb):
    b, s, h, d = q.shape
    rows = s // GRID_W
    kh = min(D_WIN_H, rows)
    kw = D_WIN_W
    n_win = kh * kw
    cols = np.arange(GRID_W)
    col_idx = np.clip(cols - kw // 2, 0, GRID_W - kw)[:, None] + np.arange(kw)[None, :]
    col_rel = col_idx - cols[:, None] + (D_WIN_W - 1)
    rpb_cols = rpb[:, :, col_rel]
    kg = k.reshape(b, rows, GRID_W, h, d)
    vg = v.reshape(b, rows, GRID_W, h, d)
    q_rows = jnp.moveaxis(q.reshape(b, rows, GRID_W, h, d), 1, 0)
    scale = d ** -0.5

    def one_row(args):
        r, q_row = args
        rs = jnp.clip(r - kh // 2, 0, rows - kh)
        k_win = lax.dynamic_slice_in_dim(kg, rs, kh, axis=1)[:, :, col_idx]
        v_win = lax.dynamic_slice_in_dim(vg, rs, kh, axis=1)[:, :, col_idx]
        row_rel = rs + jnp.arange(kh) - r + (D_WIN_H - 1)
        bias = jnp.transpose(jnp.take(rpb_cols, row_rel, axis=1), (0, 2, 1, 3))
        s_win = jnp.einsum('bchd,brcwhd->bhcrw', q_row, k_win, preferred_element_type=jnp.float32) * scale + bias[None].astype(jnp.float32)
        s_ctx = jnp.einsum('bchd,bnhd->bhcn', q_row, k_ctx, preferred_element_type=jnp.float32) * scale
        p = jax.nn.softmax(jnp.concatenate([s_win.reshape(b, h, GRID_W, n_win), s_ctx], axis=-1), axis=-1).astype(v.dtype)
        return (jnp.einsum('bhcrw,brcwhd->bchd', p[..., :n_win].reshape(b, h, GRID_W, kh, kw), v_win)
                + jnp.einsum('bhcn,bnhd->bchd', p[..., n_win:], v_ctx))

    out = lax.map(one_row, (jnp.arange(rows, dtype=jnp.int32), q_rows))
    return jnp.moveaxis(out, 0, 1).reshape(b, s, h * d)

def mixer_cd(hx, hc, w_in, lb, c_gn, d_qn, d_kn, d_rpb, w_out, with_ctx):
    b, s, _ = hx.shape
    f32 = jnp.float32
    px = jnp.split(hx @ w_in, CD_SPLITS, axis=-1)
    pc = jnp.split(hc @ w_in, CD_SPLITS, axis=-1)

    def heads_first(t, dh):
        return jnp.moveaxis(t.reshape(b, t.shape[1], -1, dh), 2, 1)

    def hgrn_inputs(p, direction):
        z = p[1 + direction].astype(f32)
        lbd = lb[direction]
        logf = jnp.logaddexp(jnp.log(lbd), jnp.log1p(-lbd) + jax.nn.log_sigmoid(z))
        key_in = -jnp.expm1(logf)
        t = (heads_first(jax.nn.silu(p[0].astype(f32)), C_DK), heads_first(key_in, C_DK),
             heads_first(p[3].astype(f32), C_DV), heads_first(logf, C_DK))
        if direction == 1:
            t = tuple(jnp.flip(u, axis=2) for u in t)
        return t

    def hgrn_out(o, p):
        o = jnp.moveaxis(o, 1, 2)
        n = o.shape[1]
        gate = p[4].reshape(b, n, C_HEADS, C_DV)
        return (rms_norm(o, c_gn).astype(gate.dtype) * jax.nn.silu(gate)).reshape(b, n, C_VW)

    s0 = jnp.zeros((b, C_HEADS, C_DK, C_DV), f32)
    qf, kf, vf, gf = hgrn_inputs(pc, 0)
    s_cf, o_cf = hgrn_chunk_scan(qf, kf, vf, gf, s0, with_ctx)
    qf, kf, vf, gf = hgrn_inputs(px, 0)
    _, o_xf = hgrn_chunk_scan(qf, kf, vf, gf, s_cf, True)
    qb_, kb_, vb_, gb_ = hgrn_inputs(pc, 1)
    s_cb, o_cb = hgrn_chunk_scan(qb_, kb_, vb_, gb_, s0, with_ctx)
    qb_, kb_, vb_, gb_ = hgrn_inputs(px, 1)
    _, o_xb = hgrn_chunk_scan(qb_, kb_, vb_, gb_, s_cb, True)
    o_lat = o_xf + jnp.flip(o_xb, axis=2)

    def d_qkv(p):
        n = p[5].shape[1]
        return (rms_norm(p[5].reshape(b, n, D_HEADS, HEAD_DIM), d_qn),
                rms_norm(p[6].reshape(b, n, D_HEADS, HEAD_DIM), d_kn),
                p[7].reshape(b, n, D_HEADS, HEAD_DIM))

    dq, dk, dv = d_qkv(px)
    dq_c, dk_c, dv_c = d_qkv(pc)
    y_x = jnp.concatenate([hgrn_out(o_lat, px), neighbourhood_attention(dq, dk, dv, dk_c, dv_c, d_rpb)], axis=-1) @ w_out
    if not with_ctx:
        return y_x, None
    o_ctx = o_cf + jnp.flip(o_cb, axis=2)
    y_c = jnp.concatenate([hgrn_out(o_ctx, pc), blocked_attention(dq_c[:, :, :, None, :], dk_c, dv_c, HEAD_DIM ** -0.5)], axis=-1) @ w_out
    return y_x, y_c

def second_inputs(seed: int = 0) -> dict:
    key = jax.random.key(seed)
    ks = jax.random.split(key, 26)

    def nrm(k, shape, scale):
        return jax.random.normal(k, shape, jnp.float32) * scale

    def gain(k, shape):
        return 1.0 + 0.05 * jax.random.normal(k, shape, jnp.float32)

    return {
        'x': nrm(ks[0], (BATCH, SEQ, D_MODEL), 1.0),
        'c': nrm(ks[1], (BATCH, D_MODEL), 1.0),
        'ctx': nrm(ks[2], (BATCH, CTX_LEN, D_MODEL), 1.0),
        'c_ctx': nrm(ks[3], (D_MODEL,), 1.0),
        'norm_g': gain(ks[4], (DEPTH_2, 3, D_MODEL)),
        'ada_w': nrm(ks[5], (DEPTH_2, D_MODEL, N_MOD * D_MODEL), ADA_STD),
        'ada_b': nrm(ks[6], (DEPTH_2, N_MOD * D_MODEL), 0.02),
        'ffn_w1': nrm(ks[7], (DEPTH_2, 2, D_MODEL, D_FF), D_MODEL ** -0.5),
        'ffn_w3': nrm(ks[8], (DEPTH_2, 2, D_MODEL, D_FF), D_MODEL ** -0.5),
        'ffn_w2': nrm(ks[9], (DEPTH_2, 2, D_FF, D_MODEL), D_FF ** -0.5),
        'ab_w_in': nrm(ks[10], (N_EVEN, D_MODEL, AB_IN), D_MODEL ** -0.5),
        'ab_a_qn': gain(ks[11], (N_EVEN, HEAD_DIM)),
        'ab_a_kn': gain(ks[12], (N_EVEN, HEAD_DIM)),
        'ab_b_qn': gain(ks[13], (N_EVEN, B_QK)),
        'ab_b_kn': gain(ks[14], (N_EVEN, B_QK)),
        'ab_b_kvn': gain(ks[15], (N_EVEN, B_KV_RANK)),
        'ab_b_wukv': nrm(ks[16], (N_EVEN, B_KV_RANK, B_HEADS * (B_NOPE + B_VDIM)), B_KV_RANK ** -0.5),
        'ab_w_out': nrm(ks[17], (N_EVEN, AB_OUT, D_MODEL), AB_OUT ** -0.5),
        'cd_w_in': nrm(ks[18], (N_ODD, D_MODEL, CD_IN), D_MODEL ** -0.5),
        'hgrn_lb': nrm(ks[19], (DEPTH_2, 2, C_W), 0.5),
        'cd_c_gn': gain(ks[20], (N_ODD, C_DV)),
        'cd_d_qn': gain(ks[21], (N_ODD, HEAD_DIM)),
        'cd_d_kn': gain(ks[22], (N_ODD, HEAD_DIM)),
        'cd_d_rpb': nrm(ks[23], (N_ODD, D_HEADS, 2 * D_WIN_H - 1, 2 * D_WIN_W - 1), 0.5),
        'cd_w_out': nrm(ks[24], (N_ODD, CD_OUT, D_MODEL), CD_OUT ** -0.5),
    }

def second_block(x, c, ctx, c_ctx, norm_g, ada_w, ada_b, ffn_w1, ffn_w3, ffn_w2, ab_w_in, ab_a_qn, ab_a_kn, ab_b_qn, ab_b_kn, ab_b_kvn, ab_b_wukv, ab_w_out, cd_w_in, hgrn_lb, cd_c_gn, cd_d_qn, cd_d_kn, cd_d_rpb, cd_w_out):
    lb_all = jnp.cumsum(jax.nn.softmax(hgrn_lb.astype(jnp.float32), axis=0), axis=0)
    lb_all = lb_all - lb_all[:1]
    for l in range(DEPTH_2):
        last = l == DEPTH_2 - 1
        i = l // 2
        mod_x = jnp.split(jax.nn.silu(c) @ ada_w[l] + ada_b[l], N_MOD, axis=-1)
        mod_c = jnp.split(jax.nn.silu(c_ctx)[None, :] @ ada_w[l] + ada_b[l], N_MOD, axis=-1)
        x = half_ffn(x, norm_g[l, 0], mod_x[0], mod_x[1], mod_x[2], ffn_w1[l, 0], ffn_w3[l, 0], ffn_w2[l, 0])
        ctx = half_ffn(ctx, norm_g[l, 0], mod_c[0], mod_c[1], mod_c[2], ffn_w1[l, 0], ffn_w3[l, 0], ffn_w2[l, 0])
        hx = modulate(rms_norm(x, norm_g[l, 1]), mod_x[3], mod_x[4])
        hc = modulate(rms_norm(ctx, norm_g[l, 1]), mod_c[3], mod_c[4])
        if l % 2 == 0:
            y_x, y_c = mixer_ab(hx, hc, ab_w_in[i], ab_a_qn[i], ab_a_kn[i], ab_b_qn[i], ab_b_kn[i], ab_b_kvn[i], ab_b_wukv[i], ab_w_out[i], not last)
        else:
            y_x, y_c = mixer_cd(hx, hc, cd_w_in[i], lb_all[l], cd_c_gn[i], cd_d_qn[i], cd_d_kn[i], cd_d_rpb[i], cd_w_out[i], not last)
        x = x + mod_x[5][:, None, :] * y_x
        x = half_ffn(x, norm_g[l, 2], mod_x[6], mod_x[7], mod_x[8], ffn_w1[l, 1], ffn_w3[l, 1], ffn_w2[l, 1])
        if not last:
            ctx = ctx + mod_c[5][:, None, :] * y_c
            ctx = half_ffn(ctx, norm_g[l, 2], mod_c[6], mod_c[7], mod_c[8], ffn_w1[l, 1], ffn_w3[l, 1], ffn_w2[l, 1])
    return x


def setup_inputs(seed=0):
    out = dict(first_inputs(seed))
    for name, value in second_inputs(seed + 1).items():
        if name != "x":
            out[name + "_2"] = value
    return out


def reference(
    x, p, conv_w_in, conv_k, conv_w_out, ssm_w_in, ssm_lam_re, ssm_lam_im, ssm_log_dt, ssm_b_re,
    ssm_b_im, ssm_c_re, ssm_c_im, ssm_d, ssm_w_glu, ssm_b_glu, ssm_w_out, rwkv_mu, rwkv_w_rkvz,
    rwkv_w0, rwkv_w1, rwkv_w2, rwkv_a0, rwkv_a1, rwkv_a2, rwkv_k_k, rwkv_k_a, rwkv_r_k,
    rwkv_lnx_g, rwkv_lnx_b, rwkv_w_out, ple_proj, ple_gate, ln_g, ln_b, c_2, ctx_2, c_ctx_2,
    norm_g_2, ada_w_2, ada_b_2, ffn_w1_2, ffn_w3_2, ffn_w2_2, ab_w_in_2, ab_a_qn_2, ab_a_kn_2,
    ab_b_qn_2, ab_b_kn_2, ab_b_kvn_2, ab_b_wukv_2, ab_w_out_2, cd_w_in_2, hgrn_lb_2, cd_c_gn_2,
    cd_d_qn_2, cd_d_kn_2, cd_d_rpb_2, cd_w_out_2,
):
    x = first_block(
        x, p, conv_w_in, conv_k, conv_w_out, ssm_w_in, ssm_lam_re, ssm_lam_im, ssm_log_dt,
        ssm_b_re, ssm_b_im, ssm_c_re, ssm_c_im, ssm_d, ssm_w_glu, ssm_b_glu, ssm_w_out, rwkv_mu,
        rwkv_w_rkvz, rwkv_w0, rwkv_w1, rwkv_w2, rwkv_a0, rwkv_a1, rwkv_a2, rwkv_k_k, rwkv_k_a,
        rwkv_r_k, rwkv_lnx_g, rwkv_lnx_b, rwkv_w_out, ple_proj, ple_gate, ln_g, ln_b,
    )
    return second_block(
        x, c_2, ctx_2, c_ctx_2, norm_g_2, ada_w_2, ada_b_2, ffn_w1_2, ffn_w3_2, ffn_w2_2,
        ab_w_in_2, ab_a_qn_2, ab_a_kn_2, ab_b_qn_2, ab_b_kn_2, ab_b_kvn_2, ab_b_wukv_2,
        ab_w_out_2, cd_w_in_2, hgrn_lb_2, cd_c_gn_2, cd_d_qn_2, cd_d_kn_2, cd_d_rpb_2,
        cd_w_out_2,
    )


_drawn_inputs = setup_inputs


def setup_inputs(seed=0):
    import zlib

    import numpy as np

    out = dict(_drawn_inputs(seed))
    spreads = {}
    factors = {'ssm_lam_re': 64.0,
     'ssm_lam_im': 64.0,
     'ssm_log_dt': 64.0,
     'ssm_b_re': 64.0,
     'ssm_b_im': 64.0,
     'ssm_c_re': 64.0,
     'ssm_c_im': 64.0,
     'ssm_w_glu': 3.661,
     'ssm_b_glu': 8.0,
     'rwkv_w1': 8.0,
     'rwkv_w2': 8.0,
     'rwkv_a0': 8.0,
     'rwkv_a1': 8.0,
     'rwkv_a2': 8.0,
     'rwkv_k_k': 8.0,
     'rwkv_k_a': 8.0,
     'rwkv_lnx_g': 8.0,
     'rwkv_lnx_b': 8.0,
     'ab_a_qn_2': 8.0,
     'ab_a_kn_2': 8.0,
     'ab_b_qn_2': 8.0,
     'ab_b_kn_2': 8.0,
     'ab_b_kvn_2': 8.0,
     'hgrn_lb_2': 5.909,
     'cd_c_gn_2': 5.783,
     'cd_d_qn_2': 8.0,
     'cd_d_kn_2': 8.0,
     'cd_d_rpb_2': 23.068}
    for name, (base, spread) in spreads.items():
        noise = np.random.default_rng([zlib.crc32(name.encode()), seed]).standard_normal(out[name].shape)
        drawn = base * np.exp(spread * noise) if base else spread * noise
        out[name] = jnp.asarray(drawn.astype(out[name].dtype))
    for name, factor in factors.items():
        out[name] = (out[name] * factor).astype(out[name].dtype)
    return out
```

```python
from contextlib import ExitStack

import numpy as np

import concourse.bass as bass
from concourse import mybir

F32 = mybir.dt.float32
ALU = mybir.AluOpType
ACT = mybir.ActivationFunctionType
AX = mybir.AxisListType.X
ENG = mybir.EngineType
MUL, ADD, SUB, MAX, MIN, BYP = ALU.mult, ALU.add, ALU.subtract, ALU.max, ALU.min, ALU.bypass

P = 128
D = 1024
KT = D // P
T = 256
DEPTH1, DEPTH2 = 4, 2
ALPHA = (2 * DEPTH1) ** 0.25
LN_EPS, GN_EPS, RMS_EPS = 1e-5, 64e-5, 1e-6
FF = 2816
FT = FF // P
G, NP_, GH = 64, 64, 16
SL = 8
SC = T // SL
NS = 4
SLOT = 16 * P
START = 4000
NEG = -1e30

COLS = {}


def _cols():
    at = 0
    for name, n in (("conv_k", 48), ("ssm_d", 8), ("b_glu", 8), ("mu", 48), ("w0", 8), ("a0", 8),
                    ("k_k", 8), ("k_a", 8), ("r_k", 8), ("lnx_g", 8), ("lnx_b", 8), ("ln_g", 32),
                    ("ln_b", 32), ("norm_g", 48), ("ada_b", 144), ("c", 16), ("aqn", 1), ("akn", 1),
                    ("bqn", 1), ("bqr", 1), ("bkn", 1), ("bkr", 1), ("kvn", 2), ("lb0", 8),
                    ("lb1", 8), ("cgn", 1), ("dqn", 1), ("dkn", 1), ("sgn", 1), ("half", 2), ("quart", 4)):
        COLS[name] = at
        at += n
    return at


NCOL = _cols()

STAGES = {}


def _stages():
    for l in range(DEPTH1):
        if l % 3 == 0:
            STAGES[f"conv_in{l}"] = (16, 2048)
        elif l == 1:
            STAGES["ssm_in"] = (8, 2048)
            STAGES["glu"] = (4, 2048)
        else:
            STAGES["rkvz"] = (16, 2048)
            STAGES["lora"] = (1, 2048)
        STAGES[f"out{l}"] = (4, 2048)
        STAGES[f"ple{l}"] = (8, 1280)
    STAGES["ada"] = (72, 2048)
    for l in range(DEPTH2):
        STAGES[f"f{l}0a"] = (22, 2048)
        STAGES[f"f{l}0b"] = (16, 1408)
        if l == 0:
            STAGES["ab_in"] = (7, 2048)
            STAGES["ab_av"] = (1, 1024)
            STAGES["ukv"] = (1, 2048)
            STAGES["ab_out"] = (4, 2048)
        else:
            STAGES["cd_in"] = (12, 2048)
            STAGES["cd_v"] = (4, 2048)
            STAGES["cd_out"] = (4, 2048)
        STAGES[f"f{l}1a"] = (22, 2048)
        STAGES[f"f{l}1b"] = (16, 1408)


_stages()


class Mark:

    def __init__(self, sem, key, v, loop=None):
        self.sem, self.key, self.v, self.loop = sem, key, v, loop


class Loop:
    def __init__(self, i, per, n):
        self.i, self.per, self.n, self.notes = i, per, n, {}


class Queue:

    def __init__(self, ctl, eng, sem, name):
        self.ctl, self.eng, self.sem, self.name = ctl, eng, sem, name
        self.n = START
        self.met = {}

    def now(self):
        return Mark(self.sem, self.name, self.n, self.ctl.loop)

    def wait(self, m):
        loop = self.ctl.loop
        if m is None or self.ctl.dry:
            return
        if m.loop is None or m.loop is not loop:
            v = m.v if m.loop is None else m.v + (m.loop.n - 1) * m.loop.per[m.key]
            if self.met.get(m.key, -1) >= v:
                return
            if loop is None:
                self.met[m.key] = v
            self.eng.wait_ge(m.sem, v)
        else:
            per = m.loop.per[m.key]
            assert m.v > 0
            if self.met.get((m.key, "loop"), -1) >= m.v:
                return
            self.met[(m.key, "loop")] = m.v
            self.eng.wait_ge(m.sem, loop.i * per + m.v if per else m.v)

    def do(self, make, *after):
        for m in after:
            self.wait(m)
        self.n += 1
        if not self.ctl.dry:
            make().then_inc(self.sem, 1)
        return self.now()

    def quiet(self, make, *after):
        for m in after:
            self.wait(m)
        if not self.ctl.dry:
            make()


class Control:
    def __init__(self, nc):
        self.nc, self.loop, self.dry = nc, None, False
        self.queues, self.straight = [], {}

    def note(self, name, mark):
        (self.straight if self.loop is None else self.loop.notes)[name] = mark

    def last(self, name):
        if self.dry:
            return None
        if self.loop is None:
            return self.straight.get(name)
        if name in self.loop.notes:
            return self.loop.notes[name]
        m = self.loop.before[name]
        return Mark(m.sem, m.key, m.v - self.loop.per[m.key], self.loop)

    def loop_over(self, n, engines, body):
        base = {q.name: q.n for q in self.queues}
        counts = [(c, c.n) for c in self.counters]
        self.dry, self.loop = True, Loop(0, {}, n)
        body(0)
        notes = self.loop.notes
        per = {q.name: q.n - base[q.name] for q in self.queues}
        for c, v in counts:
            per[c.key] = (c.n - v) * c.unit
            c.n = v
        for q in self.queues:
            q.n = base[q.name]
        self.dry = False
        with self.nc.Fori(0, n, engines=engines) as i:
            self.loop = Loop(i, per, n)
            self.loop.before = notes
            for q in self.queues:
                q.met = {k: v for k, v in q.met.items() if not isinstance(k, tuple)}
            body(i)
            self.straight.update(self.loop.notes)
            self.loop = None
        for q in self.queues:
            q.met = {k: v for k, v in q.met.items() if not isinstance(k, tuple)}
            q.n = base[q.name] + n * per[q.name]
        for c, v in counts:
            c.n = v + n * per[c.key] // c.unit


class Load:

    unit = 16

    def __init__(self, ctl, sem, key):
        self.ctl, self.sem, self.key, self.n = ctl, sem, key, 0
        ctl.counters.append(self)

    def start(self, q, dst, src, *after):
        for m in after:
            q.wait(m)
        self.n += 1
        if not self.ctl.dry:
            q.eng.dma_start(dst, src).then_inc(self.sem, 16)
        return Mark(self.sem, self.key, 16 * self.n, self.ctl.loop)


def bc(ap, n):
    return ap.unsqueeze(1).broadcast_to([ap.shape[0], n, ap.shape[1]])


def bc_in(ap, n):
    return ap.unsqueeze(2).broadcast_to([ap.shape[0], ap.shape[1], n])


class Arena:

    def __init__(self, tensor, size):
        self.t, self.size, self.at = tensor, size, 0

    def __call__(self, *shape):
        n = int(np.prod(shape))
        ap = self.t[:, self.at:self.at + n]
        self.at += n
        assert self.at <= self.size, (self.at, self.size)
        if len(shape) == 1:
            return ap
        names = "abcde"[:len(shape)]
        return ap.rearrange(f"p ({' '.join(names)}) -> p {' '.join(names)}",
                            **{c: s for c, s in zip(names[1:], shape[1:])})


class Machine:

    def __init__(self, nc, t, es):
        self.nc, self.t, self.es = nc, t, es
        self.ctl = ctl = Control(nc)
        ctl.counters = []
        self.P = Queue(ctl, nc.tensor, self.sem("s_pe"), "P")
        self.V = Queue(ctl, nc.vector, self.sem("s_dve"), "V")
        self.A = Queue(ctl, nc.scalar, self.sem("s_act"), "A")
        self.G = Queue(ctl, nc.gpsimd, self.sem("s_pool"), "G")
        self.S = Queue(ctl, nc.sync, self.sem("s_sp"), "S")
        ctl.queues = [self.P, self.V, self.A, self.G, self.S]
        for q in ctl.queues[:4]:
            q.eng.sem_inc(q.sem, START)
        self.slot_sem = [self.sem(f"s_slot{k}") for k in range(NS)]
        self.s_free = self.sem("s_free")
        self.P.eng.sem_inc(self.s_free, START)
        self.n, self.key, self.unit = 0, "free", 1
        ctl.counters.append(self)
        self.loaded = 0
        self.ring = self.sbuf("ring", NS, SLOT)
        self.H = self.sbuf("H", KT, 2 * T)
        self.cols = self.sbuf("cols", NCOL)
        self.ident = self.sbuf("ident", P)
        self.ones = self.sbuf("ones", P)
        self.blk64 = self.sbuf("blk64", P)
        self.mod = self.sbuf("mod", DEPTH2 * 9 * KT * 2)
        self.arena_size = 39500
        self.arena = self.sbuf("arena", self.arena_size)
        self.bank = [es.enter_context(nc.psum_tensor(f"bank{k}", [P, 512], F32)) for k in range(8)]
        self.misc = Load(ctl, self.sem("s_misc"), "misc")
        self.shuffle = Load(ctl, self.sem("s_shuffle"), "shuffle")
        self.moved = Load(ctl, self.sem("s_moved"), "moved")

    def sem(self, name):
        return self.es.enter_context(self.nc.semaphore(name))

    def sbuf(self, name, *shape):
        return self.es.enter_context(self.nc.sbuf_tensor(name, [P, *shape], F32))

    def col(self, name, k=0):
        return self.cols[:, bass.ds(k + COLS[name], 1)]

    def bounds(self, *queues):
        marks = [q.now() for q in (self.P, self.V, self.A, self.G)] + [self.freed()]
        for q in queues or (self.P, self.V, self.A, self.G, self.S):
            for m in marks:
                if not (q is self.P and m.key in ("P", "free")):
                    q.wait(m)

    def feed(self, names):
        sp = self.nc.sync
        for name in names:
            nch, width = STAGES[name]
            src, b = self.t[name], self.loaded

            def put(j, at, ahead):
                k = (b + j) % NS
                sp.wait_ge(self.s_free, ahead + (START + b + j - NS + 1))
                sp.dma_start(self.ring[:, k, 0:width], src[at, :, :].rearrange("a p n -> (a p) n")
                             if at is not j else src[j, :, :]).then_inc(self.slot_sem[k], 16)

            full = nch // NS if nch >= 2 * NS else 0
            if full:
                with self.nc.Fori(0, full, engines=[ENG.SP]) as i:
                    for j in range(NS):
                        put(j, bass.ds(i * NS + j, 1), i * NS)
            for j in range(full * NS, nch):
                put(j, j, 0)
            self.loaded += nch

    def take(self):
        n, k = self.n, self.n % NS
        loop = self.ctl.loop
        if not self.ctl.dry:
            v = 16 * (n // NS + 1)
            if loop is None:
                self.P.eng.wait_ge(self.slot_sem[k], v)
            else:
                assert loop.per["free"] % NS == 0
                self.P.eng.wait_ge(self.slot_sem[k], loop.i * (16 * loop.per["free"] // NS) + v)
        return self.ring[:, k, :]

    def freed(self):
        return Mark(self.s_free, "free", START + self.n, self.ctl.loop)

    def give(self, make):
        self.n += 1
        if not self.ctl.dry:
            make().then_inc(self.s_free, 1)
        return self.freed()

    def mm(self, out, lhsT, rhs, start, stop):
        return lambda: self.nc.tensor.matmul(out, lhsT, rhs, start=start, stop=stop)

    def product(self, out, w, nk, rhs, tile0=0, last=True, start=True, stop=True):
        m = None
        for k in range(nk):
            make = self.mm(out, w[:, (tile0 + k) * P:(tile0 + k + 1) * P], rhs(k),
                           start and k == 0, stop and k == nk - 1)
            if k < nk - 1:
                self.P.quiet(make)
            elif last:
                m = self.give(make)
            else:
                m = self.P.do(make)
        return m

    def colsum(self, out, src, nk, mat=None, after=()):
        for m in after:
            self.P.wait(m)
        mat = self.ones if mat is None else mat
        for k in range(nk):
            make = self.mm(out, mat[:, :], src(k), k == 0, k == nk - 1)
            m = self.P.do(make) if k == nk - 1 else self.P.quiet(make)
        return m

    def rstd(self, out, var, scale, eps, after):
        m = self.V.do(lambda: self.nc.vector.tensor_scalar(out, var, scale, eps, MUL, ADD), after)
        m = self.A.do(lambda: self.nc.scalar.activation(out, out, ACT.Sqrt), m)
        return self.V.do(lambda: self.nc.vector.reciprocal(out, out), m)

    def layer_norm(self, R, l, dst, tmp, after):
        P_, V, A, nc = self.P, self.V, self.A, self.nc
        dev, sq, rs = tmp(KT, T), tmp(KT, T), tmp(T)
        mean, var = self.bank[0][:, 0:T], self.bank[1][:, 0:T]
        m = self.colsum(mean, lambda k: R[:, k, :], KT, after=[after])
        m = V.do(lambda: nc.vector.scalar_tensor_tensor(dev[:, :, :], bc(mean, KT), -1.0 / D, R, MUL, ADD), m)
        s = A.do(lambda: nc.scalar.activation(sq[:, :, :], dev[:, :, :], ACT.Square), m)
        m = self.colsum(var, lambda k: sq[:, k, :], KT, after=[s])
        m = self.rstd(rs, var, 1.0 / D, LN_EPS, m)
        m = V.do(lambda: nc.vector.tensor_tensor(dev[:, :, :], dev[:, :, :], bc(rs, KT), MUL), m)
        for k in range(KT):
            g, b = self.col("ln_g", 8 * l + k), self.col("ln_b", 8 * l + k)
            V.do(lambda: nc.vector.tensor_scalar(dst[:, k, :], dev[:, k, :], g, b, MUL, ADD), m)

    def tail(self, l, Y, tmp, ready, order=None):
        P_, V, A, nc, X = self.P, self.V, self.A, self.nc, self.H
        R, R2, sig, pT = tmp(KT, T), tmp(KT, T), tmp(2, T), tmp(2, T)
        got = self.misc.start(self.G, pT[:, :, :], self.t["p"][l])
        P_.wait(ready)
        free = [None] * 8
        for c in range(4):
            w = self.take()
            for e in range(2):
                m, b = 2 * c + e, (2 * c + e) % 8
                y = self.bank[b][:, 0:T]
                done = self.product(y, w, KT, lambda k: Y[:, k, :], e * KT, e == 1)
                x, r = X[:, m, 0:T], R[:, m, :]
                if order == "sc":
                    y = y.rearrange("p (s c) -> p c s", s=SL)
                    x, r = (a.rearrange("p (c s) -> p c s", s=SL) for a in (x, r))
                free[b] = V.do(lambda: nc.vector.scalar_tensor_tensor(r, x, ALPHA, y, MUL, ADD), done)
        rdy = V.now()
        P_.wait(rdy)
        P_.wait(got)
        for m in range(KT):
            w = self.take()
            bg, bp, e = m % 4, 4 + m % 4, m % 2
            gate, proj = self.bank[bg][:, 0:T], self.bank[bp][:, 0:T]
            P_.wait(free[bg])
            P_.wait(free[bp])
            self.product(gate, w, KT, lambda k: R[:, k, :], 0, False)
            done = self.product(proj, w, 2, lambda k: pT[:, k, :], KT, True)
            s = A.do(lambda: nc.scalar.activation(sig[:, e, :], gate, ACT.Sigmoid), done, free[bp])
            v = V.do(lambda: nc.vector.tensor_tensor(sig[:, e, :], sig[:, e, :], proj, MUL), s)
            free[bg] = free[bp] = v
            V.do(lambda: nc.vector.tensor_tensor(R2[:, m, :], R[:, m, :], sig[:, e, :], ADD), v)
            if e == 1:
                A.wait(V.now())
        self.bounds(P_)
        self.layer_norm(R2, l, X[:, :, 0:T], tmp, V.now())
        self.bounds()

    def conv_layer(self, l):
        P_, V, A, nc, X, ctl = self.P, self.V, self.A, self.nc, self.H, self.ctl
        tmp = Arena(self.arena, self.arena_size)
        Y = tmp(KT, T)
        U = [tmp(T + 2) for _ in range(2)]
        hs, sz, cv = ([tmp(T) for _ in range(2)] for _ in range(3))
        for e in range(2):
            V.do(lambda: nc.vector.memset(U[e][:, 0:2], 0.0))
        V.wait(V.now())
        kofs = 24 * (l // 3)

        def pair(i):
            for e in range(2):
                b = self.bank[4 * e:4 * e + 4]
                P_.wait(ctl.last(f"free{e}"))
                w = self.take()
                self.product(b[0][:, 0:T], w, KT, lambda k: X[:, k, 0:T], 0, False)
                hm = self.product(b[1][:, 0:T], w, KT, lambda k: X[:, k, 0:T], KT, True)
                w = self.take()
                self.product(b[2][:, 0:T], w, KT, lambda k: X[:, k, 0:T], 0, False)
                zm = self.product(b[3][:, 0:T], w, KT, lambda k: X[:, k, 0:T], KT, True)
                u = U[e]
                A.wait(ctl.last(f"free{e}"))
                a = A.do(lambda: nc.scalar.copy(hs[e], b[1][:, 0:T]), hm)
                z = A.do(lambda: nc.scalar.activation(sz[e], b[3][:, 0:T], ACT.Silu), zm)
                V.do(lambda: nc.vector.tensor_tensor(u[:, 2:T + 2], b[0][:, 0:T], hs[e], MUL), a)
                taps = [self.col("conv_k", i * 2 + (kofs + 8 * tap + e)) for tap in range(3)]
                V.do(lambda: nc.vector.tensor_scalar(cv[e], u[:, 0:T], taps[0], None, MUL), V.now())
                for tap in (1, 2):
                    V.do(lambda: nc.vector.scalar_tensor_tensor(
                        cv[e], u[:, tap:T + tap], taps[tap], cv[e], MUL, ADD), V.now())
                V.do(lambda: nc.vector.tensor_tensor(cv[e], cv[e], b[2][:, 0:T], MUL), V.now(), z)
                y = Y[:, bass.ds(i * 2 + e, 1), :].rearrange("p a t -> p (a t)")
                f = V.do(lambda: nc.vector.tensor_tensor(y, cv[e], sz[e], MUL), V.now())
                ctl.note(f"free{e}", f)

        ctl.loop_over(4, [ENG.PE, ENG.DVE, ENG.Activation], pair)
        self.tail(l, Y, tmp, V.now())

    def ssm_layer(self, l):
        P_, V, A, Gq, nc, X, ctl, t = self.P, self.V, self.A, self.G, self.nc, self.H, self.ctl, self.t
        v_, bank = nc.vector, self.bank
        tmp = Arena(self.arena, self.arena_size)
        UF, UP, ZZ = tmp(KT, SL, SC), tmp(G, SC), tmp(SC, 2, G)
        TT, CA = tmp(G, P), tmp(G, SL + 1, GH)
        Zs = X[:, :, T:2 * T]
        AB, ABT = tmp(16, SL, GH), tmp(16, P)
        t2 = tmp(16 * (SL + 1) * GH)
        B1, B2, C1, C2 = (tmp(G, GH) for _ in range(4))
        small = tmp(10 * G)
        lre, lim, ldt, th, er, ar, ai, w1, w2, w3 = (small[:, G * k:G * k + G] for k in range(10))
        PWr, PWi = tmp(SL + 1, G), tmp(SL + 1, G)
        A8r, A8i = tmp(2, G), tmp(2, G)
        q1, q2 = tmp(2, G), tmp(2, G)
        b1, b2 = t2[:, 0:1024], t2[:, 1024:2048]
        for dst, name in ((lre, "s_lre"), (lim, "s_lim"), (ldt, "s_ldt")):
            self.misc.start(Gq, dst[:, :], t[name][:, :])
        for dst, name in ((b1, "s_b1"), (b2, "s_b2"), (C1, "s_c1"), (C2, "s_c2")):
            flat = dst if name in ("s_b1", "s_b2") else dst.rearrange("p g h -> p (g h)")
            got = self.misc.start(Gq, flat, t[name][:, :])
        b1, b2 = (b.rearrange("p (g h) -> p g h", g=G) for b in (b1, b2))

        free = [None] * 8
        for c in range(8):
            w = self.take()
            for e in range(2):
                m = 2 * c + e
                b = m % 8
                P_.wait(free[b])
                o = bank[b][:, 0:T]
                done = self.product(o, w, KT, lambda k: X[:, k, 0:T], e * KT, e == 1)
                o = o.rearrange("p (c s) -> p s c", s=SL)
                if m < 8:
                    free[b] = V.do(lambda: v_.tensor_copy(UF[:, m, :, :], o), done)
                else:
                    z = Zs[:, m - 8, :].rearrange("p (s c) -> p s c", s=SL)
                    free[b] = A.do(lambda: nc.scalar.activation(z, o, ACT.Silu), done)
            if c == 3:
                u_ready = V.now()
        sc1, sc2 = t["scratch_u"], t["scratch_y"]
        wrote = self.shuffle.start(Gq, sc1.rearrange("(p n) -> p n", p=P),
                                   UF.rearrange("p m s c -> p (m s c)"), u_ready)
        Gq.wait(wrote)
        for s in range(SL):
            src = bass.AP(tensor=sc1.tensor, offset=s * SC,
                          ap=[[KT * T, GH], [T, KT], [GH * KT * T, 8], [1, SC]])
            u_in = self.shuffle.start(Gq, UP[s * GH:(s + 1) * GH, :, :]
                                      .rearrange("h (m g) c -> h m g c", g=8), src)

        V.wait(got)
        A.wait(got)
        dt = w1
        d = A.do(lambda: nc.scalar.activation(dt, ldt, ACT.Exp))
        V.do(lambda: v_.tensor_tensor(er, lre, dt, MUL), d)
        V.do(lambda: v_.tensor_tensor(th, lim, dt, MUL))
        d = V.now()
        A.do(lambda: nc.scalar.activation(er, er, ACT.Exp), d)
        V.do(lambda: v_.tensor_scalar(w2, th, 1 / (2 * np.pi), 12582912.0, MUL, ADD), V.now())
        V.do(lambda: v_.tensor_scalar(w2, w2, -12582912.0, None, ADD), V.now())
        for part in (6.28125, 1.9340515136718750e-3, 1.2556659418 * 1e-6):
            V.do(lambda: v_.scalar_tensor_tensor(th, w2, -part, th, MUL, ADD), V.now())
        V.do(lambda: v_.tensor_scalar(th, th, 3.1415925, -3.1415925, MIN, MAX), V.now())
        V.do(lambda: v_.scalar_tensor_tensor(w2, th, -1.0, th, MUL, MAX), V.now())
        V.do(lambda: v_.tensor_scalar(w2, w2, -1.0, np.pi / 2, MUL, ADD), V.now())
        A.do(lambda: nc.scalar.activation(w2, w2, ACT.Sin), V.now())
        A.do(lambda: nc.scalar.activation(th, th, ACT.Sin))
        V.do(lambda: v_.tensor_tensor(ar, er, w2, MUL), A.now())
        V.do(lambda: v_.tensor_tensor(ai, er, th, MUL))
        fr, fi, n = w1, w2, w3
        V.do(lambda: v_.tensor_tensor(fr, lre, lre, MUL))
        V.do(lambda: v_.tensor_tensor(fi, lim, lim, MUL), V.now())
        V.do(lambda: v_.tensor_tensor(th, fr, fi, ADD), V.now())
        V.do(lambda: v_.reciprocal(th, th), V.now())
        V.do(lambda: v_.tensor_scalar(n, ar, -1.0, None, ADD))

        def cross(out, x, y, z, w, op):
            V.do(lambda: v_.tensor_tensor(er, z, w, MUL), V.now())
            V.do(lambda: v_.tensor_tensor(out, x, y, MUL))
            V.do(lambda: v_.tensor_tensor(out, out, er, op), V.now())

        cross(fr, n, lre, ai, lim, ADD)
        cross(fi, ai, lre, n, lim, SUB)
        V.do(lambda: v_.tensor_tensor(fr, fr, th, MUL), V.now())
        V.do(lambda: v_.tensor_tensor(fi, fi, th, MUL), V.now())
        sgn = self.col("sgn")
        V.do(lambda: v_.tensor_scalar(fi, fi, sgn, None, MUL), V.now())
        V.do(lambda: v_.tensor_tensor(B1[:, :, :], b1, bc_in(fr, GH), MUL), V.now())
        V.do(lambda: v_.tensor_tensor(B2[:, :, :], b2, bc_in(fi, GH), MUL))
        V.do(lambda: v_.tensor_tensor(B1[:, :, :], B1[:, :, :], B2[:, :, :], ADD), V.now())
        V.do(lambda: v_.tensor_tensor(B2[:, :, :], b2, bc_in(fr, GH), MUL), V.now())
        V.do(lambda: v_.tensor_tensor(b1, b1, bc_in(fi, GH), MUL))
        V.do(lambda: v_.tensor_tensor(B2[:, :, :], B2[:, :, :], b1, SUB), V.now())
        V.do(lambda: v_.tensor_scalar(C1[:, :, :], C1[:, :, :], sgn, -1.0, MUL, MUL))
        V.do(lambda: v_.tensor_scalar(C2[:, :, :], C2[:, :, :], -1.0, None, MUL))
        V.do(lambda: v_.memset(PWr[:, 0, :], 1.0))
        V.do(lambda: v_.memset(PWi[:, 0, :], 0.0))
        V.do(lambda: v_.tensor_copy(PWr[:, 1, :], ar))
        V.do(lambda: v_.tensor_copy(PWi[:, 1, :], ai))
        p1 = t2[:, 0:4 * G].rearrange("p (a g) -> p a g", g=G)
        for k in (1, 2, 4):
            lr, li = PWr[:, 1:1 + k, :], PWi[:, 1:1 + k, :]
            hr, hi = bc(PWr[:, k, :], k), bc(PWi[:, k, :], k)
            orr, oi, s = PWr[:, 1 + k:1 + 2 * k, :], PWi[:, 1 + k:1 + 2 * k, :], p1[:, 0:k, :]
            for out, x, y, op in ((orr, hr, hi, SUB), (oi, hi, hr, ADD)):
                V.do(lambda: v_.tensor_tensor(s, li, y, MUL), V.now())
                V.do(lambda: v_.tensor_tensor(out, lr, x, MUL))
                V.do(lambda: v_.tensor_tensor(out, out, s, op), V.now())
        for h in range(2):
            V.do(lambda: v_.tensor_copy(A8r[:, h, :], PWr[:, SL, :]), V.now())
            V.do(lambda: v_.tensor_scalar(A8i[:, h, :], PWi[:, SL, :], sgn, 1.0 - 2 * h, MUL, MUL))
        RPr, RPi = tmp(SL, G), tmp(SL, G)
        US = small[:, 0:16 * SC].rearrange("p (g c) -> p g c", g=16)
        for s in range(SL):
            V.do(lambda: v_.tensor_copy(RPr[:, s, :], PWr[:, SL - 1 - s, :]))
            V.do(lambda: v_.tensor_scalar(RPi[:, s, :], PWi[:, SL - 1 - s, :], sgn, None, MUL))
        V.do(lambda: v_.memset(TT[:, :, :], 0.0))
        V.do(lambda: v_.memset(ZZ[:, 0, :, :], 0.0))
        P_.wait(u_in)
        V.wait(u_in)
        self.bounds()

        KS = ABT

        def block(i):
            V.wait(ctl.last("pe"))
            Gq.wait(ctl.last("pe"))
            g16 = bass.ds(i * 16, 16)
            back = lambda pw: pw[:, :, g16].rearrange("p s g -> p g s").unsqueeze(3).broadcast_to(
                [P, 16, SL, GH])
            over = lambda b, n: b[:, g16, :].unsqueeze(2).broadcast_to([P, 16, n, GH])
            s2 = t2[:, 0:16 * SL * GH].rearrange("p (g s h) -> p g s h", g=16, s=SL)
            Gq.wait(V.now())
            y = Gq.do(lambda: nc.gpsimd.tensor_tensor(s2, back(RPi), over(B2, SL), MUL))
            V.do(lambda: v_.tensor_tensor(AB, back(RPr), over(B1, SL), MUL))
            ab = V.do(lambda: v_.tensor_tensor(AB, AB, s2, ADD), y, V.now())
            us = V.do(lambda: v_.tensor_copy(US[:, :, :], UP[:, g16, :]))
            P_.wait(ctl.last("k_read"))
            P_.wait(us)
            for g in range(16):
                tr = P_.do(lambda: nc.tensor.transpose(
                    bank[g // 4][:, P * (g % 4):P * (g % 4 + 1)],
                    AB[:, g, :, :].rearrange("p s h -> p (s h)"), self.ident[:, :]), ab)
            for b in range(4):
                copy = lambda: nc.scalar.copy(ABT[:, 4 * b:4 * b + 4, :].rearrange("p g n -> p (g n)"),
                                              bank[b][:, :])
                abt = A.do(copy, tr)
            for g in range(16):
                u = US[:, g, :]
                o0, o1 = bank[0][:, 32 * g:32 * g + 32], bank[1][:, 32 * g:32 * g + 32]
                P_.quiet(self.mm(o0, ABT[:, g, :], u, True, True), abt)
                P_.quiet(self.mm(o1[0:64, :], ABT[:, g, 64:128], u, True, True))
                vm = P_.do(self.mm(o1[64:128, :], ABT[:, g, 0:64], u, True, True))
            for h in range(2):
                zo = ZZ[:, 1:SC, h, g16]
                vr = V.do(lambda: v_.tensor_copy(
                    zo, bank[h][:, :].rearrange("p (g c) -> p c g", g=16)[:, 0:SC - 1, :]), vm)
            n = SL + 1
            s9 = t2[:, 0:16 * n * GH].rearrange("p (g s h) -> p g s h", g=16, s=n)
            pw = lambda p: p[:, :, g16].rearrange("p s g -> p g s").unsqueeze(3).broadcast_to(
                [P, 16, n, GH])
            y = Gq.do(lambda: nc.gpsimd.tensor_tensor(s9, pw(PWi), over(C2, n), MUL), ab)
            c = CA[:, g16, :, :]
            V.do(lambda: v_.tensor_tensor(c, pw(PWr), over(C1, n), MUL))
            bs = AB[:, 0:2, :, :].rearrange("p a s h -> p (a s) h")
            V.do(lambda: v_.tensor_copy(bs, B1[:, g16, :]), tr)
            ca = V.do(lambda: v_.tensor_tensor(c, c, s9, ADD), y, V.now())
            for g in range(16):
                rhs = CA[:, bass.ds(i * 16 + g, 1), 0:SL, :].rearrange("p a s h -> p (a s h)")
                km = P_.do(self.mm(bank[4 + g // 4][0:GH, P * (g % 4):P * (g % 4 + 1)],
                                   bs[:, g, :], rhs, True, True), ca)
            for b in range(4):
                copy = lambda: nc.scalar.copy(KS[0:GH, 4 * b:4 * b + 4, :]
                                              .rearrange("p g n -> p (g n)"), bank[4 + b][0:GH, :])
                ks = A.do(copy, km, vr)
            ctl.note("k_read", ks)
            ctl.note("pe", km)
            for s in range(SL):
                toe = self.moved.start(
                    A, TT[s * GH:(s + 1) * GH, g16, s * GH:P], KS[0:GH, :, 0:(SL - s) * GH], ks)
            A.wait(toe)
            P_.wait(toe)

        ctl.loop_over(4, [ENG.PE, ENG.DVE, ENG.Activation, ENG.Pool], block)
        self.bounds(P_, V)

        def steps(i):
            for h in range(2):
                old, new = (ZZ[:, bass.ds(i * 2 + (1 + h + e), 1), :, :].rearrange("p a r g -> p (a r) g")
                            for e in range(2))
                V.do(lambda: v_.tensor_tensor(q1[:, :, :], old, A8r[:, :, :], MUL), V.now())
                for r in range(2):
                    V.do(lambda: v_.tensor_tensor(q2[:, r, :], old[:, 1 - r, :], A8i[:, r, :], MUL))
                V.do(lambda: v_.tensor_tensor(q1[:, :, :], q1[:, :, :], q2[:, :, :], ADD), V.now())
                V.do(lambda: v_.tensor_tensor(new, new, q1[:, :, :], ADD), V.now())

        ctl.loop_over((SC - 2) // 2, [ENG.DVE], steps)
        P_.wait(V.now())
        YP = AB.rearrange("p g s h -> p (g s h)").rearrange("p (g c) -> p g c", g=G)
        for g in range(G):
            o = bank[g // 16][:, 32 * (g % 16):32 * (g % 16) + 32]
            P_.quiet(self.mm(o, TT[:, g, :], UP[:, g, :], True, False))
            ym = P_.do(self.mm(o, CA[:, g, 1:SL + 1, :].rearrange("p s h -> p (s h)"),
                               ZZ[:, 0:SC, 0, g], False, True))
            if g % 16 == 15:
                b = g // 16
                cp = A.do(lambda: nc.scalar.copy(YP[:, 16 * b:16 * b + 16, :]
                                                 .rearrange("p g c -> p (g c)"), bank[b][:, :]), ym)
        wrote = self.moved.start(A, sc2.rearrange("(p n) -> p n", p=P),
                                   YP.rearrange("p g c -> p (g c)"), cp)
        A.wait(wrote)
        YF = ABT.rearrange("p g n -> p (g n)").rearrange("p (m s c) -> p m s c", m=KT, s=SL)
        for s in range(SL):
            src = bass.AP(tensor=sc2.tensor, offset=s * GH * KT * T,
                          ap=[[SC, 8], [KT * T, GH], [T, KT], [1, SC]])
            back = self.moved.start(A, YF[:, :, s, :], src)
        yf = YF.rearrange("p m s c -> p m (s c)")
        uf = UF.rearrange("p m s c -> p m (s c)")
        V.wait(back)
        for k in range(KT):
            V.do(lambda: v_.scalar_tensor_tensor(yf[:, k, :], uf[:, k, :], self.col("ssm_d", k),
                                                 yf[:, k, :], MUL, ADD))
        ge = A.do(lambda: nc.scalar.activation(yf, yf, ACT.Gelu_apprx_tanh), V.now())
        P_.wait(ge)
        Y = UP.rearrange("p g c -> p (g c)").rearrange("p (m n) -> p m n", m=KT)
        for c in range(4):
            w = self.take()
            for e in range(2):
                m = 2 * c + e
                o = bank[m][:, 0:T]
                done = self.product(o, w, KT, lambda k: yf[:, k, :], e * KT, e == 1)
                sg = uf[:, m, :]
                a = A.do(lambda: nc.scalar.activation(sg, o, ACT.Sigmoid, bias=self.col("b_glu", m)), done)
                V.do(lambda: v_.tensor_tensor(sg, sg, yf[:, m, :], MUL), a)
                V.do(lambda: v_.tensor_tensor(Y[:, m, :], sg, Zs[:, m, :], MUL), V.now())
        ready = V.now()
        self.bounds()
        tail = Arena(self.arena, self.arena_size)
        tail.at = 2 * KT * T
        self.tail(l, Y, tail, ready, "sc")


    def rwkv_layer(self, l):
        P_, V, A, Gq, nc, X, ctl, t = self.P, self.V, self.A, self.G, self.nc, self.H, self.ctl, self.t
        v_, s_, bank, tt = nc.vector, nc.scalar, self.bank, nc.vector.tensor_tensor
        keep = Arena(self.arena, self.arena_size)
        RKVZ, LD, AA, Y = keep(4, KT, T), keep(KT, T), keep(KT, T), keep(KT, T)
        masks = keep(1280)
        tmp = Arena(self.arena, self.arena_size)
        tmp.at = keep.at
        dx, XS = tmp(KT, T), tmp(6, KT, T)
        gm = self.misc.start(Gq, masks, t["r_masks"][:, :])
        x = X[:, :, 0:T]
        V.do(lambda: tt(dx[:, :, 1:T], x[:, :, 0:T - 1], x[:, :, 1:T], SUB))
        V.do(lambda: v_.tensor_scalar(dx[:, :, 0:1], x[:, :, 0:1], -1.0, None, MUL))
        V.wait(V.now())
        mixed = []
        for n in range(6):
            for k in range(KT):
                V.do(lambda: v_.scalar_tensor_tensor(XS[:, n, k, :], dx[:, k, :],
                                                     self.col("mu", 8 * n + k), x[:, k, :], MUL, ADD))
            mixed.append(V.now())
        w = self.take()
        lw, la = bank[0][0:64, 0:T], bank[1][64:128, 0:T]
        hw, ha = tmp(T), tmp(T)
        P_.wait(mixed[5])
        for k in range(KT):
            P_.quiet(self.mm(lw, w[:, 64 * k:64 * k + 64], XS[:, 4, k, :], k == 0, k == KT - 1))
        for k in range(KT):
            mk = self.mm(la, w[:, 512 + 64 * k:576 + 64 * k], XS[:, 5, k, :], k == 0, k == KT - 1)
            m = P_.do(mk) if k == KT - 1 else P_.quiet(mk)
        A.do(lambda: s_.activation(hw[0:64, :], lw, ACT.Tanh), m)
        m = A.do(lambda: s_.copy(ha[64:128, :], la))
        P_.wait(m)
        for k in range(KT):
            for e, (h, dst, bias) in enumerate(((hw, LD, "w0"), (ha, AA, "a0"))):
                b, r = bank[(2 * k + e) % 8], slice(64 * e, 64 * e + 64)
                if k >= 4:
                    P_.wait(freed[2 * k + e - 8])
                mk = self.mm(b[:, 0:T], w[r, 1024 + P * k:1024 + P * (k + 1)], h[r, :], True, True)
                m = self.give(mk) if (k, e) == (KT - 1, 1) else P_.do(mk)
                m = A.do(lambda: s_.activation(dst[:, k, :], b[:, 0:T], ACT.Sigmoid,
                                               bias=self.col(bias, k)), m)
                freed = [m] if (k, e) == (0, 0) else freed + [m]
        V.do(lambda: v_.tensor_scalar(LD[:, :, :], LD[:, :, :], -float(np.exp(-0.5)), None, MUL), m)
        self.bounds(P_, A)

        def project(n):
            for c in range(4):
                w = self.take()
                for e in range(2):
                    m = 2 * c + e
                    P_.wait(ctl.last(f"b{m}"))
                    o = bank[m][:, 0:T]
                    done = self.product(
                        o, w, KT, lambda k: XS[:, bass.ds(n, 1), k, :].rearrange("p a t -> p (a t)"),
                        e * KT, e == 1)
                    dst = RKVZ[:, bass.ds(n, 1), m, :].rearrange("p a t -> p (a t)")
                    if e:
                        f = A.do(lambda: s_.copy(dst, o), done)
                    else:
                        f = V.do(lambda: v_.tensor_copy(dst, o), done)
                    ctl.note(f"b{m}", f)

        ctl.loop_over(4, [ENG.PE, ENG.DVE, ENG.Activation], project)
        for q in (P_, V, A, Gq):
            q.wait(gm)
        self.bounds()

        tmp = Arena(self.arena, self.arena_size)
        tmp.at = keep.at
        kk, kp, cu, wi, wv, wx, bt, kt, sq, O, OS, bo = (tmp(2, T) for _ in range(12))
        AR = tmp(2, 2, 2, P)
        NQ, AQ = tmp(8, 2 * P), tmp(8, 2 * P)
        NN, XX, XT, MM, YY = (tmp(8, P) for _ in range(5))
        tok = tmp(4, 4, P)
        Vz = tmp(2, 4, P)
        Gs, XG, XA, SAz, SA = tmp(8, 64), tmp(8, 64), tmp(4, P), tmp(2, 2 * P), tmp(2, 2 * P)
        ST = tmp(2, P)
        mask2 = masks[:, 0:256]
        mN, m0, m0T = (masks[:, 256 + P * k:384 + P * k] for k in range(3))
        level = [masks[:, 640 + P * k:768 + P * k] for k in range(5)]
        Z0 = V.do(lambda: v_.memset(SAz[:, :, :], 0.0))
        V.wait(Z0)

        def heads(i):
            two = bass.ds(i * 2, 2)
            r, k, v, z = (RKVZ[:, n, two, :] for n in range(4))
            a, ld = AA[:, two, :], LD[:, two, :]
            flat = lambda ap: ap.rearrange("p j t -> p (j t)")
            V.do(lambda: v_.memset(ST[:, :, :], 0.0), ctl.last("end_p"))
            for j in range(2):
                kj = RKVZ[:, 1, bass.ds(i * 2 + j, 1), :].rearrange("p a t -> p (a t)")
                aj = AA[:, bass.ds(i * 2 + j, 1), :].rearrange("p a t -> p (a t)")
                V.do(lambda: v_.tensor_scalar(kk[:, j, :], kj, self.col("k_k", i * 2 + j), None, MUL),
                     ctl.last("end_p"), ctl.last("end_a"), ctl.last("end_g"))
                V.do(lambda: v_.tensor_scalar(kp[:, j, :], aj, -1.0, self.col("k_a", i * 2 + j), ADD, MUL))
            s = A.do(lambda: s_.activation(sq[:, :, :], kk[:, :, :], ACT.Square), V.now(), ctl.last("end_v"))
            V.do(lambda: v_.scalar_tensor_tensor(kp[:, :, :], kp[:, :, :], 1.0, k, ADD, MUL), V.now())
            m = P_.do(self.mm(bank[7][:, :], self.blk64[:, :], flat(sq), True, True), s, ctl.last("end_v"))
            m = A.do(lambda: s_.activation(flat(sq), bank[7][:, :], ACT.Sqrt), m)
            V.do(lambda: v_.tensor_copy(cu[:, :, :], ld))
            for lv in range(6):
                h = 1 << lv
                c = flat(cu).rearrange("p (b two h) -> p b two h", two=2, h=h)
                carry = c[:, :, 0, h - 1:h].broadcast_to([P, 2 * T // (2 * h), h])
                V.do(lambda: tt(c[:, :, 1, :], c[:, :, 1, :], carry, ADD), V.now())
            e1 = A.do(lambda: s_.activation(wi[:, :, :], cu[:, :, :], ACT.Exp), V.now())
            e2 = A.do(lambda: s_.activation(wv[:, :, :], cu[:, :, :], ACT.Exp, scale=-1.0))
            V.do(lambda: tt(wx[:, :, :], cu[:, :, :], ld, SUB), V.now())
            e3 = A.do(lambda: s_.activation(wx[:, :, :], wx[:, :, :], ACT.Exp), V.now())
            V.do(lambda: v_.tensor_scalar(sq[:, :, :], sq[:, :, :], 1e-12, None, MAX), m)
            V.do(lambda: v_.reciprocal(sq[:, :, :], sq[:, :, :]), V.now())
            V.do(lambda: tt(kk[:, :, :], kk[:, :, :], sq[:, :, :], MUL), V.now())
            ar = lambda which: AR[:, :, :, which, :].rearrange("p j b t -> p (j b) t")
            at4 = lambda ap: ap.rearrange("p j (b t) -> p (j b) t", t=P)
            V.do(lambda: tt(kt[:, :, :], kp[:, :, :], wv[:, :, :], MUL), e2)
            V.do(lambda: tt(ar(1), at4(r), at4(wi), MUL), e1)
            V.do(lambda: tt(bt[:, :, :], kk[:, :, :], a, MUL), V.now())
            V.do(lambda: v_.scalar_tensor_tensor(ar(0), at4(kk), -1.0, at4(wx), MUL, MUL), e3)
            pre = V.do(lambda: tt(bt[:, :, :], bt[:, :, :], wv[:, :, :], MUL), V.now())
            for j in range(2):
                if j:
                    P_.wait(masked)
                for e in range(2):
                    rows = slice(64 * e, 64 * e + 64)
                    for tb in range(2):
                        tk = slice(P * tb, P * tb + P)
                        both = AR[rows, j, tb, :, :].rearrange("p w t -> p (w t)")
                        half = slice(256 * tb, 256 * tb + 256)
                        P_.quiet(self.mm(bank[2 * e][:, half], bt[rows, j, tk], both, True, True), pre)
                        P_.quiet(self.mm(bank[2 * e + 1][:, half], kt[rows, j, tk], both, True, True))
                        m = P_.do(self.mm(bank[4 + e][:, tk], AR[rows, j, tb, 0, :], bt[rows, j, tk],
                                          True, True))
                for e in range(2):
                    u = slice(4 * j + 2 * e, 4 * j + 2 * e + 2)
                    q = lambda b: b[:, :].rearrange("p (b t) -> p b t", b=2)
                    V.do(lambda: tt(NQ[:, u, :], q(bank[2 * e]), bc(mask2, 2), MUL), m)
                    V.do(lambda: tt(AQ[:, u, :], q(bank[2 * e + 1]), bc(mask2, 2), MUL))
                    masked = V.do(lambda: tt(NN[:, u, :], bank[4 + e][:, 0:256]
                                             .rearrange("p (b t) -> p b t", b=2), bc(mN, 2), MUL))
            P_.wait(masked)
            for n in range(4):
                for jb in range(4):
                    j, tk = jb // 2, slice(P * (jb % 2), P * (jb % 2) + P)
                    if n == 0:
                        src = RKVZ[:, 2, bass.ds(i * 2 + j, 1), tk].rearrange("p a t -> p (a t)")
                        src = self.stage_v(src, O[:, j, tk])
                    else:
                        src = (bt[:, j, tk], kt[:, j, tk], AR[:, j, jb % 2, 0, :])[n - 1]
                    m = P_.do(lambda: nc.tensor.transpose(bank[n][:, P * jb:P * jb + P], src,
                                                          self.ident[:, :]))
            for n in range(4):
                cp = A.do(lambda: s_.copy(tok[:, n, :, :].rearrange("p a b -> p (a b)"), bank[n][:, :]), m)
            P_.wait(cp)
            NT = NQ[:, :, 0:P]
            V.do(lambda: tt(XX[:, :, :], NN[:, :, :], bc(m0, 8), MUL), V.now())
            V.do(lambda: tt(XT[:, :, :], NT, bc(m0T, 8), MUL))
            V.do(lambda: tt(XX[:, :, :], XX[:, :, :], bc(self.ident[:, :], 8), ADD), V.now())
            xx = V.do(lambda: tt(XT[:, :, :], XT[:, :, :], bc(self.ident[:, :], 8), ADD))
            p1 = None
            for lv in range(5):
                mm_ = Gq.do(lambda: nc.gpsimd.tensor_tensor(MM[:, :, :], NT, bc(level[lv], 8), MUL),
                            masked, p1)
                P_.wait(mm_)
                P_.wait(xx)
                for u in range(8):
                    p1 = P_.do(self.mm(bank[4 + u // 4][:, P * (u % 4):P * (u % 4) + P], MM[:, u, :],
                                       XX[:, u, :], True, True))
                for b in range(2):
                    y = A.do(lambda: s_.copy(YY[:, 4 * b:4 * b + 4, :].rearrange("p u t -> p (u t)"),
                                             bank[4 + b][:, :]), p1)
                P_.wait(y)
                for u in range(8):
                    c = slice(P * (u % 4), P * (u % 4) + P)
                    m = P_.do(self.mm(bank[u // 4][:, c], YY[:, u, :], XT[:, u, :], True, True))
                if lv < 4:
                    for u in range(8):
                        c = slice(P * (u % 4), P * (u % 4) + P)
                        m = P_.do(self.mm(bank[2 + u // 4][:, c], XT[:, u, :], YY[:, u, :], True, True))
                for b in range(2):
                    u4 = slice(4 * b, 4 * b + 4)
                    q = lambda bk: bk[:, :].rearrange("p (u t) -> p u t", u=4)
                    xx = V.do(lambda: tt(XT[:, u4, :], XT[:, u4, :], q(bank[b]), ADD), m)
                    if lv < 4:
                        xx = V.do(lambda: tt(XX[:, u4, :], XX[:, u4, :], q(bank[2 + b]), ADD))
            unit = lambda u: (u // 4, (u // 2) % 2, u % 2)
            for u in range(8):
                j, e, tb = unit(u)
                m = P_.do(self.mm(bank[4][:, 64 * u:64 * u + 64], AQ[:, u, 0:P],
                                  tok[:, 0, 2 * j + tb, 64 * e:64 * e + 64], True, True))
            g = A.do(lambda: s_.copy(Gs.rearrange("p u v -> p (u v)"), bank[4][:, :]), m)
            for h in range(2):
                vz = A.do(lambda: s_.activation(Vz[:, h, :, :], tok[:, 0, :, :], ACT.Copy,
                                                scale=self.col("half", h)), cp)
            P_.wait(xx)
            for u in range(8):
                j, e, tb = unit(u)
                P_.quiet(self.mm(bank[6][64 * e:64 * e + 64, P * (2 * j + tb):P * (2 * j + tb) + P],
                                 tok[:, 3, 2 * j + tb, 64 * e:64 * e + 64], XT[:, u, :], True, True))
            P_.wait(g)
            for u in range(8):
                m = P_.do(self.mm(bank[5][:, 64 * u:64 * u + 64], XT[:, u, :], Gs[:, u, :], True, True))
            xa = A.do(lambda: s_.copy(XA.rearrange("p u t -> p (u t)"), bank[6][:, :]), m)
            V.do(lambda: v_.tensor_copy(XG.rearrange("p u v -> p (u v)"), bank[5][:, :]), m)
            P_.wait(xa)
            P_.wait(vz)
            xgb = XG.rearrange("p (je tb) v -> p tb je v", tb=2)
            st, os_, copied = V.now(), None, [None, None]
            for c in range(4):
                tb, h = c // 2, c % 2
                rows, bk = slice(64 * h, 64 * h + 64), bank[4 + (c % 2)]
                saz = SAz[rows, h, :].rearrange("p (je v) -> p je v", je=4)
                xg = xgb[rows, tb, :, :]
                P_.wait(st)
                if c:
                    for j in range(2):
                        m = P_.do(self.mm(bk[rows, P * j:P * j + P], XA[:, 2 * j + tb, rows], ST[:, j, :],
                                          True, True))
                    sa = V.do(lambda: tt(saz, xg, bk[rows, 0:2 * P].rearrange("p (je v) -> p je v", je=4),
                                         ADD), m, copied[h])
                    P_.wait(os_)
                    for j in range(2):
                        m = P_.do(self.mm(bank[7][:, P * j + 0:P * j + 64], ST[:, j, :],
                                          AR[:, j, tb, 1, rows], True, True))
                    os_ = A.do(lambda: s_.copy(
                        OS[:, :, 64 * c:64 * c + 64],
                        bank[7][:, 0:2 * P].rearrange("p (j t) -> p j t", j=2)[:, :, 0:64]), m)
                else:
                    sa = V.do(lambda: v_.tensor_copy(saz, xg), V.now(), ctl.last("end_p"))
                    V.do(lambda: v_.memset(OS[:, :, 0:64], 0.0))
                both = copied[h] = A.do(lambda: s_.copy(SA[rows, tb, :], SAz[rows, h, :]), sa)
                if c < 3:
                    P_.wait(sa)
                    for j in range(2):
                        o = bank[6][:, P * j:P * j + P]
                        P_.quiet(self.mm(o, self.ident[:, :], ST[:, j, :], True, False))
                        P_.quiet(self.mm(o, tok[:, 1, 2 * j + tb, :], SAz[:, h, P * j:P * j + P],
                                         False, False))
                        m = P_.do(self.mm(o, tok[:, 2, 2 * j + tb, :], Vz[:, h, 2 * j + tb, :],
                                          False, True))
                    for j in range(2):
                        for e in range(2):
                            rw = slice(64 * e, 64 * e + 64)
                            st = V.do(lambda: v_.tensor_scalar(
                                ST[rw, j, 64 * e:64 * e + 64], bank[6][rw, P * j + 64 * e:P * j + 64 * e + 64],
                                wi[rw, j, 64 * c + 63:64 * c + 64], None, MUL), m)
            P_.wait(both)
            for u in range(8):
                j, e, tb = unit(u)
                o = bank[u // 4][64 * e:64 * e + 64, P * (2 * (u // 4 - u // 4) + tb):P * tb + P]
                P_.quiet(self.mm(o, SA[:, tb, P * j + 64 * e:P * j + 64 * e + 64], NQ[:, u, P:2 * P],
                                 True, False))
                m = P_.do(self.mm(o, tok[:, 0, 2 * j + tb, 64 * e:64 * e + 64], AQ[:, u, P:2 * P],
                                  False, True))
            for j in range(2):
                V.do(lambda: tt(O[:, j, :], OS[:, j, :], bank[j][:, 0:T], ADD), m, os_)
            m = P_.do(self.mm(bank[4][:, :], self.blk64[:, :], flat(O), True, True), V.now())
            V.do(lambda: tt(bo[:, :, :], r, kp[:, :, :], MUL))
            for j in range(2):
                V.do(lambda: v_.tensor_scalar(bo[:, j, :], bo[:, j, :], self.col("r_k", i * 2 + j), None, MUL),
                     V.now())
            mb = P_.do(self.mm(bank[5][:, :], self.blk64[:, :], flat(bo), True, True), V.now())
            V.do(lambda: v_.scalar_tensor_tensor(flat(O), bank[4][:, :], -1.0 / 64, flat(O), MUL, ADD), m)
            s = A.do(lambda: s_.activation(sq[:, :, :], O[:, :, :], ACT.Square), V.now())
            m = P_.do(self.mm(bank[6][:, :], self.blk64[:, :], flat(sq), True, True), s)
            rs = flat(wx)
            self.rstd(rs, bank[6][:, :], 1.0 / 64, GN_EPS, m)
            V.do(lambda: tt(flat(O), flat(O), rs, MUL), V.now())
            for j in range(2):
                V.do(lambda: v_.tensor_scalar(O[:, j, :], O[:, j, :], self.col("lnx_g", i * 2 + j),
                                              self.col("lnx_b", i * 2 + j), MUL, ADD), V.now())
            V.do(lambda: tt(bo[:, :, :], v, bank[5][:, :].rearrange("p (j t) -> p j t", j=2), MUL), mb)
            V.do(lambda: tt(O[:, :, :], O[:, :, :], bo[:, :, :], ADD), V.now())
            sz = A.do(lambda: s_.activation(OS[:, :, :], z, ACT.Silu), V.now())
            f = V.do(lambda: tt(Y[:, two, :], O[:, :, :], OS[:, :, :], MUL), sz)
            ctl.note("end_v", f)
            ctl.note("end_a", A.now())
            ctl.note("end_p", P_.now())
            ctl.note("end_g", Gq.now())

        ctl.loop_over(4, [ENG.PE, ENG.DVE, ENG.Activation, ENG.Pool], heads)
        self.bounds()
        tail = Arena(self.arena, self.arena_size)
        tail.at = keep.at
        self.tail(l, Y, tail, V.now())

    def stage_v(self, src, dst):
        m = self.V.do(lambda: self.nc.vector.tensor_copy(dst, src))
        self.P.wait(m)
        return dst


    def ada(self):
        P_, V, A, nc, ctl = self.P, self.V, self.A, self.nc, self.ctl
        v_ = nc.vector
        tmp = Arena(self.arena, self.arena_size)
        sc = tmp(KT, 2)
        c = self.cols[:, COLS["c"]:COLS["c"] + 2 * KT].rearrange("p (k n) -> p k n", n=2)
        got = self.misc.start(self.G, self.H[:, :, T:2 * T], self.t["ctx"])
        for q in (V, P_, A):
            q.wait(got)
        m = A.do(lambda: nc.scalar.activation(sc[:, :, :], c, ACT.Silu))
        P_.wait(m)
        mod = self.mod[:, :]

        def sixteen(i):
            for h in range(2):
                P_.wait(ctl.last(f"mod{h}"))
                for q in range(4):
                    w = self.take()
                    for e in range(2):
                        n = 2 * q + e
                        done = self.product(self.bank[h][:, 2 * n:2 * n + 2], w, KT,
                                            lambda k: sc[:, k, :], e * KT, e == 1)
                at = i * 16 + 8 * h
                bias = self.cols[:, bass.ds(at + COLS["ada_b"], 8)].unsqueeze(2).broadcast_to([P, 8, 2])
                out = mod[:, bass.ds(at * 2, 16)].rearrange("p (m n) -> p m n", n=2)
                f = V.do(lambda: v_.tensor_tensor(
                    out, self.bank[h][:, 0:16].rearrange("p (m n) -> p m n", n=2), bias, ADD), done)
                ctl.note(f"mod{h}", f)

        ctl.loop_over(9, [ENG.PE, ENG.DVE], sixteen)
        m5 = mod.rearrange("p (l w k n) -> p l w k n", l=DEPTH2, w=9, k=KT)
        V.wait(V.now())
        for l in range(DEPTH2):
            for s in range(3):
                at = COLS["norm_g"] + KT * (3 * l + s)
                g = bc_in(self.cols[:, at:at + KT], 2)
                sl = m5[:, l, 3 * s + 1, :, :]
                V.do(lambda: v_.scalar_tensor_tensor(sl, sl, 1.0, g, ADD, MUL))
                if s != 1:
                    gt = m5[:, l, 3 * s + 2, :, :]
                    V.do(lambda: v_.tensor_scalar(gt, gt, 0.5, None, MUL))
        self.bounds()

    def mod_col(self, l, which, k, n):
        return self.mod[:, bass.ds((k * 2) + ((l * 9 + which) * KT * 2 + n), 1)]

    def modulated(self, l, s, dst, sq, nt):
        V, A, nc, H = self.V, self.A, self.nc, self.H
        m = A.do(lambda: nc.scalar.activation(sq[:, :, 0:nt], H[:, :, 0:nt], ACT.Square))
        m = self.colsum(self.bank[0][:, 0:nt], lambda k: sq[:, k, 0:nt], KT, after=[m])
        rs = sq[:, 0, 0:nt]
        m = self.rstd(rs, self.bank[0][:, 0:nt], 1.0 / D, RMS_EPS, m)
        V.do(lambda: nc.vector.tensor_tensor(dst[:, :, 0:nt], H[:, :, 0:nt], bc(rs, KT), MUL), m)
        V.wait(V.now())
        for k in range(KT):
            for n in range(nt // T):
                d = dst[:, k, n * T:n * T + T]
                m = V.do(lambda: nc.vector.tensor_scalar(
                    d, d, self.mod_col(l, 3 * s + 1, k, n), self.mod_col(l, 3 * s, k, n), MUL, ADD))
        self.P.wait(m)

    def gated_sum(self, o, l, which, m, nt, done):
        for n in range(nt // T):
            h = self.H[:, bass.ds(m, 1), n * T:n * T + T].rearrange("p a t -> p (a t)")
            f = self.V.do(lambda: self.nc.vector.scalar_tensor_tensor(
                h, o[:, n * T:n * T + T], self.mod_col(l, which, m, n), h, MUL, ADD), done)
        return f

    def ffn(self, l, s):
        P_, V, A, nc, ctl = self.P, self.V, self.A, self.nc, self.ctl
        nt = T if (l, s) == (DEPTH2 - 1, 1) else 2 * T
        tmp = Arena(self.arena, self.arena_size)
        hm, U, sq = tmp(KT, 2 * T), tmp(FT, 2 * T), tmp(KT, 2 * T)
        act = [tmp(2 * T) for _ in range(4)]
        self.modulated(l, 2 * s, hm, sq, nt)

        def pair(m, j):
            P_.wait(ctl.last(f"u{j}"))
            w = self.take()
            a, b = self.bank[2 * j][:, 0:nt], self.bank[2 * j + 1][:, 0:nt]
            self.product(a, w, KT, lambda k: hm[:, k, 0:nt], 0, False)
            done = self.product(b, w, KT, lambda k: hm[:, k, 0:nt], KT, True)
            A.wait(ctl.last(f"u{j}"))
            g = A.do(lambda: nc.scalar.activation(act[j][:, 0:nt], a, ACT.Silu), done)
            u = U[:, bass.ds(m, 1), 0:nt].rearrange("p a t -> p (a t)")
            ctl.note(f"u{j}", V.do(lambda: nc.vector.tensor_tensor(u, act[j][:, 0:nt], b, MUL), g))

        full = FT // NS
        ctl.loop_over(full, [ENG.PE, ENG.DVE, ENG.Activation],
                      lambda i: [pair(i * NS + j, j) for j in range(NS)])
        for j in range(FT % NS):
            pair(full * NS + j, j)
        self.bounds(P_)

        def down(i):
            for j in range(4):
                P_.wait(ctl.last(f"d{j}"))
                o = self.bank[j][:, 0:nt]
                h = FT // 2
                self.product(o, self.take(), h, lambda k: U[:, k, 0:nt], 0, True, True, False)
                done = self.product(o, self.take(), h, lambda k: U[:, h + k, 0:nt], 0, True, False, True)
                ctl.note(f"d{j}", self.gated_sum(o, l, 6 * s + 2, i * 4 + j, nt, done))

        ctl.loop_over(2, [ENG.PE, ENG.DVE], down)
        self.bounds()

    def softmax_units(self, units, scale, sc, on_pair):
        P_, V, A, nc = self.P, self.V, self.A, self.nc
        v_, s_ = nc.vector, nc.scalar
        ctl = self.ctl
        pr, pt, st, sb = sc
        for n, (qs, ks, nk, vs, out, bias, close) in enumerate(units):
            d, b = n % 2, self.bank[n % 2]
            P_.wait(ctl.last(f"s{d}"))
            for c, (q, k) in enumerate(zip(qs, ks)):
                mk = self.mm(b[:, 0:nk], q, k, c == 0, c == len(qs) - 1)
                m = P_.do(mk) if c == len(qs) - 1 else P_.quiet(mk)
            mx, ng, sm, rc = (st[:, d, k:k + 1] for k in range(4))
            src, sscale = b[:, 0:nk], scale
            V.wait(ctl.last(f"p{d}"))
            if bias is not None:
                V.do(lambda: v_.scalar_tensor_tensor(sb[:, d, 0:T], b[:, 0:T], scale, bias, MUL, ADD), m)
                V.do(lambda: v_.tensor_scalar(sb[:, d, T:nk], b[:, T:nk], scale, None, MUL))
                ctl.note(f"s{d}", V.now())
                src, sscale = sb[:, d, 0:nk], 1.0
            V.do(lambda: v_.reduce_max(mx, src, AX), m, V.now() if bias is not None else None)
            m = V.do(lambda: v_.tensor_scalar(ng, mx, -sscale, None, MUL), V.now())
            A.wait(ctl.last(f"t{d}"))
            m = A.do(lambda: s_.activation(pr[:, d, 0:nk], src, ACT.Exp, bias=ng, scale=sscale,
                                           accum_out=sm), m)
            if bias is None:
                ctl.note(f"s{d}", m)
            V.do(lambda: v_.reciprocal(rc, sm), m)
            m = V.do(lambda: v_.tensor_scalar(pr[:, d, 0:nk], pr[:, d, 0:nk], rc, None, MUL), V.now())
            tb = self.bank[2 + d]
            P_.wait(ctl.last(f"e{d}"))
            P_.wait(m)
            nb = nk // P
            for k in range(nb):
                m = P_.do(lambda: nc.tensor.transpose(tb[:, P * k:P * k + P], pr[:, d, P * k:P * k + P],
                                                      self.ident[:, :]))
            ctl.note(f"t{d}", m)
            ctl.note(f"p{d}", m)
            A.wait(ctl.last(f"o{d}"))
            m = A.do(lambda: s_.copy(pt[:, d, 0:nk], tb[:, 0:nk]), m)
            ctl.note(f"e{d}", m)
            P_.wait(m)
            if close == "first":
                P_.wait(ctl.last("pair"))
            for k in range(nb):
                m = P_.do(self.mm(out, vs[k], pt[:, d, P * k:P * k + P], k == 0, k == nb - 1))
            ctl.note(f"o{d}", m)
            if close == "last":
                on_pair(n, m)

    def headnorm(self, tile, sums, gain, div, nt, tmp, rope=None, dst=None, squares=None):
        P_, V, A, nc, ctl = self.P, self.V, self.A, self.nc, self.ctl
        v_ = nc.vector
        n = self.hn = (self.hn + 1) % 2
        bank, rs, rot = self.bank[4 + n], tmp[n][:, 0:nt], tmp[n][:, 0:T]
        dst = tile if dst is None else dst
        P_.wait(ctl.last(f"hn{n}"))
        for k, (mat, sqr) in enumerate(sums):
            mk = self.mm(bank[:, 0:nt], mat, sqr, k == 0, k == len(sums) - 1)
            m = P_.do(mk, squares) if k == len(sums) - 1 else P_.quiet(mk, squares)
        V.wait(V.now())
        m = self.rstd(rs, bank[:, 0:nt], 1.0 / div, RMS_EPS, m)
        m = V.do(lambda: v_.scalar_tensor_tensor(dst, tile, gain, rs, MUL, MUL), m)
        if rope:
            mat, cos, sin = rope
            m = P_.do(self.mm(bank[:, 0:T], mat, dst[:, 0:T], True, True), m)
            V.do(lambda: v_.tensor_tensor(rot, bank[:, 0:T], sin, MUL), m)
            V.do(lambda: v_.tensor_tensor(dst[:, 0:T], dst[:, 0:T], cos, MUL))
            m = V.do(lambda: v_.tensor_tensor(dst[:, 0:T], dst[:, 0:T], rot, ADD), V.now())
        ctl.note(f"hn{n}", m)
        return m

    def mixer_ab(self):
        P_, V, A, nc, ctl, t = self.P, self.V, self.A, self.nc, self.ctl, self.t
        v_, s_ = nc.vector, nc.scalar
        N = 2 * T
        self.hn = 0
        tmp = Arena(self.arena, self.arena_size)
        hm, sq = tmp(KT, N), tmp(KT, N)
        AQ, AK, BQN, BQR, KV, KR = (tmp(n, N) for n in (4, 1, 4, 2, 2, 1))
        BKN, BKR = tmp(4, N), tmp(2, N)
        AV, BV = tmp(4, P), tmp(4, 512)
        con = tmp(128 * 7 + 4 * T)
        nt2 = [tmp(N) for _ in range(2)]
        got = self.misc.start(self.G, con, t["ab_consts"][:, :])
        blk32, E0, E1, F0, F1, RA, RB = (con[:, P * k:P * k + P] for k in range(7))
        cosA, sinA, cosB, sinB = (con[:, 896 + T * k:896 + T * k + T] for k in range(4))
        self.modulated(0, 1, hm, sq, N)
        tiles_ = [AQ[:, k, :] for k in range(4)] + [AK[:, 0, :]] + [BQN[:, k, :] for k in range(4)] + \
            [BQR[:, k, :] for k in range(2)] + [KV[:, k, :] for k in range(2)] + [KR[:, 0, :]]
        free = [None] * 8
        for c in range(7):
            w = self.take()
            for e in range(2):
                m = 2 * c + e
                b = m % 8
                P_.wait(free[b])
                done = self.product(self.bank[b][:, :], w, KT, lambda k: hm[:, k, :], e * KT, e == 1)
                q = V if e else A
                cp = (lambda: v_.tensor_copy(tiles_[m], self.bank[b][:, :])) if e else \
                    (lambda: s_.copy(tiles_[m], self.bank[b][:, :]))
                free[b] = q.do(cp, done)
        w = self.take()
        P_.wait(free[6])
        for tb in range(4):
            for k in range(KT):
                mk = self.mm(self.bank[6][:, P * tb:P * tb + P], hm[:, k, P * tb:P * tb + P],
                             w[:, P * k:P * k + P], k == 0, k == KT - 1)
                if (tb, k) == (3, KT - 1):
                    m = self.give(mk)
                else:
                    P_.quiet(mk)
        A.do(lambda: s_.copy(AV.rearrange("p a b -> p (a b)"), self.bank[6][:, :]), m)
        for q in (V, P_, A):
            q.wait(got)
        self.bounds()
        A.do(lambda: s_.activation(sq[:, 0:2, :], KV[:, :, :], ACT.Square))
        m = A.do(lambda: s_.activation(sq[:, 2, :], KR[:, 0, :], ACT.Square))
        both = [(self.ones[:, :], sq[:, k, :]) for k in range(2)]
        for k in range(2):
            m2 = self.headnorm(KV[:, k, :], both, self.col("kvn", k), 256, N, nt2, squares=m)
        w = self.take()
        P_.wait(m2)
        for k in range(4):
            b = self.bank[k]
            for c in range(2):
                mk = self.mm(b[:, :], w[:, P * (2 * k + c):P * (2 * k + c + 1)], KV[:, c, :],
                             c == 0, c == 1)
                m3 = P_.do(mk) if c else P_.quiet(mk)
            A.do(lambda: s_.copy(BKN[:, k, :], b[:, :]), m3)
        P_.wait(A.now())
        for tb in range(4):
            for c in range(2):
                mk = self.mm(self.bank[tb][:, :], KV[:, c, P * tb:P * tb + P],
                             w[:, 1024 + 512 * c:1536 + 512 * c], c == 0, c == 1)
                if (tb, c) == (3, 1):
                    m3 = self.give(mk)
                else:
                    m3 = P_.do(mk) if c else P_.quiet(mk)
            V.do(lambda: v_.tensor_copy(BV[:, tb, :], self.bank[tb][:, :]), m3)
        blk64 = self.blk64[:, :]
        m = A.do(lambda: s_.activation(sq[:, 3:7, :], BKN[:, :, :], ACT.Square), A.now())
        rb = (RB, cosB, sinB)
        for k in range(4):
            self.headnorm(BKN[:, k, :], [(blk64, sq[:, 3 + k, :]), ((E0, E1)[k % 2], sq[:, 2, :])],
                          self.col("bkn"), 96, N, nt2, squares=m)
        for k in range(2):
            self.headnorm(KR[:, 0, :], [(blk32, sq[:, 2, :]), (F0, sq[:, 3 + 2 * k, :]),
                                        (F1, sq[:, 4 + 2 * k, :])],
                          self.col("bkr"), 96, N, nt2, rope=rb, dst=BKR[:, k, :])
        A.wait(P_.now())
        A.do(lambda: s_.activation(sq[:, 0:4, :], BQN[:, :, :], ACT.Square))
        m = A.do(lambda: s_.activation(sq[:, 4:6, :], BQR[:, :, :], ACT.Square))
        for k in range(4):
            self.headnorm(BQN[:, k, :], [(blk64, sq[:, k, :]), ((E0, E1)[k % 2], sq[:, 4 + k // 2, :])],
                          self.col("bqn"), 96, N, nt2, squares=m)
        for k in range(2):
            self.headnorm(BQR[:, k, :], [(blk32, sq[:, 4 + k, :]), (F0, sq[:, 2 * k, :]),
                                         (F1, sq[:, 2 * k + 1, :])],
                          self.col("bqr"), 96, N, nt2, rope=rb)
        A.wait(P_.now())
        A.do(lambda: s_.activation(sq[:, 0:4, :], AQ[:, :, :], ACT.Square))
        m = A.do(lambda: s_.activation(sq[:, 4, :], AK[:, 0, :], ACT.Square))
        ra = (RA, cosA, sinA)
        for k in range(4):
            self.headnorm(AQ[:, k, :], [(blk64, sq[:, k, :])], self.col("aqn"), 64, N, nt2, rope=ra,
                          squares=m)
        self.headnorm(AK[:, 0, :], [(blk64, sq[:, 4, :])], self.col("akn"), 64, N, nt2, rope=ra)
        self.bounds()

        wk = Arena(self.arena, self.arena_size)
        att = wk(KT, N)
        qm, kn, kr, vb = wk(2, 2, N), wk(N), wk(N), wk(4, P)
        sc = (tmp(2, N), tmp(2, N), tmp(2, 4), None)
        assert wk.at <= 2 * KT * N

        def streams(e, q, k, v, bank):
            for qb in range(4):
                k0, tb0 = (0, 0) if qb < 2 else (T, 2)
                yield (tuple(a[:, P * qb:P * qb + P] for a in q), tuple(a[:, k0:N] for a in k), N - k0,
                       [v[:, tb, 64 * e:64 * e + 64] for tb in range(tb0, 4)],
                       bank[64 * e:64 * e + 64, P * qb:P * qb + P], None,
                       {(0, 0): "first", (1, 3): "last"}.get((e, qb)))

        def heads(i, first, Q, rope):
            for q in (V, A):
                q.wait(ctl.last("pair_p"))
            qt = Q[:, bass.ds(i, 1), :].rearrange("p a t -> p (a t)")
            for e in range(2):
                V.do(lambda: v_.tensor_scalar(qm[:, 0, e, :], qt, self.col("half", e), None, MUL))
            if rope is not None:
                r, p = rope
                qr = BQR[:, bass.ds(r, 1), :].rearrange("p a t -> p (a t)")
                for e in range(2):
                    V.do(lambda: v_.tensor_scalar(qm[:, 1, e, :], qr, self.col("quart", 2 * p + e),
                                                  None, MUL))
                V.do(lambda: v_.tensor_copy(kn, BKN[:, bass.ds(i, 1), :].rearrange("p a t -> p (a t)")))
                V.do(lambda: v_.tensor_copy(kr, BKR[:, bass.ds(r, 1), :].rearrange("p a t -> p (a t)")))
                V.do(lambda: v_.tensor_copy(vb[:, :, :], BV[:, :, bass.ds(i * P, P)]))
            P_.wait(V.now())
            units = []
            for e in range(2):
                if rope is None:
                    units += streams(e, (qm[:, 0, e, :],), (AK[:, 0, :],), AV, self.bank[6])
                else:
                    units += streams(e, (qm[:, 0, e, :], qm[:, 1, e, :]), (kn, kr), vb, self.bank[6])

            def pair(n, m):
                out = att[:, bass.ds(i + first, 1), :].rearrange("p a t -> p (a t)")
                ctl.note("pair", A.do(lambda: s_.copy(out, self.bank[6][:, :]), m))

            self.softmax_units(units, (64 if rope is None else 96) ** -0.5, sc, pair)
            ctl.note("pair_p", P_.now())

        engines = [ENG.PE, ENG.DVE, ENG.Activation]
        ctl.straight.clear()
        ctl.loop_over(4, engines, lambda i: heads(i, 0, AQ, None))
        self.bounds()
        ctl.loop_over(2, engines, lambda r: [heads(r * 2 + p, 4, BQN, (r, p)) for p in range(2)])
        self.bounds()
        self.mixer_out(0, att, N)

    def mixer_out(self, l, att, nt):
        for c in range(4):
            w = self.take()
            for e in range(2):
                m = 2 * c + e
                o = self.bank[m][:, 0:nt]
                done = self.product(o, w, KT, lambda k: att[:, k, 0:nt], e * KT, e == 1)
                self.gated_sum(o, l, 5, m, nt, done)
        self.bounds()


    def mixer_cd(self):
        P_, V, A, Gq, nc, ctl, t = self.P, self.V, self.A, self.G, self.nc, self.ctl, self.t
        v_, s_, tt, bank = nc.vector, nc.scalar, nc.vector.tensor_tensor, self.bank
        N = 2 * T
        self.hn = 0
        tmp = Arena(self.arena, self.arena_size)
        DQ, DK, IV, DV = tmp(4, T), tmp(4, N), tmp(4, 512), tmp(4, 512)
        Q, GT, ZF, ZB = tmp(4, T), tmp(4, T), tmp(4, N), tmp(4, N)
        att = tmp(KT, T)
        base = tmp.at
        hm, sq = tmp(KT, N), tmp(KT, N)
        self.modulated(1, 1, hm, sq, N)
        places = [(ZF[:, k, :], N) for k in range(4)] + [(ZB[:, k, :], N) for k in range(4)] + \
            [(DK[:, k, :], N) for k in range(4)] + [(Q[:, k, :], T) for k in range(4)] + \
            [(GT[:, k, :], T) for k in range(4)] + [(DQ[:, k, :], T) for k in range(4)]
        free = [None] * 8
        for c in range(12):
            w = self.take()
            for e in range(2):
                m = 2 * c + e
                b, (dst, n) = m % 8, places[m]
                P_.wait(free[b])
                done = self.product(bank[b][:, 0:n], w, KT, lambda k: hm[:, k, 0:n], e * KT, e == 1)
                if 12 <= m < 20:
                    free[b] = A.do(lambda: s_.activation(dst, bank[b][:, 0:n], ACT.Silu), done)
                else:
                    free[b] = V.do(lambda: v_.tensor_copy(dst, bank[b][:, 0:n]), done)
        for f in free:
            P_.wait(f)
        for n, dst in enumerate((IV, DV)):
            for h in range(2):
                w = self.take()
                for tb in range(4):
                    for k in range(4):
                        mk = self.mm(bank[4 * n + tb][:, :], hm[:, 4 * h + k, P * tb:P * tb + P],
                                     w[:, 512 * k:512 * k + 512], h + k == 0, h == 1 and k == 3)
                        if (tb, k) == (3, 3):
                            m = self.give(mk)
                        else:
                            P_.quiet(mk)
            for tb in range(4):
                A.do(lambda: s_.copy(dst[:, tb, :], bank[4 * n + tb][:, :]), m)
        self.bounds()

        wk = Arena(self.arena, self.arena_size)
        wk.at = base
        masks = wk(16, P)
        got = self.misc.start(Gq, masks.rearrange("p a b -> p (a b)"), t["h_masks"][:, :])
        for q in (V, P_, A):
            q.wait(got)
        KY, PS, SS = wk(4, N), wk(4, N), wk(4, N)
        M, Mq = wk(4, T), wk(4, T)
        AT = wk(16, P)
        khT = wk(3, 4, P)
        ST, lbt, zero = wk(4, P), wk(8), wk(512)
        flat = lambda ap: ap.rearrange("p a b -> p (a b)")
        V.do(lambda: v_.memset(zero, 0.0))
        d = self.cols[:, COLS["lb1"]:COLS["lb1"] + 8]
        d0 = self.cols[:, COLS["lb0"]:COLS["lb0"] + 8]
        lb, ol = wk(8), wk(8)
        V.do(lambda: tt(lbt, d, d0, SUB))
        A.do(lambda: s_.activation(lb, lbt, ACT.Sigmoid), V.now())
        m = A.do(lambda: s_.activation(ol, lbt, ACT.Sigmoid, scale=-1.0))
        V.wait(m)
        P_.wait(V.now())
        OB = [bank[6], bank[7]]
        for b in OB:
            P_.quiet(lambda: nc.tensor.matmul(b[:, :], zero[:, 0:P], zero, start=True, stop=False,
                                              skip_group_check=True))
        outp = lambda i, e, tb: OB[i // 2][64 * e:64 * e + 64, T * (i % 2) + P * tb:T * (i % 2) + P * tb + P]

        def add(out, lhsT, rhs):
            return lambda: nc.tensor.matmul(out, lhsT, rhs, start=False, stop=False,
                                            skip_group_check=True)

        for dr, Z in enumerate((ZF, ZB)):
            a1 = A.do(lambda: s_.activation(flat(PS), flat(Z), ACT.Sigmoid), V.now(), P_.now())
            a2 = A.do(lambda: s_.activation(flat(KY), flat(Z), ACT.Sigmoid, scale=-1.0))
            for k in range(4):
                c = 4 * dr + k
                V.do(lambda: v_.tensor_scalar(PS[:, k, :], PS[:, k, :], ol[:, c:c + 1], lb[:, c:c + 1],
                                              MUL, ADD), a1)
            for k in range(4):
                c = 4 * dr + k
                V.do(lambda: v_.tensor_scalar(KY[:, k, :], KY[:, k, :], ol[:, c:c + 1], None, MUL), a2)
            V.do(lambda: v_.tensor_scalar(flat(PS), flat(PS), 1.1e-19, None, MAX), V.now())
            m = A.do(lambda: s_.activation(flat(PS), flat(PS), ACT.Ln), V.now())
            V.do(lambda: v_.memset(flat(SS), 0.0))
            V.wait(m)
            A.wait(V.now())
            tg, so = (1, 0) if dr == 0 else (0, 1)

            def score(units, mask, lhs, rhs, after):
                P_.wait(after)
                for e in range(2):
                    rows = slice(64 * e, 64 * e + 64)
                    for i in range(4):
                        for tb in range(2):
                            u, tk = i * 2 + tb, slice(P * tb, P * tb + P)
                            o = bank[2 * e + u // 4][:, P * (u % 4):P * (u % 4) + P]
                            m = P_.do(self.mm(o, lhs[rows, i, tk], rhs[rows, i, tk], True, True))
                V.wait(m)
                for q in range(4):
                    a = V.do(lambda: tt(AT[:, 4 * q:4 * q + 4, :],
                                        bank[q][:, :].rearrange("p (u t) -> p u t", u=4),
                                        bc(masks[:, mask, :], 4), MUL))
                P_.wait(a)
                for e in range(2):
                    for i in range(4):
                        for tb in range(2):
                            m = P_.do(add(outp(i, e, tb), IV[:, tb, P * i + 64 * e:P * i + 64 * e + 64],
                                          AT[:, 8 * e + 2 * i + tb, :]))
                return m

            used = score(16, 14, KY, Q, V.now())
            for lv in range(7):
                h = 1 << lv
                halves = lambda ap, n: ap.rearrange("p a (b two h) -> p (a b) two h", two=2, h=h) \
                    if n == N else ap[:, :, 0:T].rearrange("p a (b two h) -> p a b two h", two=2, h=h)
                x4 = lambda ap, w: halves(ap, T)[:, :, :, w, :]
                A.wait(used)
                A.do(lambda: s_.activation(x4(M, tg), x4(PS, tg), ACT.Exp), V.now())
                m = A.do(lambda: s_.activation(x4(M, so), x4(SS, so), ACT.Exp))
                V.do(lambda: tt(x4(M, tg), x4(M, tg), x4(Q, tg), MUL), m)
                mq = V.do(lambda: tt(x4(M, so), x4(M, so), x4(KY, so), MUL))
                p, s = halves(PS, N), halves(SS, N)
                last = (h - 1) if dr == 0 else 0
                n = 4 * N // (2 * h)
                tot = lambda w: p[:, :, w, last:last + 1].broadcast_to([P, n, h])
                V.do(lambda: tt(s[:, :, so, :], s[:, :, so, :], tot(tg), ADD))
                V.do(lambda: tt(p[:, :, tg, :], p[:, :, tg, :], tot(so), ADD), V.now())
                used = score(16, lv + 7 * dr, M, M, mq)
            V.wait(V.now())
            m = A.do(lambda: s_.activation(flat(SS), flat(SS), ACT.Exp), V.now())
            a1 = A.do(lambda: s_.activation(M[:, :, :], PS[:, :, 0:T], ACT.Exp), used)
            kh = V.do(lambda: tt(flat(SS), flat(SS), flat(KY), MUL), m)
            qh = V.do(lambda: tt(flat(Mq), flat(M), flat(Q), MUL), a1)
            order = (2, 3, 0, 1) if dr == 0 else (3, 2, 1, 0)
            P_.wait(kh)
            for n, b in enumerate(order[:3]):
                for i in range(4):
                    m = P_.do(lambda: nc.tensor.transpose(bank[n][:, P * i:P * i + P],
                                                          SS[:, i, P * b:P * b + P], self.ident[:, :]))
                A.do(lambda: s_.copy(flat(khT[:, n, :, :]), bank[n][:, :]), m)
            P_.wait(A.now())
            for n, b in enumerate(order[:3]):
                for i in range(4):
                    m = P_.do(self.mm(bank[3 + n][:, P * i:P * i + P], khT[:, n, i, :],
                                      IV[:, b, P * i:P * i + P], True, True))
            V.do(lambda: v_.memset(flat(ST), 0.0), m)
            V.wait(V.now())
            for n, b in enumerate(order):
                end = P * b + (P - 1 if dr == 0 else 0)
                if n >= 1:
                    pb = order[n - 1]
                    pe = P * pb + (P - 1 if dr == 0 else 0)
                    if n == 1:
                        V.do(lambda: v_.memset(zero[:, 0:8], 0.0))
                    for i in range(4):
                        V.do(lambda: v_.tensor_copy(lbt[:, i:i + 1], PS[:, i, pe:pe + 1]), V.now())
                    w = A.do(lambda: s_.activation(lbt[:, 4:8], lbt[:, 0:4], ACT.Exp), V.now())
                    V.wait(P_.now())
                    for e in range(2):
                        rw = slice(64 * e, 64 * e + 64)
                        for i in range(4):
                            sd = ST[rw, i, 64 * e:64 * e + 64]
                            u = bank[2 + n][rw, P * i + 64 * e:P * i + 64 * e + 64]
                            V.do(lambda: v_.scalar_tensor_tensor(sd, sd, lbt[rw, 4 + i:5 + i], u, MUL, ADD), w)
                if n >= 2:
                    P_.wait(V.now())
                    for i in range(4):
                        o = OB[i // 2][:, T * (i % 2) + P * b:T * (i % 2) + P * b + P]
                        m = P_.do(add(o, ST[:, i, :], Mq[:, i, P * b:P * b + P]))
            self.bounds()
        for b in OB:
            m = P_.do(lambda: nc.tensor.matmul(b[:, :], zero[:, 0:P], zero, start=False, stop=True,
                                               skip_group_check=True))
        O = M
        for k in range(2):
            V.do(lambda: v_.tensor_copy(flat(O[:, 2 * k:2 * k + 2, :]), OB[k][:, :]), m)
        m = A.do(lambda: s_.activation(flat(Mq), flat(O), ACT.Square), V.now())
        hn = [AT[:, 4 * k:4 * k + 4, :].rearrange("p a b -> p (a b)") for k in range(2)]
        for k in range(4):
            g = self.headnorm(O[:, k, :], [(self.blk64[:, :], Mq[:, k, :])], self.col("cgn"), 64, T, hn,
                              squares=m)
            V.do(lambda: tt(att[:, k, :], O[:, k, :], GT[:, k, :], MUL), g)
        m = A.do(lambda: s_.activation(flat(Mq), flat(DQ), ACT.Square), P_.now())
        for k in range(4):
            self.headnorm(DQ[:, k, :], [(self.blk64[:, :], Mq[:, k, :])], self.col("dqn"), 64, T, hn,
                          squares=m)
        m = A.do(lambda: s_.activation(flat(KY), flat(DK), ACT.Square))
        for k in range(4):
            self.headnorm(DK[:, k, :], [(self.blk64[:, :], KY[:, k, :])], self.col("dkn"), 64, N, hn,
                          squares=m)
        self.bounds()
        wk = Arena(self.arena, self.arena_size)
        wk.at = base
        bias, nm = wk(8, 2, T), wk(2, T)
        qm, kn, vb, bi = wk(2, T), wk(N), wk(4, P), wk(2, 2, T)
        sc = (wk(2, N), wk(2, N), wk(2, 4), wk(2, N))
        self.misc.start(Gq, bias.rearrange("p a b c -> p (a b c)"), t["d_bias"][:, :], V.now())
        got = self.misc.start(Gq, nm.rearrange("p b c -> p (b c)"), t["d_mask"][:, :])
        V.wait(got)
        V.do(lambda: tt(bias.rearrange("p a b c -> p a (b c)"), bias.rearrange("p a b c -> p a (b c)"),
                        bc(nm.rearrange("p b c -> p (b c)"), 8), ADD))
        V.wait(V.now())

        def heads(i):
            for q in (V, A):
                q.wait(ctl.last("pair_p"))
            V.wait(ctl.last("pair"))
            qt = DQ[:, bass.ds(i, 1), :].rearrange("p a t -> p (a t)")
            for e in range(2):
                V.do(lambda: v_.tensor_scalar(qm[:, e, :], qt, self.col("half", e), None, MUL))
            V.do(lambda: v_.tensor_copy(kn, DK[:, bass.ds(i, 1), :].rearrange("p a t -> p (a t)")))
            V.do(lambda: v_.tensor_copy(vb[:, :, :], DV[:, :, bass.ds(i * P, P)]))
            V.do(lambda: v_.tensor_copy(bi[:, :, :, :], bias[:, bass.ds(i * 2, 2), :, :]))
            P_.wait(V.now())
            V.wait(V.now())
            units = [((qm[:, e, P * qb:P * qb + P],), (kn,), N,
                      [vb[:, tb, 64 * e:64 * e + 64] for tb in range(4)],
                      bank[6][64 * e:64 * e + 64, P * qb:P * qb + P], bi[:, e, qb, :],
                      {(0, 0): "first", (1, 1): "last"}.get((e, qb)))
                     for e in range(2) for qb in range(2)]

            def pair(n, m):
                out = att[:, bass.ds(i + 4, 1), :].rearrange("p a t -> p (a t)")
                ctl.note("pair", A.do(lambda: s_.copy(out, bank[6][:, 0:T]), m))

            self.softmax_units(units, 64 ** -0.5, sc, pair)
            ctl.note("pair_p", P_.now())

        ctl.straight.clear()
        ctl.loop_over(4, [ENG.PE, ENG.DVE, ENG.Activation], heads)
        self.bounds()
        self.mixer_out(1, att, T)


def build(nc, t, parts, dumps=()):
    with ExitStack() as es:
        m = Machine(nc, t, es)
        g = m.G
        first = Load(m.ctl, m.sem("s_first"), "first")
        for dst, name in ((m.cols, "cols"), (m.ident, "ident"), (m.ones, "ones"), (m.blk64, "blk64")):
            got = first.start(g, dst[:, :], t[name][:, :])
        got = first.start(g, m.H[:, :, 0:T], t["x"])
        for q in (m.P, m.V, m.A, g):
            q.wait(got)
        names = [s for p in parts for s in PART_STAGES[p]]
        m.feed(names)
        for p in parts:
            kind, l = p[:-1], int(p[-1])
            if kind == "conv":
                m.conv_layer(l)
            if kind == "ssm":
                m.ssm_layer(l)
            if kind == "rwkv":
                m.rwkv_layer(l)
            if kind == "ada":
                m.ada()
            if kind == "ffn":
                m.ffn(l // 2, l % 2)
            if kind == "ab":
                m.mixer_ab()
            if kind == "cd":
                m.mixer_cd()
        m.bounds(m.S)
        s_out = m.sem("s_out")
        m.S.eng.dma_start(t["out"], m.H[:, :, 0:T]).then_inc(s_out, 16)
        m.S.eng.wait_ge(s_out, 16)
        for n, (name, ap) in enumerate(m.dumps if dumps else ()):
            m.S.eng.dma_start(t[name], ap).then_inc(s_out, 16)
            m.S.eng.wait_ge(s_out, 16 * (n + 2))


PART_STAGES = {
    "conv0": ["conv_in0", "out0", "ple0"], "ssm1": ["ssm_in", "glu", "out1", "ple1"],
    "rwkv2": ["lora", "rkvz", "out2", "ple2"], "conv3": ["conv_in3", "out3", "ple3"], "ada0": ["ada"],
    "ffn0": ["f00a", "f00b"], "ab0": ["ab_in", "ab_av", "ukv", "ab_out"], "ffn1": ["f01a", "f01b"],
    "ffn2": ["f10a", "f10b"], "cd0": ["cd_in", "cd_v", "cd_out"], "ffn3": ["f11a", "f11b"],
}
PARTS = ["conv0", "ssm1", "rwkv2", "conv3", "ada0", "ffn0", "ab0", "ffn1", "ffn2", "cd0", "ffn3"]


def tiles(w, order):
    return np.concatenate([w[k * P:(k + 1) * P, m * P:(m + 1) * P] for k, m in order], axis=1)


def whole(w, per=2):
    nk, nm = w.shape[0] // P, w.shape[1] // P
    return np.stack([tiles(w, [(k, m) for m in range(c, c + per) for k in range(nk)])
                     for c in range(0, nm, per)])


def fcol(v):
    return np.ascontiguousarray(v.reshape(-1, P).T)


def fmajor(a):
    return np.ascontiguousarray(a.T.reshape(-1, P, a.shape[0]).transpose(1, 0, 2))


def lay_out(inp):
    o = {}
    o["x"] = fmajor(inp["x"][0])
    o["p"] = np.stack([fmajor(inp["p"][l, 0]) for l in range(DEPTH1)])
    for l in (0, 3):
        w = inp["conv_w_in"][l // 3]
        bg, cg, h, z = (w[:, k * D:(k + 1) * D] for k in range(4))
        o[f"conv_in{l}"] = np.concatenate([
            np.stack([np.concatenate([tiles(a, [(k, m) for k in range(KT)]) for a in ab], axis=1)
                      for ab in ((cg, h), (bg, z))]) for m in range(KT)])
        o[f"out{l}"] = whole(inp["conv_w_out"][l // 3])
    for l in range(DEPTH1):
        o[f"ple{l}"] = np.stack([np.concatenate([
            tiles(inp["ple_gate"][l], [(k, m) for k in range(KT)]),
            tiles(inp["ple_proj"][l], [(k, m) for k in range(2)])], axis=1) for m in range(KT)])
    c = np.zeros((P, NCOL), np.float32)

    def put(name, a):
        c[:, COLS[name]:COLS[name] + a.shape[1]] = a

    put("conv_k", np.concatenate([fcol(inp["conv_k"][j, s]) for j in range(2) for s in range(3)], 1))
    put("ln_g", np.concatenate([fcol(inp["ln_g"][l]) for l in range(4)], 1))
    put("ln_b", np.concatenate([fcol(inp["ln_b"][l]) for l in range(4)], 1))
    lay_out_more(inp, o, put)
    o["cols"] = c
    o["ident"] = np.eye(P, dtype=np.float32)
    o["ones"] = np.ones((P, P), np.float32)
    o["blk64"] = np.kron(np.eye(2), np.ones((64, 64))).astype(np.float32)
    return o


def lay_out_more(inp, o, put):
    o["ssm_in"], o["glu"] = whole(inp["ssm_w_in"][0]), whole(inp["ssm_w_glu"][0])
    o["out1"] = whole(inp["ssm_w_out"][0])
    twice = lambda a: np.ascontiguousarray(np.concatenate([a.T, a.T]))
    o["s_lre"], o["s_lim"] = twice(inp["ssm_lam_re"][0]), twice(inp["ssm_lam_im"][0])
    o["s_ldt"] = np.ascontiguousarray(np.broadcast_to(inp["ssm_log_dt"][0][None], (P, G)))
    br, bi = (inp[n][0].transpose(1, 0, 2).reshape(NP_, G * GH) for n in ("ssm_b_re", "ssm_b_im"))
    cr, ci = (inp[n][0].transpose(2, 0, 1).reshape(NP_, G * GH) for n in ("ssm_c_re", "ssm_c_im"))
    o["s_b1"], o["s_b2"] = np.concatenate([br, bi]), np.concatenate([bi, br])
    o["s_c1"], o["s_c2"] = np.concatenate([cr, ci]), np.concatenate([ci, cr])
    put("ssm_d", fcol(inp["ssm_d"][0]))
    put("b_glu", fcol(inp["ssm_b_glu"][0]))
    put("sgn", np.concatenate([-np.ones((64, 1)), np.ones((64, 1))]))
    o["rkvz"] = np.concatenate([whole(inp["rwkv_w_rkvz"][0, n]) for n in range(4)])
    o["out2"] = whole(inp["rwkv_w_out"][0])
    low = lambda w: w.reshape(KT, P, 64).transpose(1, 0, 2).reshape(P, 512)
    o["lora"] = np.concatenate([low(inp["rwkv_w1"][0]), low(inp["rwkv_a1"][0]),
                                np.concatenate([inp["rwkv_w2"][0], inp["rwkv_a2"][0]])], axis=1)[None]
    put("mu", np.concatenate([fcol(inp["rwkv_mu"][0, n]) for n in range(6)], 1))
    for name in ("w0", "a0", "k_k", "k_a", "r_k", "lnx_g", "lnx_b"):
        put(name, fcol(inp["rwkv_" + name][0]))
    put("half", np.kron(np.eye(2), np.ones((64, 1))))
    s_, t_ = np.meshgrid(np.arange(P), np.arange(P), indexing="ij")
    chunk = s_ // 64 == t_ // 64

    def joins(lv):
        return (s_ >> (lv + 1) == t_ >> (lv + 1)) & ((t_ >> lv) % 2 == 1) & ((s_ >> lv) % 2 == 0)

    o["r_masks"] = np.concatenate(
        [chunk & (s_ < t_), chunk & (s_ <= t_), (chunk & (s_ < t_)).T, joins(0).T, joins(0)]
        + [joins(lv) for lv in range(1, 6)], axis=1).astype(np.float32)
    o["ctx"] = fmajor(inp["ctx_2"][0])
    c2 = np.stack([inp["c_2"][0].reshape(KT, P), inp["c_ctx_2"].reshape(KT, P)], axis=-1)
    put("c", c2.transpose(1, 0, 2).reshape(P, 2 * KT))
    o["ada"] = np.concatenate([whole(inp["ada_w_2"][l]) for l in range(DEPTH2)])
    put("ada_b", np.concatenate([fcol(inp["ada_b_2"][l]) for l in range(DEPTH2)], 1))
    put("norm_g", np.concatenate([fcol(inp["norm_g_2"][l, s]) for l in range(2) for s in range(3)], 1))
    for l in range(DEPTH2):
        for s in range(2):
            w1, w3, w2 = (inp[n][l, s] for n in ("ffn_w1_2", "ffn_w3_2", "ffn_w2_2"))
            o[f"f{l}{s}a"] = np.concatenate([whole(w1, 1), whole(w3, 1)], axis=2)
            o[f"f{l}{s}b"] = whole(w2, 1).reshape(KT, P, 2, FT // 2 * P).transpose(0, 2, 1, 3).reshape(
                2 * KT, P, FT // 2 * P)
    w = inp["ab_w_in_2"][0]
    ab = {}
    at = 0
    for name, n in (("aq", 512), ("ak", 128), ("av", 128), ("bq", 768), ("bkv", 256), ("bkr", 32)):
        ab[name] = w[:, at:at + n]
        at += n
    perm = [h for i in range(4) for h in (i, i + 4)]
    aq = ab["aq"].reshape(D, 8, 64)[:, perm].reshape(D, 512)
    bq = ab["bq"].reshape(D, 8, 96)
    o["ab_in"] = whole(np.concatenate([aq, ab["ak"], bq[:, :, :64].reshape(D, 512),
                                       bq[:, :, 64:].reshape(D, 256), ab["bkv"],
                                       np.tile(ab["bkr"], (1, 4))], axis=1))
    o["ab_av"] = moving(ab["av"])[None]
    u = inp["ab_b_wukv_2"][0].reshape(256, 8, 128)
    o["ukv"] = np.concatenate([tiles(u[:, :, :64].reshape(256, 512), [(k, m) for m in range(4) for k in (0, 1)]),
                               moving(u[:, :, 64:].reshape(256, 512))], axis=1)[None]
    wo = inp["ab_w_out_2"][0]
    o["ab_out"] = whole(np.concatenate([wo[:512].reshape(8, 64, D)[perm].reshape(512, D), wo[512:]]))
    put("aqn", np.tile(inp["ab_a_qn_2"][0], 2)[:, None])
    put("akn", np.tile(inp["ab_a_kn_2"][0], 2)[:, None])
    for name, g in (("bq", inp["ab_b_qn_2"][0]), ("bk", inp["ab_b_kn_2"][0])):
        put(name + "n", np.tile(g[:64], 2)[:, None])
        put(name + "r", np.tile(g[64:], 4)[:, None])
    put("kvn", fcol(inp["ab_b_kvn_2"][0]))
    put("quart", np.kron(np.eye(4), np.ones((32, 1))))
    f = np.arange(P)
    E = [(f[:, None] // 32 == 2 * p + f[None] // 64) for p in range(2)]

    def rotate(hb):
        r = np.zeros((P, P))
        for d in range(P):
            if d % hb < hb // 2:
                r[d + hb // 2, d] = -1
            else:
                r[d - hb // 2, d] = 1
        return r

    def rope(dim):
        inv = np.float32(10000.0) ** (-np.arange(0, dim // 2, 2, dtype=np.float32) / np.float32(dim // 2))
        pos = np.arange(T)
        ang = np.concatenate([np.concatenate([a, a], 1) for a in
                              ((pos // 64)[:, None] * inv[None], (pos % 64)[:, None] * inv[None])], 1)
        ang = np.tile(ang.astype(np.float32).T, (P // dim, 1))
        return [np.cos(ang), np.sin(ang)]

    o["ab_consts"] = np.concatenate(
        [f[:, None] // 32 == f[None] // 32, E[0], E[1], E[0].T, E[1].T, rotate(32), rotate(16)]
        + rope(64) + rope(32), axis=1).astype(np.float32)

    w = inp["cd_w_in_2"][0]
    q, zf, zb, iv, gate, dq, dk, dv = (w[:, 512 * k:512 * k + 512] for k in range(8))
    o["cd_in"] = whole(np.concatenate([zf, zb, dk, q, gate, dq], axis=1))
    o["cd_v"] = np.concatenate([moving(a).reshape(P, 2, 4 * 512).transpose(1, 0, 2) for a in (iv, dv)])
    o["cd_out"] = whole(inp["cd_w_out_2"][0])
    for n in range(2):
        put(f"lb{n}", np.concatenate([fcol(inp["hgrn_lb_2"][n, d]) for d in range(2)], 1))
    for name, key in (("cgn", "cd_c_gn_2"), ("dqn", "cd_d_qn_2"), ("dkn", "cd_d_kn_2")):
        put(name, np.tile(inp[key][0], 2)[:, None])
    none = np.zeros((P, P))
    o["h_masks"] = np.concatenate([joins(lv) for lv in range(7)] + [joins(lv).T for lv in range(7)]
                                  + [np.eye(P), none], axis=1).astype(np.float32)
    tok = np.arange(T)
    row, col = tok // 64, tok % 64
    start = np.clip(col - 8, 0, 48)
    inside = (col[None] >= start[:, None]) & (col[None] < start[:, None] + 16)
    dr = row[None] - row[:, None] + 7
    dc = np.where(inside, col[None] - col[:, None] + 15, 0)
    rpb = np.where(inside[None], inp["cd_d_rpb_2"][0][:, dr, dc], np.float32(0))
    o["d_bias"] = np.ascontiguousarray(rpb.reshape(8, 2, P, T).transpose(2, 0, 1, 3).reshape(P, -1))
    o["d_mask"] = np.where(inside, 0, NEG).astype(np.float32).reshape(2, P, T).transpose(
        1, 0, 2).reshape(P, -1)


def moving(w):
    return np.ascontiguousarray(w.reshape(-1, P, w.shape[1]).transpose(1, 0, 2).reshape(P, -1))


def kernel(**inputs):
    import concourse.bacc as bacc
    from concourse.bass_utils import run_bass_kernel_spmd

    arrays = lay_out({k: np.asarray(v) for k, v in inputs.items()})
    nc = bacc.Bacc("TRN2", target_bir_lowering=False, num_devices=1)
    t, send = {}, {}
    for name, a in arrays.items():
        send["in_" + name] = np.ascontiguousarray(a)
        t[name] = nc.dram_tensor("in_" + name, a.shape, F32, kind="ExternalInput").ap()
    for name in ("scratch_u", "scratch_y"):
        t[name] = nc.dram_tensor(name, (D * T,), F32, kind="Internal").ap()
    t["out"] = nc.dram_tensor("out_x", (P, KT, T), F32, kind="ExternalOutput").ap()
    build(nc, t, PARTS)
    got = run_bass_kernel_spmd(nc, [send], core_ids=[0]).results[0]["out_x"]
    return np.ascontiguousarray(got.transpose(1, 0, 2).reshape(D, T).T)[None]
```

```python
from contextlib import ExitStack

import numpy as np

import concourse.bass as bass
from concourse import mybir

F32, F32R = mybir.dt.float32, mybir.dt.float32r
ALU = mybir.AluOpType
ACT = mybir.ActivationFunctionType
AX = mybir.AxisListType.X
ENG = mybir.EngineType
MUL, ADD, SUB, MAX, MIN, BYP = ALU.mult, ALU.add, ALU.subtract, ALU.max, ALU.min, ALU.bypass

P = 128
D = 1024
KT = D // P
T = 256
DEPTH1, DEPTH2 = 4, 2
ALPHA = (2 * DEPTH1) ** 0.25
LN_EPS, GN_EPS, RMS_EPS = 1e-5, 64e-5, 1e-6
FF = 2816
FT = FF // P
G, NP_, GH = 64, 64, 16
SL = 8
SC = T // SL
NS = 4
SLOT = 16 * P
ADA = DEPTH2 * 9 * D // 512
ADA_SSM = 20
START = 4000
NEG = -1e30

COLS = {}


def _cols():
    at = 0
    for name, n in (("conv_k", 48), ("ssm_d", 8), ("b_glu", 8), ("mu", 48), ("w0", 8), ("a0", 8),
                    ("k_k", 8), ("k_a", 8), ("r_k", 8), ("lnx_g", 8), ("lnx_b", 8), ("ln_g", 32),
                    ("ln_b", 32), ("norm_g", 48), ("ada_b", 144), ("c", 16), ("aqn", 1), ("akn", 1),
                    ("bqn", 1), ("bqr", 1), ("bkn", 1), ("bkr", 1), ("kvn", 2), ("lb0", 8),
                    ("lb1", 8), ("cgn", 1), ("dqn", 1), ("dkn", 1), ("sgn", 1), ("half", 2), ("quart", 4)):
        COLS[name] = at
        at += n
    return at


NCOL = _cols()

STAGES = {}


def _stages():
    for l in range(DEPTH1):
        if l % 3 == 0:
            STAGES[f"conv_in{l}"] = (16, 2048)
        elif l == 1:
            STAGES["ssm_in"] = (8, 2048)
            STAGES["glu"] = (4, 2048)
        else:
            STAGES["rkvz"] = (16, 2048)
            STAGES["lora"] = (1, 2048)
        STAGES[f"out{l}"] = (4, 2048)
        STAGES[f"ple{l}"] = (8, 1280)
    STAGES["ada_s"] = (2 * ADA_SSM, 2048)
    STAGES["ada_r"] = (2 * (ADA - ADA_SSM), 2048)
    for l in range(DEPTH2):
        STAGES[f"f{l}0a"] = (22, 2048)
        STAGES[f"f{l}0b"] = (16, 1408)
        if l == 0:
            STAGES["ab_in"] = (7, 2048)
            STAGES["ab_av"] = (1, 1024)
            STAGES["ukv"] = (1, 2048)
            STAGES["ab_out"] = (4, 2048)
        else:
            STAGES["cd_in"] = (12, 2048)
            STAGES["cd_v"] = (4, 2048)
            STAGES["cd_out"] = (4, 2048)
        STAGES[f"f{l}1a"] = (22, 2048)
        STAGES[f"f{l}1b"] = (16, 1408)


_stages()


class Mark:

    def __init__(self, sem, key, v, loop=None):
        self.sem, self.key, self.v, self.loop = sem, key, v, loop


class Loop:
    def __init__(self, i, per, n):
        self.i, self.per, self.n, self.notes = i, per, n, {}


class Queue:

    def __init__(self, ctl, eng, sem, name):
        self.ctl, self.eng, self.sem, self.name = ctl, eng, sem, name
        self.n = START
        self.met = {}

    def now(self):
        return Mark(self.sem, self.name, self.n, self.ctl.loop)

    def wait(self, m):
        loop = self.ctl.loop
        if m is None or self.ctl.dry:
            return
        if m.loop is None or m.loop is not loop:
            v = m.v if m.loop is None else m.v + (m.loop.n - 1) * m.loop.per[m.key]
            if self.met.get(m.key, -1) >= v:
                return
            if loop is None:
                self.met[m.key] = v
            self.eng.wait_ge(m.sem, v)
        else:
            per = m.loop.per[m.key]
            assert m.v > 0
            if self.met.get((m.key, "loop"), -1) >= m.v:
                return
            self.met[(m.key, "loop")] = m.v
            self.eng.wait_ge(m.sem, loop.i * per + m.v if per else m.v)

    def do(self, make, *after):
        for m in after:
            self.wait(m)
        self.n += 1
        if not self.ctl.dry:
            make().then_inc(self.sem, 1)
        return self.now()

    def quiet(self, make, *after):
        for m in after:
            self.wait(m)
        if not self.ctl.dry:
            make()


class Control:
    def __init__(self, nc):
        self.nc, self.loop, self.dry = nc, None, False
        self.queues, self.straight = [], {}

    def note(self, name, mark):
        (self.straight if self.loop is None else self.loop.notes)[name] = mark

    def last(self, name):
        if self.dry:
            return None
        if self.loop is None:
            return self.straight.get(name)
        if name in self.loop.notes:
            return self.loop.notes[name]
        m = self.loop.before[name]
        return Mark(m.sem, m.key, m.v - self.loop.per[m.key], self.loop)

    def loop_over(self, n, engines, body):
        base = {q.name: q.n for q in self.queues}
        counts = [(c, c.n) for c in self.counters]
        self.dry, self.loop = True, Loop(0, {}, n)
        body(0)
        notes = self.loop.notes
        per = {q.name: q.n - base[q.name] for q in self.queues}
        for c, v in counts:
            per[c.key] = (c.n - v) * c.unit
            c.n = v
        for q in self.queues:
            q.n = base[q.name]
        self.dry = False
        with self.nc.Fori(0, n, engines=engines) as i:
            self.loop = Loop(i, per, n)
            self.loop.before = notes
            for q in self.queues:
                q.met = {k: v for k, v in q.met.items() if not isinstance(k, tuple)}
            body(i)
            self.straight.update(self.loop.notes)
            self.loop = None
        for q in self.queues:
            q.met = {k: v for k, v in q.met.items() if not isinstance(k, tuple)}
            q.n = base[q.name] + n * per[q.name]
        for c, v in counts:
            c.n = v + n * per[c.key] // c.unit


class Load:

    unit = 16

    def __init__(self, ctl, sem, key):
        self.ctl, self.sem, self.key, self.n = ctl, sem, key, 0
        ctl.counters.append(self)

    def start(self, q, dst, src, *after):
        for m in after:
            q.wait(m)
        self.n += 1
        if not self.ctl.dry:
            q.eng.dma_start(dst, src).then_inc(self.sem, 16)
        return Mark(self.sem, self.key, 16 * self.n, self.ctl.loop)


def bc(ap, n):
    return ap.unsqueeze(1).broadcast_to([ap.shape[0], n, ap.shape[1]])


def bc_in(ap, n):
    return ap.unsqueeze(2).broadcast_to([ap.shape[0], ap.shape[1], n])


def fr(ap):
    return ap.bitcast(F32R)


class Arena:

    def __init__(self, tensor, size):
        self.t, self.size, self.at = tensor, size, 0

    def __call__(self, *shape):
        n = int(np.prod(shape))
        ap = self.t[:, self.at:self.at + n]
        self.at += n
        assert self.at <= self.size, (self.at, self.size)
        if len(shape) == 1:
            return ap
        names = "abcde"[:len(shape)]
        return ap.rearrange(f"p ({' '.join(names)}) -> p {' '.join(names)}",
                            **{c: s for c, s in zip(names[1:], shape[1:])})


class Machine:

    def __init__(self, nc, t, es):
        self.nc, self.t, self.es = nc, t, es
        self.ctl = ctl = Control(nc)
        ctl.counters = []
        self.P = Queue(ctl, nc.tensor, self.sem("s_pe"), "P")
        self.V = Queue(ctl, nc.vector, self.sem("s_dve"), "V")
        self.A = Queue(ctl, nc.scalar, self.sem("s_act"), "A")
        self.G = Queue(ctl, nc.gpsimd, self.sem("s_pool"), "G")
        self.S = Queue(ctl, nc.sync, self.sem("s_sp"), "S")
        ctl.queues = [self.P, self.V, self.A, self.G, self.S]
        for q in ctl.queues[:4]:
            q.eng.sem_inc(q.sem, START)
        self.slot_sem = [self.sem(f"s_slot{k}") for k in range(NS)]
        self.s_free = self.sem("s_free")
        self.P.eng.sem_inc(self.s_free, START)
        self.n, self.key, self.unit = 0, "free", 1
        ctl.counters.append(self)
        self.loaded = 0
        self.ring = self.sbuf("ring", NS, SLOT)
        self.H = self.sbuf("H", KT, 2 * T)
        self.cols = self.sbuf("cols", NCOL)
        self.ident = self.sbuf("ident", P)
        self.ones = self.sbuf("ones", P)
        self.blk64 = self.sbuf("blk64", P)
        self.cond = self.sbuf("cond", KT, 2)
        self.row = self.sbuf("row", 512)
        self.mod = self.sbuf("mod", DEPTH2 * 9 * KT * 2)
        self.arena_all, self.scopes = 39200, 0
        self.bank = [es.enter_context(nc.psum_tensor(f"bank{k}", [P, 512], F32)) for k in range(8)]
        self.misc = Load(ctl, self.sem("s_misc"), "misc")
        self.shuffle = Load(ctl, self.sem("s_shuffle"), "shuffle")
        self.sent = Load(ctl, self.sem("s_sent"), "sent")
        self.moved = Load(ctl, self.sem("s_moved"), "moved")

    def scope(self, **boxes):
        es, self.scopes, self.box = ExitStack(), self.scopes + 1, {}
        boxes["arena"] = (self.arena_all - sum(int(np.prod(s)) for s in boxes.values()),)
        for name, shape in boxes.items():
            self.box[name] = es.enter_context(
                self.nc.sbuf_tensor(f"{name}_{self.scopes}", [P, *shape], F32))
        self.arena, self.arena_size = self.box["arena"], boxes["arena"][0]
        return es

    def sem(self, name):
        return self.es.enter_context(self.nc.semaphore(name))

    def sbuf(self, name, *shape):
        return self.es.enter_context(self.nc.sbuf_tensor(name, [P, *shape], F32))

    def col(self, name, k=0):
        return self.cols[:, bass.ds(k + COLS[name], 1)]

    def bounds(self, *queues):
        marks = [q.now() for q in (self.P, self.V, self.A, self.G)] + [self.freed()]
        for q in queues or (self.P, self.V, self.A, self.G, self.S):
            for m in marks:
                if not (q is self.P and m.key in ("P", "free")):
                    q.wait(m)

    def feed(self, names):
        sp = self.nc.sync
        for name in names:
            nch, width = STAGES[name]
            src, b = self.t[name], self.loaded

            def put(j, at, ahead):
                k = (b + j) % NS
                sp.wait_ge(self.s_free, ahead + (START + b + j - NS + 1))
                sp.dma_start(self.ring[:, k, 0:width], src[at, :, :].rearrange("a p n -> (a p) n")
                             if at is not j else src[j, :, :]).then_inc(self.slot_sem[k], 16)

            full = nch // NS if nch >= 2 * NS else 0
            if full:
                with self.nc.Fori(0, full, engines=[ENG.SP]) as i:
                    for j in range(NS):
                        put(j, bass.ds(i * NS + j, 1), i * NS)
            for j in range(full * NS, nch):
                put(j, j, 0)
            self.loaded += nch

    def take(self):
        n, k = self.n, self.n % NS
        loop = self.ctl.loop
        if not self.ctl.dry:
            v = 16 * (n // NS + 1)
            if loop is None:
                self.P.eng.wait_ge(self.slot_sem[k], v)
            else:
                assert loop.per["free"] % NS == 0
                self.P.eng.wait_ge(self.slot_sem[k], loop.i * (16 * loop.per["free"] // NS) + v)
        return self.ring[:, k, :]

    def freed(self):
        return Mark(self.s_free, "free", START + self.n, self.ctl.loop)

    def give(self, make):
        self.n += 1
        if not self.ctl.dry:
            make().then_inc(self.s_free, 1)
        return self.freed()

    def mm(self, out, lhsT, rhs, start, stop):
        return lambda: self.nc.tensor.matmul(out, lhsT, rhs, start=start, stop=stop)

    def product(self, out, w, nk, rhs, tile0=0, last=True, start=True, stop=True):
        m = None
        for k in range(nk):
            make = self.mm(out, w[:, (tile0 + k) * P:(tile0 + k + 1) * P], rhs(k),
                           start and k == 0, stop and k == nk - 1)
            if k < nk - 1:
                self.P.quiet(make)
            elif last:
                m = self.give(make)
            else:
                m = self.P.do(make)
        return m

    def w_buffer(self, n, part):
        return (2 * n + part) % self.box["w_hi"].shape[1]

    def split_part(self, ahead, tiles, part):
        nc, n = self.nc, self.n + ahead
        k, loop, buf = n % NS, self.ctl.loop, self.w_buffer(n, part)
        raw = self.ring[:, k, part * tiles[0] * P:(part * tiles[0] + tiles[part]) * P]
        hi, lo = (self.box[x][:, buf, 0:tiles[part] * P] for x in ("w_hi", "w_lo"))
        if part == 0 and not self.ctl.dry:
            v = 16 * (n // NS + 1)
            self.A.eng.wait_ge(self.slot_sem[k],
                               v if loop is None else loop.i * (16 * loop.per["free"] // NS) + v)
        m = self.A.do(lambda: nc.scalar.copy(fr(hi), raw), self.ctl.last(f"used{buf}"))
        m = self.V.do(lambda: nc.vector.tensor_tensor(fr(lo), raw, hi, SUB), m)
        self.ctl.note(f"split{buf}", m)
        return m

    def product_split(self, out, part, nk, rhs, start=True, stop=True):
        buf = self.w_buffer(self.n, part)
        self.P.wait(self.ctl.last(f"split{buf}"))
        for k in range(nk):
            at = slice(k * P, (k + 1) * P)
            wh, wl = (fr(self.box[n][:, buf, at]) for n in ("w_hi", "w_lo"))
            xh, xl = (fr(x) for x in rhs(k))
            for n, (a, b) in enumerate(((wh, xh), (wh, xl), (wl, xh))):
                end = k == nk - 1 and n == 2
                make = self.mm(out, a, b, start and k == 0 and n == 0, stop and end)
                if not end:
                    self.P.quiet(make)
        m = self.give(make) if part else self.P.do(make)
        self.ctl.note(f"used{buf}", m)
        return m

    def colsum(self, out, src, nk, mat=None, after=()):
        for m in after:
            self.P.wait(m)
        mat = self.ones if mat is None else mat
        for k in range(nk):
            make = self.mm(out, mat[:, :], src(k), k == 0, k == nk - 1)
            m = self.P.do(make) if k == nk - 1 else self.P.quiet(make)
        return m

    def rstd(self, out, var, scale, eps, after):
        m = self.V.do(lambda: self.nc.vector.tensor_scalar(out, var, scale, eps, MUL, ADD), after)
        m = self.A.do(lambda: self.nc.scalar.activation(out, out, ACT.Sqrt), m)
        return self.V.do(lambda: self.nc.vector.reciprocal(out, out), m)

    def layer_norm(self, R, l, dst, tmp, after):
        P_, V, A, nc = self.P, self.V, self.A, self.nc
        dev, sq, rs = tmp(KT, T), tmp(KT, T), tmp(T)
        mean, var = self.bank[0][:, 0:T], self.bank[1][:, 0:T]
        m = self.colsum(mean, lambda k: R[:, k, :], KT, after=[after])
        m = V.do(lambda: nc.vector.scalar_tensor_tensor(dev[:, :, :], bc(mean, KT), -1.0 / D, R, MUL, ADD), m)
        s = A.do(lambda: nc.scalar.activation(sq[:, :, :], dev[:, :, :], ACT.Square), m)
        m = self.colsum(var, lambda k: sq[:, k, :], KT, after=[s])
        m = self.rstd(rs, var, 1.0 / D, LN_EPS, m)
        m = V.do(lambda: nc.vector.tensor_tensor(dev[:, :, :], dev[:, :, :], bc(rs, KT), MUL), m)
        for k in range(KT):
            g, b = self.col("ln_g", 8 * l + k), self.col("ln_b", 8 * l + k)
            V.do(lambda: nc.vector.tensor_scalar(dst[:, k, :], dev[:, k, :], g, b, MUL, ADD), m)

    BOXES = dict(w_hi=(4, SLOT // 2), w_lo=(4, SLOT // 2), x_hi=(KT, T), x_lo=(KT, T),
                 y_hi=(KT, T), y_lo=(KT, T), p_hi=(2, T), p_lo=(2, T))
    EIGHTS = (KT, KT)

    def halves(self, name):
        hi, lo = self.box[name + "_hi"], self.box[name + "_lo"]
        return lambda k: (hi[:, k, :], lo[:, k, :])

    def split_input(self, name, x, n, after):
        hi, lo = self.box[name + "_hi"], self.box[name + "_lo"]
        for k in range(0, n, 4):
            at = slice(k, min(k + 4, n))
            m = self.A.do(lambda: self.nc.scalar.copy(fr(hi[:, at, :]), x[:, at, :]), after)
            m = self.V.do(lambda: self.nc.vector.tensor_tensor(fr(lo[:, at, :]), x[:, at, :],
                                                               hi[:, at, :], SUB), m)
        return m

    def tail(self, l, order=None, ahead=False):
        P_, V, A, nc, X = self.P, self.V, self.A, self.nc, self.H
        tmp = Arena(self.arena, self.arena_size)
        R, R2, sig, pT = tmp(KT, T), tmp(KT, T), tmp(2, T), tmp(2, T)
        r_hi, r_lo = self.box["x_hi"], self.box["x_lo"]
        got = self.misc.start(self.G, pT[:, :, :], self.t["p"][l])
        gates = (KT, 2)
        if not ahead:
            for part in range(2):
                self.split_part(0, self.EIGHTS, part)
        P_.wait(self.split_input("y", X[:, :, T:2 * T], KT, V.now()))
        A.wait(got)
        P_.wait(self.split_input("p", pT, 2, None))
        y_at, r_at, p_at = (self.halves(n) for n in "yxp")
        free = [None] * 8
        for m in range(8):
            e = m % 2
            y = self.bank[m][:, 0:T]
            self.split_part(1, self.EIGHTS if m < 6 else gates, e)
            done = self.product_split(y, e, KT, y_at)
            x, r = X[:, m, 0:T], R[:, m, :]
            if order == "sc":
                y = y.rearrange("p (s c) -> p c s", s=SL)
                x, r = (a.rearrange("p (c s) -> p c s", s=SL) for a in (x, r))
            f = V.do(lambda: nc.vector.scalar_tensor_tensor(r, x, ALPHA, y, MUL, ADD), done)
            free[m] = f
            f = V.do(lambda: nc.vector.tensor_copy(fr(r_hi[:, m, :]), R[:, m, :]), f)
            rdy = V.do(lambda: nc.vector.tensor_tensor(fr(r_lo[:, m, :]), R[:, m, :], r_hi[:, m, :], SUB), f)
        P_.wait(rdy)
        for m in range(KT):
            bg, bp, e = m % 4, 4 + m % 4, m % 2
            gate, proj = self.bank[bg][:, 0:T], self.bank[bp][:, 0:T]
            P_.wait(free[bg])
            P_.wait(free[bp])
            for part in range(2 if m < KT - 1 else 0):
                self.split_part(1, gates, part)
            self.product_split(gate, 0, KT, r_at)
            done = self.product_split(proj, 1, 2, p_at)
            s = A.do(lambda: nc.scalar.activation(sig[:, e, :], gate, ACT.Sigmoid), done, free[bp])
            v = V.do(lambda: nc.vector.tensor_tensor(sig[:, e, :], sig[:, e, :], proj, MUL), s)
            free[bg] = free[bp] = v
            V.do(lambda: nc.vector.tensor_tensor(R2[:, m, :], R[:, m, :], sig[:, e, :], ADD), v)
            if e == 1:
                A.wait(V.now())
        self.bounds(P_)
        self.layer_norm(R2, l, X[:, :, 0:T], tmp, V.now())
        self.bounds()

    def conv_layer(self, l):
        P_, V, A, nc, X, ctl = self.P, self.V, self.A, self.nc, self.H, self.ctl
        tmp = Arena(self.arena, self.arena_size)
        U = [tmp(T + 2) for _ in range(2)]
        hs, sz, cv = ([tmp(T) for _ in range(2)] for _ in range(3))
        for e in range(2):
            V.do(lambda: nc.vector.memset(U[e][:, 0:2], 0.0))
        V.wait(V.now())
        kofs, up = 24 * (l // 3), self.EIGHTS
        x_at = self.halves("x")
        P_.wait(self.split_input("x", X[:, :, 0:T], KT, None))
        for part in range(2):
            P_.wait(self.split_part(0, up, part))

        def pair(i):
            for e in range(2):
                b = self.bank[4 * e:4 * e + 4]
                u = U[e]
                P_.wait(ctl.last(f"free{e}"))
                self.split_part(1, up, 0)
                self.product_split(b[0][:, 0:T], 0, KT, x_at)
                self.split_part(1, up, 1)
                hm = self.product_split(b[1][:, 0:T], 1, KT, x_at)
                self.split_part(1, up, 0)
                A.wait(ctl.last(f"free{e}"))
                a = A.do(lambda: nc.scalar.copy(hs[e], b[1][:, 0:T]), hm)
                V.do(lambda: nc.vector.tensor_tensor(u[:, 2:T + 2], b[0][:, 0:T], hs[e], MUL), a)
                taps = [self.col("conv_k", i * 2 + (kofs + 8 * tap + e)) for tap in range(3)]
                V.do(lambda: nc.vector.tensor_scalar(cv[e], u[:, 0:T], taps[0], None, MUL), V.now())
                for tap in (1, 2):
                    V.do(lambda: nc.vector.scalar_tensor_tensor(
                        cv[e], u[:, tap:T + tap], taps[tap], cv[e], MUL, ADD), V.now())
                taps_done = V.now()
                cm = self.product_split(b[2][:, 0:T], 0, KT, x_at)
                self.split_part(1, up, 1)
                zm = self.product_split(b[3][:, 0:T], 1, KT, x_at)
                z = A.do(lambda: nc.scalar.activation(sz[e], b[3][:, 0:T], ACT.Silu), zm)
                V.do(lambda: nc.vector.tensor_tensor(cv[e], cv[e], b[2][:, 0:T], MUL), taps_done, cm)
                y = X[:, bass.ds(i * 2 + e, 1), T:2 * T].rearrange("p a t -> p (a t)")
                f = V.do(lambda: nc.vector.tensor_tensor(y, cv[e], sz[e], MUL), V.now(), z)
                ctl.note(f"free{e}", f)

        ctl.loop_over(4, [ENG.PE, ENG.DVE, ENG.Activation], pair)
        self.bounds()
        self.tail(l, ahead=True)

    def ssm_layer(self, l):
        P_, V, A, Gq, nc, X, ctl, t = self.P, self.V, self.A, self.G, self.nc, self.H, self.ctl, self.t
        v_, bank = nc.vector, self.bank
        tmp = Arena(self.arena, self.arena_size)
        UF, UP, ZZ = tmp(KT, SL, SC), tmp(G, SC), tmp(SC, 2, G)
        TT, CA = tmp(G, P), tmp(G, SL + 1, GH)
        Zs = X[:, :, T:2 * T]
        AB, ABT = tmp(16, SL, GH), tmp(16, P)
        t2 = tmp(16 * (SL + 1) * GH)
        B1, B2, C1, C2 = (tmp(G, GH) for _ in range(4))
        small = tmp(10 * G)
        lre, lim, ldt, th, er, ar, ai, w1, w2, w3 = (small[:, G * k:G * k + G] for k in range(10))
        PWr, PWi = tmp(SL + 1, G), tmp(SL + 1, G)
        A8r, A8i = tmp(2, G), tmp(2, G)
        q1, q2 = (small[:, 128 * k:128 * k + 128].rearrange("p (r g) -> p r g", g=G) for k in range(2))
        b1, b2 = t2[:, 0:1024], t2[:, 1024:2048]
        for dst, name in ((lre, "s_lre"), (lim, "s_lim"), (ldt, "s_ldt")):
            self.misc.start(Gq, dst[:, :], t[name][:, :])
        for dst, name in ((b1, "s_b1"), (b2, "s_b2"), (C1, "s_c1"), (C2, "s_c2")):
            flat = dst if name in ("s_b1", "s_b2") else dst.rearrange("p g h -> p (g h)")
            got = self.misc.start(Gq, flat, t[name][:, :])
        b1, b2 = (b.rearrange("p (g h) -> p g h", g=G) for b in (b1, b2))

        free = [None] * 8
        for c in range(8):
            w = self.take()
            for e in range(2):
                m = 2 * c + e
                b = m % 8
                P_.wait(free[b])
                o = bank[b][:, 0:T]
                done = self.product(o, w, KT, lambda k: X[:, k, 0:T], e * KT, e == 1)
                o = o.rearrange("p (c s) -> p s c", s=SL)
                if m < 8:
                    free[b] = V.do(lambda: v_.tensor_copy(UF[:, m, :, :], o), done)
                else:
                    z = Zs[:, m - 8, :].rearrange("p (s c) -> p s c", s=SL)
                    free[b] = A.do(lambda: nc.scalar.activation(z, o, ACT.Silu), done)
            if c == 3:
                u_ready = V.now()
        c = self.cols[:, COLS["c"]:COLS["c"] + 2 * KT].rearrange("p (k n) -> p k n", n=2)
        P_.wait(A.do(lambda: nc.scalar.activation(self.cond[:, :, :], c, ACT.Silu)))
        for b in (6, 7):
            P_.wait(free[b])
        sc1, sc2 = t["scratch_u"], t["scratch_y"]
        wrote = self.shuffle.start(Gq, sc1.rearrange("(p n) -> p n", p=P),
                                   UF.rearrange("p m s c -> p (m s c)"), u_ready)
        Gq.wait(wrote)
        for s in range(SL):
            src = bass.AP(tensor=sc1.tensor, offset=s * SC,
                          ap=[[KT * T, GH], [T, KT], [GH * KT * T, 8], [1, SC]])
            u_in = self.shuffle.start(Gq, UP[s * GH:(s + 1) * GH, :, :]
                                      .rearrange("h (m g) c -> h m g c", g=8), src)

        V.wait(got)
        A.wait(got)
        dt = w1
        d = A.do(lambda: nc.scalar.activation(dt, ldt, ACT.Exp))
        V.do(lambda: v_.tensor_tensor(er, lre, dt, MUL), d)
        V.do(lambda: v_.tensor_tensor(th, lim, dt, MUL))
        d = V.now()
        A.do(lambda: nc.scalar.activation(er, er, ACT.Exp), d)
        V.do(lambda: v_.tensor_scalar(w2, th, 1 / (2 * np.pi), 12582912.0, MUL, ADD), V.now())
        V.do(lambda: v_.tensor_scalar(w2, w2, -12582912.0, None, ADD), V.now())
        for part in (6.28125, 1.9340515136718750e-3, 1.2556659418 * 1e-6):
            V.do(lambda: v_.scalar_tensor_tensor(th, w2, -part, th, MUL, ADD), V.now())
        V.do(lambda: v_.tensor_scalar(th, th, 3.1415925, -3.1415925, MIN, MAX), V.now())
        V.do(lambda: v_.scalar_tensor_tensor(w2, th, -1.0, th, MUL, MAX), V.now())
        V.do(lambda: v_.tensor_scalar(w2, w2, -1.0, np.pi / 2, MUL, ADD), V.now())
        A.do(lambda: nc.scalar.activation(w2, w2, ACT.Sin), V.now())
        A.do(lambda: nc.scalar.activation(th, th, ACT.Sin))
        V.do(lambda: v_.tensor_tensor(ar, er, w2, MUL), A.now())
        V.do(lambda: v_.tensor_tensor(ai, er, th, MUL))
        fr, fi, n = w1, w2, w3
        V.do(lambda: v_.tensor_tensor(fr, lre, lre, MUL))
        V.do(lambda: v_.tensor_tensor(fi, lim, lim, MUL), V.now())
        V.do(lambda: v_.tensor_tensor(th, fr, fi, ADD), V.now())
        V.do(lambda: v_.reciprocal(th, th), V.now())
        V.do(lambda: v_.tensor_scalar(n, ar, -1.0, None, ADD))

        def cross(out, x, y, z, w, op):
            V.do(lambda: v_.tensor_tensor(er, z, w, MUL), V.now())
            V.do(lambda: v_.tensor_tensor(out, x, y, MUL))
            V.do(lambda: v_.tensor_tensor(out, out, er, op), V.now())

        cross(fr, n, lre, ai, lim, ADD)
        cross(fi, ai, lre, n, lim, SUB)
        V.do(lambda: v_.tensor_tensor(fr, fr, th, MUL), V.now())
        V.do(lambda: v_.tensor_tensor(fi, fi, th, MUL), V.now())
        sgn = self.col("sgn")
        V.do(lambda: v_.tensor_scalar(fi, fi, sgn, None, MUL), V.now())
        V.do(lambda: v_.tensor_tensor(B1[:, :, :], b1, bc_in(fr, GH), MUL), V.now())
        V.do(lambda: v_.tensor_tensor(B2[:, :, :], b2, bc_in(fi, GH), MUL))
        V.do(lambda: v_.tensor_tensor(B1[:, :, :], B1[:, :, :], B2[:, :, :], ADD), V.now())
        V.do(lambda: v_.tensor_tensor(B2[:, :, :], b2, bc_in(fr, GH), MUL), V.now())
        V.do(lambda: v_.tensor_tensor(b1, b1, bc_in(fi, GH), MUL))
        V.do(lambda: v_.tensor_tensor(B2[:, :, :], B2[:, :, :], b1, SUB), V.now())
        V.do(lambda: v_.tensor_scalar(C1[:, :, :], C1[:, :, :], sgn, -1.0, MUL, MUL))
        V.do(lambda: v_.tensor_scalar(C2[:, :, :], C2[:, :, :], -1.0, None, MUL))
        V.do(lambda: v_.memset(PWr[:, 0, :], 1.0))
        V.do(lambda: v_.memset(PWi[:, 0, :], 0.0))
        V.do(lambda: v_.tensor_copy(PWr[:, 1, :], ar))
        V.do(lambda: v_.tensor_copy(PWi[:, 1, :], ai))
        p1 = t2[:, 0:4 * G].rearrange("p (a g) -> p a g", g=G)
        for k in (1, 2, 4):
            lr, li = PWr[:, 1:1 + k, :], PWi[:, 1:1 + k, :]
            hr, hi = bc(PWr[:, k, :], k), bc(PWi[:, k, :], k)
            orr, oi, s = PWr[:, 1 + k:1 + 2 * k, :], PWi[:, 1 + k:1 + 2 * k, :], p1[:, 0:k, :]
            for out, x, y, op in ((orr, hr, hi, SUB), (oi, hi, hr, ADD)):
                V.do(lambda: v_.tensor_tensor(s, li, y, MUL), V.now())
                V.do(lambda: v_.tensor_tensor(out, lr, x, MUL))
                V.do(lambda: v_.tensor_tensor(out, out, s, op), V.now())
        for h in range(2):
            V.do(lambda: v_.tensor_copy(A8r[:, h, :], PWr[:, SL, :]), V.now())
            V.do(lambda: v_.tensor_scalar(A8i[:, h, :], PWi[:, SL, :], sgn, 1.0 - 2 * h, MUL, MUL))
        RPr, RPi = tmp(SL, G), tmp(SL, G)
        US = small[:, 0:16 * SC].rearrange("p (g c) -> p g c", g=16)
        for s in range(SL):
            V.do(lambda: v_.tensor_copy(RPr[:, s, :], PWr[:, SL - 1 - s, :]))
            V.do(lambda: v_.tensor_scalar(RPi[:, s, :], PWi[:, SL - 1 - s, :], sgn, None, MUL))
        self.ada_at = 0
        self.ada_products(32, 0)
        V.do(lambda: v_.memset(TT[:, :, :], 0.0))
        V.do(lambda: v_.memset(ZZ[:, 0, :, :], 0.0))
        P_.wait(u_in)
        V.wait(u_in)
        self.bounds()

        KS = ABT

        def block(i):
            V.wait(ctl.last("pe"))
            Gq.wait(ctl.last("pe"))
            g16 = bass.ds(i * 16, 16)
            back = lambda pw: pw[:, :, g16].rearrange("p s g -> p g s").unsqueeze(3).broadcast_to(
                [P, 16, SL, GH])
            over = lambda b, n: b[:, g16, :].unsqueeze(2).broadcast_to([P, 16, n, GH])
            s2 = t2[:, 0:16 * SL * GH].rearrange("p (g s h) -> p g s h", g=16, s=SL)
            Gq.wait(V.now())
            y = Gq.do(lambda: nc.gpsimd.tensor_tensor(s2, back(RPi), over(B2, SL), MUL))
            V.do(lambda: v_.tensor_tensor(AB, back(RPr), over(B1, SL), MUL))
            ab = V.do(lambda: v_.tensor_tensor(AB, AB, s2, ADD), y, V.now())
            us = V.do(lambda: v_.tensor_copy(US[:, :, :], UP[:, g16, :]))
            P_.wait(ctl.last("k_read"))
            self.ada_at, ada = 0, lambda n: self.ada_products(n, i * 2 + 4, (6, 2))
            ada(8)
            P_.wait(ctl.last("row_read1"))
            P_.wait(us)
            for g in range(16):
                tr = P_.do(lambda: nc.tensor.transpose(
                    bank[g // 4][:, P * (g % 4):P * (g % 4 + 1)],
                    AB[:, g, :, :].rearrange("p s h -> p (s h)"), self.ident[:, :]), ab)
            for b in range(4):
                copy = lambda: nc.scalar.copy(ABT[:, 4 * b:4 * b + 4, :].rearrange("p g n -> p (g n)"),
                                              bank[b][:, :])
                abt = A.do(copy, tr)
            for g in range(16):
                u = US[:, g, :]
                o0, o1 = bank[0][:, 32 * g:32 * g + 32], bank[1][:, 32 * g:32 * g + 32]
                P_.quiet(self.mm(o0, ABT[:, g, :], u, True, True), abt)
                P_.quiet(self.mm(o1[0:64, :], ABT[:, g, 64:128], u, True, True))
                vm = P_.do(self.mm(o1[64:128, :], ABT[:, g, 0:64], u, True, True))
            for h in range(2):
                zo = ZZ[:, 1:SC, h, g16]
                vr = V.do(lambda: v_.tensor_copy(
                    zo, bank[h][:, :].rearrange("p (g c) -> p c g", g=16)[:, 0:SC - 1, :]), vm)
            ada(8)
            P_.wait(ctl.last("row_read0"))
            n = SL + 1
            s9 = t2[:, 0:16 * n * GH].rearrange("p (g s h) -> p g s h", g=16, s=n)
            pw = lambda p: p[:, :, g16].rearrange("p s g -> p g s").unsqueeze(3).broadcast_to(
                [P, 16, n, GH])
            y = Gq.do(lambda: nc.gpsimd.tensor_tensor(s9, pw(PWi), over(C2, n), MUL), ab)
            c = CA[:, g16, :, :]
            V.do(lambda: v_.tensor_tensor(c, pw(PWr), over(C1, n), MUL))
            bs = AB[:, 0:2, :, :].rearrange("p a s h -> p (a s) h")
            V.do(lambda: v_.tensor_copy(bs, B1[:, g16, :]), tr)
            ca = V.do(lambda: v_.tensor_tensor(c, c, s9, ADD), y, V.now())
            for g in range(16):
                rhs = CA[:, bass.ds(i * 16 + g, 1), 0:SL, :].rearrange("p a s h -> p (a s h)")
                km = P_.do(self.mm(bank[4 + g // 4][0:GH, P * (g % 4):P * (g % 4 + 1)],
                                   bs[:, g, :], rhs, True, True), ca)
            for b in range(4):
                copy = lambda: nc.scalar.copy(KS[0:GH, 4 * b:4 * b + 4, :]
                                              .rearrange("p g n -> p (g n)"), bank[4 + b][0:GH, :])
                ks = A.do(copy, km, vr)
            ctl.note("k_read", ks)
            ctl.note("pe", km)
            for s in range(SL):
                toe = self.moved.start(
                    A, TT[s * GH:(s + 1) * GH, g16, s * GH:P], KS[0:GH, :, 0:(SL - s) * GH], ks)
            A.wait(toe)
            P_.wait(toe)

        ctl.loop_over(4, [ENG.PE, ENG.DVE, ENG.Activation, ENG.Pool], block)
        self.bounds(P_, V)

        def steps(i):
            for h in range(2):
                old, new = (ZZ[:, bass.ds(i * 2 + (1 + h + e), 1), :, :].rearrange("p a r g -> p (a r) g")
                            for e in range(2))
                V.do(lambda: v_.tensor_tensor(q1[:, :, :], old, A8r[:, :, :], MUL), V.now())
                for r in range(2):
                    V.do(lambda: v_.tensor_tensor(q2[:, r, :], old[:, 1 - r, :], A8i[:, r, :], MUL))
                V.do(lambda: v_.tensor_tensor(q1[:, :, :], q1[:, :, :], q2[:, :, :], ADD), V.now())
                V.do(lambda: v_.tensor_tensor(new, new, q1[:, :, :], ADD), V.now())

        ctl.loop_over((SC - 2) // 2, [ENG.DVE], steps)

        def meanwhile(i):
            self.ada_at = 0
            self.ada_products(16, i * 2 + 12)

        ctl.loop_over(4, [ENG.PE, ENG.Activation, ENG.Pool], meanwhile)
        P_.wait(V.now())
        YP = AB.rearrange("p g s h -> p (g s h)").rearrange("p (g c) -> p g c", g=G)
        for g in range(G):
            o = bank[g // 16][:, 32 * (g % 16):32 * (g % 16) + 32]
            P_.quiet(self.mm(o, TT[:, g, :], UP[:, g, :], True, False))
            ym = P_.do(self.mm(o, CA[:, g, 1:SL + 1, :].rearrange("p s h -> p (s h)"),
                               ZZ[:, 0:SC, 0, g], False, True))
            if g % 16 == 15:
                b = g // 16
                cp = A.do(lambda: nc.scalar.copy(YP[:, 16 * b:16 * b + 16, :]
                                                 .rearrange("p g c -> p (g c)"), bank[b][:, :]), ym)
        wrote = self.moved.start(A, sc2.rearrange("(p n) -> p n", p=P),
                                   YP.rearrange("p g c -> p (g c)"), cp)
        A.wait(wrote)
        YF = ABT.rearrange("p g n -> p (g n)").rearrange("p (m s c) -> p m s c", m=KT, s=SL)
        for s in range(SL):
            src = bass.AP(tensor=sc2.tensor, offset=s * GH * KT * T,
                          ap=[[SC, 8], [KT * T, GH], [T, KT], [1, SC]])
            back = self.moved.start(A, YF[:, :, s, :], src)
        yf = YF.rearrange("p m s c -> p m (s c)")
        uf = UF.rearrange("p m s c -> p m (s c)")
        V.wait(back)
        for k in range(KT):
            V.do(lambda: v_.scalar_tensor_tensor(yf[:, k, :], uf[:, k, :], self.col("ssm_d", k),
                                                 yf[:, k, :], MUL, ADD))
        ge = A.do(lambda: nc.scalar.activation(yf, yf, ACT.Gelu_apprx_tanh), V.now())
        P_.wait(ge)
        for c in range(4):
            w = self.take()
            for e in range(2):
                m = 2 * c + e
                o = bank[m][:, 0:T]
                done = self.product(o, w, KT, lambda k: yf[:, k, :], e * KT, e == 1)
                sg = uf[:, m, :]
                a = A.do(lambda: nc.scalar.activation(sg, o, ACT.Sigmoid, bias=self.col("b_glu", m)), done)
                V.do(lambda: v_.tensor_tensor(sg, sg, yf[:, m, :], MUL), a)
                V.do(lambda: v_.tensor_tensor(Zs[:, m, :], sg, Zs[:, m, :], MUL), V.now())
        self.bounds()

    def rwkv_layer(self, l):
        P_, V, A, Gq, nc, X, ctl, t = self.P, self.V, self.A, self.G, self.nc, self.H, self.ctl, self.t
        v_, s_, bank, tt = nc.vector, nc.scalar, self.bank, nc.vector.tensor_tensor
        keep = Arena(self.arena, self.arena_size)
        RKVZ, LD, AA, Y = keep(4, KT, T), keep(KT, T), keep(KT, T), X[:, :, T:2 * T]
        masks = keep(1280)
        tmp = Arena(self.arena, self.arena_size)
        tmp.at = keep.at
        dx, XS = tmp(KT, T), tmp(6, KT, T)
        gm = self.misc.start(Gq, masks, t["r_masks"][:, :])
        x = X[:, :, 0:T]
        V.do(lambda: tt(dx[:, :, 1:T], x[:, :, 0:T - 1], x[:, :, 1:T], SUB))
        V.do(lambda: v_.tensor_scalar(dx[:, :, 0:1], x[:, :, 0:1], -1.0, None, MUL))
        V.wait(V.now())
        mixed = []
        for n in range(6):
            for k in range(KT):
                V.do(lambda: v_.scalar_tensor_tensor(XS[:, n, k, :], dx[:, k, :],
                                                     self.col("mu", 8 * n + k), x[:, k, :], MUL, ADD))
            mixed.append(V.now())
        w = self.take()
        lw, la = bank[0][0:64, 0:T], bank[1][64:128, 0:T]
        hw, ha = tmp(T), tmp(T)
        P_.wait(mixed[5])
        for k in range(KT):
            P_.quiet(self.mm(lw, w[:, 64 * k:64 * k + 64], XS[:, 4, k, :], k == 0, k == KT - 1))
        for k in range(KT):
            mk = self.mm(la, w[:, 512 + 64 * k:576 + 64 * k], XS[:, 5, k, :], k == 0, k == KT - 1)
            m = P_.do(mk) if k == KT - 1 else P_.quiet(mk)
        A.do(lambda: s_.activation(hw[0:64, :], lw, ACT.Tanh), m)
        m = A.do(lambda: s_.copy(ha[64:128, :], la))
        P_.wait(m)
        for k in range(KT):
            for e, (h, dst, bias) in enumerate(((hw, LD, "w0"), (ha, AA, "a0"))):
                b, r = bank[(2 * k + e) % 8], slice(64 * e, 64 * e + 64)
                if k >= 4:
                    P_.wait(freed[2 * k + e - 8])
                mk = self.mm(b[:, 0:T], w[r, 1024 + P * k:1024 + P * (k + 1)], h[r, :], True, True)
                m = self.give(mk) if (k, e) == (KT - 1, 1) else P_.do(mk)
                m = A.do(lambda: s_.activation(dst[:, k, :], b[:, 0:T], ACT.Sigmoid,
                                               bias=self.col(bias, k)), m)
                freed = [m] if (k, e) == (0, 0) else freed + [m]
        V.do(lambda: v_.tensor_scalar(LD[:, :, :], LD[:, :, :], -float(np.exp(-0.5)), None, MUL), m)
        self.bounds(P_, A)

        def project(n):
            for c in range(4):
                w = self.take()
                for e in range(2):
                    m = 2 * c + e
                    P_.wait(ctl.last(f"b{m}"))
                    o = bank[m][:, 0:T]
                    done = self.product(
                        o, w, KT, lambda k: XS[:, bass.ds(n, 1), k, :].rearrange("p a t -> p (a t)"),
                        e * KT, e == 1)
                    dst = RKVZ[:, bass.ds(n, 1), m, :].rearrange("p a t -> p (a t)")
                    if e:
                        f = A.do(lambda: s_.copy(dst, o), done)
                    else:
                        f = V.do(lambda: v_.tensor_copy(dst, o), done)
                    ctl.note(f"b{m}", f)

        ctl.loop_over(4, [ENG.PE, ENG.DVE, ENG.Activation], project)
        for q in (P_, V, A, Gq):
            q.wait(gm)
        self.bounds()

        tmp = Arena(self.arena, self.arena_size)
        tmp.at = keep.at
        kk, kp, cu, wi, wv, wx, bt, kt, sq, O, OS, bo = (tmp(2, T) for _ in range(12))
        AR = tmp(2, 2, 2, P)
        NQ, AQ = tmp(8, 2 * P), tmp(8, 2 * P)
        NN, XX, XT, MM, YY = (tmp(8, P) for _ in range(5))
        tok = tmp(4, 4, P)
        Vz = tmp(2, 4, P)
        Gs, XG, XA, SAz, SA = tmp(8, 64), tmp(8, 64), tmp(4, P), tmp(2, 2 * P), tmp(2, 2 * P)
        ST = tmp(2, P)
        mask2 = masks[:, 0:256]
        mN, m0, m0T = (masks[:, 256 + P * k:384 + P * k] for k in range(3))
        level = [masks[:, 640 + P * k:768 + P * k] for k in range(5)]
        Z0 = V.do(lambda: v_.memset(SAz[:, :, :], 0.0))
        V.wait(Z0)

        def heads(i):
            two = bass.ds(i * 2, 2)
            self.ada_at, ada = 0, lambda n: self.ada_products(n, i * 4 + ADA_SSM)
            r, k, v, z = (RKVZ[:, n, two, :] for n in range(4))
            a, ld = AA[:, two, :], LD[:, two, :]
            flat = lambda ap: ap.rearrange("p j t -> p (j t)")
            V.do(lambda: v_.memset(ST[:, :, :], 0.0), ctl.last("end_p"))
            for j in range(2):
                kj = RKVZ[:, 1, bass.ds(i * 2 + j, 1), :].rearrange("p a t -> p (a t)")
                aj = AA[:, bass.ds(i * 2 + j, 1), :].rearrange("p a t -> p (a t)")
                V.do(lambda: v_.tensor_scalar(kk[:, j, :], kj, self.col("k_k", i * 2 + j), None, MUL),
                     ctl.last("end_p"), ctl.last("end_a"), ctl.last("end_g"))
                V.do(lambda: v_.tensor_scalar(kp[:, j, :], aj, -1.0, self.col("k_a", i * 2 + j), ADD, MUL))
            s = A.do(lambda: s_.activation(sq[:, :, :], kk[:, :, :], ACT.Square), V.now(), ctl.last("end_v"))
            V.do(lambda: v_.scalar_tensor_tensor(kp[:, :, :], kp[:, :, :], 1.0, k, ADD, MUL), V.now())
            m = P_.do(self.mm(bank[7][:, :], self.blk64[:, :], flat(sq), True, True), s, ctl.last("end_v"))
            m = A.do(lambda: s_.activation(flat(sq), bank[7][:, :], ACT.Sqrt), m)
            ada(8)
            P_.wait(m)
            ada(8)
            V.do(lambda: v_.tensor_copy(cu[:, :, :], ld))
            for lv in range(6):
                h = 1 << lv
                c = flat(cu).rearrange("p (b two h) -> p b two h", two=2, h=h)
                carry = c[:, :, 0, h - 1:h].broadcast_to([P, 2 * T // (2 * h), h])
                V.do(lambda: tt(c[:, :, 1, :], c[:, :, 1, :], carry, ADD), V.now())
            e1 = A.do(lambda: s_.activation(wi[:, :, :], cu[:, :, :], ACT.Exp), V.now())
            e2 = A.do(lambda: s_.activation(wv[:, :, :], cu[:, :, :], ACT.Exp, scale=-1.0))
            V.do(lambda: tt(wx[:, :, :], cu[:, :, :], ld, SUB), V.now())
            e3 = A.do(lambda: s_.activation(wx[:, :, :], wx[:, :, :], ACT.Exp), V.now())
            V.do(lambda: v_.tensor_scalar(sq[:, :, :], sq[:, :, :], 1e-12, None, MAX), m)
            V.do(lambda: v_.reciprocal(sq[:, :, :], sq[:, :, :]), V.now())
            V.do(lambda: tt(kk[:, :, :], kk[:, :, :], sq[:, :, :], MUL), V.now())
            ar = lambda which: AR[:, :, :, which, :].rearrange("p j b t -> p (j b) t")
            at4 = lambda ap: ap.rearrange("p j (b t) -> p (j b) t", t=P)
            V.do(lambda: tt(kt[:, :, :], kp[:, :, :], wv[:, :, :], MUL), e2)
            V.do(lambda: tt(ar(1), at4(r), at4(wi), MUL), e1)
            V.do(lambda: tt(bt[:, :, :], kk[:, :, :], a, MUL), V.now())
            V.do(lambda: v_.scalar_tensor_tensor(ar(0), at4(kk), -1.0, at4(wx), MUL, MUL), e3)
            pre = V.do(lambda: tt(bt[:, :, :], bt[:, :, :], wv[:, :, :], MUL), V.now())
            for j in range(2):
                if j:
                    P_.wait(masked)
                for e in range(2):
                    rows = slice(64 * e, 64 * e + 64)
                    for tb in range(2):
                        tk = slice(P * tb, P * tb + P)
                        both = AR[rows, j, tb, :, :].rearrange("p w t -> p (w t)")
                        half = slice(256 * tb, 256 * tb + 256)
                        P_.quiet(self.mm(bank[2 * e][:, half], bt[rows, j, tk], both, True, True), pre)
                        P_.quiet(self.mm(bank[2 * e + 1][:, half], kt[rows, j, tk], both, True, True))
                        m = P_.do(self.mm(bank[4 + e][:, tk], AR[rows, j, tb, 0, :], bt[rows, j, tk],
                                          True, True))
                for e in range(2):
                    u = slice(4 * j + 2 * e, 4 * j + 2 * e + 2)
                    q = lambda b: b[:, :].rearrange("p (b t) -> p b t", b=2)
                    V.do(lambda: tt(NQ[:, u, :], q(bank[2 * e]), bc(mask2, 2), MUL), m)
                    V.do(lambda: tt(AQ[:, u, :], q(bank[2 * e + 1]), bc(mask2, 2), MUL))
                    masked = V.do(lambda: tt(NN[:, u, :], bank[4 + e][:, 0:256]
                                             .rearrange("p (b t) -> p b t", b=2), bc(mN, 2), MUL))
            P_.wait(masked)
            for n in range(4):
                for jb in range(4):
                    j, tk = jb // 2, slice(P * (jb % 2), P * (jb % 2) + P)
                    if n == 0:
                        src = RKVZ[:, 2, bass.ds(i * 2 + j, 1), tk].rearrange("p a t -> p (a t)")
                        src = self.stage_v(src, O[:, j, tk])
                    else:
                        src = (bt[:, j, tk], kt[:, j, tk], AR[:, j, jb % 2, 0, :])[n - 1]
                    m = P_.do(lambda: nc.tensor.transpose(bank[n][:, P * jb:P * jb + P], src,
                                                          self.ident[:, :]))
            for n in range(4):
                cp = A.do(lambda: s_.copy(tok[:, n, :, :].rearrange("p a b -> p (a b)"), bank[n][:, :]), m)
            P_.wait(cp)
            NT = NQ[:, :, 0:P]
            V.do(lambda: tt(XX[:, :, :], NN[:, :, :], bc(m0, 8), MUL), V.now())
            V.do(lambda: tt(XT[:, :, :], NT, bc(m0T, 8), MUL))
            V.do(lambda: tt(XX[:, :, :], XX[:, :, :], bc(self.ident[:, :], 8), ADD), V.now())
            xx = V.do(lambda: tt(XT[:, :, :], XT[:, :, :], bc(self.ident[:, :], 8), ADD))
            p1 = None
            for lv in range(5):
                mm_ = Gq.do(lambda: nc.gpsimd.tensor_tensor(MM[:, :, :], NT, bc(level[lv], 8), MUL),
                            masked, p1)
                P_.wait(mm_)
                P_.wait(xx)
                for u in range(8):
                    p1 = P_.do(self.mm(bank[4 + u // 4][:, P * (u % 4):P * (u % 4) + P], MM[:, u, :],
                                       XX[:, u, :], True, True))
                ada(2 if lv < 4 else 0)
                for b in range(2):
                    y = A.do(lambda: s_.copy(YY[:, 4 * b:4 * b + 4, :].rearrange("p u t -> p (u t)"),
                                             bank[4 + b][:, :]), p1)
                P_.wait(y)
                for u in range(8):
                    c = slice(P * (u % 4), P * (u % 4) + P)
                    m = P_.do(self.mm(bank[u // 4][:, c], YY[:, u, :], XT[:, u, :], True, True))
                if lv < 4:
                    for u in range(8):
                        c = slice(P * (u % 4), P * (u % 4) + P)
                        m = P_.do(self.mm(bank[2 + u // 4][:, c], XT[:, u, :], YY[:, u, :], True, True))
                ada(2 if lv < 4 else 0)
                for b in range(2):
                    u4 = slice(4 * b, 4 * b + 4)
                    q = lambda bk: bk[:, :].rearrange("p (u t) -> p u t", u=4)
                    xx = V.do(lambda: tt(XT[:, u4, :], XT[:, u4, :], q(bank[b]), ADD), m)
                    if lv < 4:
                        xx = V.do(lambda: tt(XX[:, u4, :], XX[:, u4, :], q(bank[2 + b]), ADD))
            unit = lambda u: (u // 4, (u // 2) % 2, u % 2)
            for u in range(8):
                j, e, tb = unit(u)
                m = P_.do(self.mm(bank[4][:, 64 * u:64 * u + 64], AQ[:, u, 0:P],
                                  tok[:, 0, 2 * j + tb, 64 * e:64 * e + 64], True, True))
            g = A.do(lambda: s_.copy(Gs.rearrange("p u v -> p (u v)"), bank[4][:, :]), m)
            for h in range(2):
                vz = A.do(lambda: s_.activation(Vz[:, h, :, :], tok[:, 0, :, :], ACT.Copy,
                                                scale=self.col("half", h)), cp)
            P_.wait(xx)
            for u in range(8):
                j, e, tb = unit(u)
                P_.quiet(self.mm(bank[6][64 * e:64 * e + 64, P * (2 * j + tb):P * (2 * j + tb) + P],
                                 tok[:, 3, 2 * j + tb, 64 * e:64 * e + 64], XT[:, u, :], True, True))
            P_.wait(g)
            for u in range(8):
                m = P_.do(self.mm(bank[5][:, 64 * u:64 * u + 64], XT[:, u, :], Gs[:, u, :], True, True))
            xa = A.do(lambda: s_.copy(XA.rearrange("p u t -> p (u t)"), bank[6][:, :]), m)
            V.do(lambda: v_.tensor_copy(XG.rearrange("p u v -> p (u v)"), bank[5][:, :]), m)
            P_.wait(xa)
            P_.wait(vz)
            for b in range(2):
                P_.wait(ctl.last(f"row_read{b}"))
            xgb = XG.rearrange("p (je tb) v -> p tb je v", tb=2)
            st, os_, copied = V.now(), None, [None, None]
            for c in range(4):
                tb, h = c // 2, c % 2
                rows, bk = slice(64 * h, 64 * h + 64), bank[4 + (c % 2)]
                saz = SAz[rows, h, :].rearrange("p (je v) -> p je v", je=4)
                xg = xgb[rows, tb, :, :]
                P_.wait(st)
                if c:
                    for j in range(2):
                        m = P_.do(self.mm(bk[rows, P * j:P * j + P], XA[:, 2 * j + tb, rows], ST[:, j, :],
                                          True, True))
                    sa = V.do(lambda: tt(saz, xg, bk[rows, 0:2 * P].rearrange("p (je v) -> p je v", je=4),
                                         ADD), m, copied[h])
                    P_.wait(os_)
                    for j in range(2):
                        m = P_.do(self.mm(bank[7][:, P * j + 0:P * j + 64], ST[:, j, :],
                                          AR[:, j, tb, 1, rows], True, True))
                    os_ = A.do(lambda: s_.copy(
                        OS[:, :, 64 * c:64 * c + 64],
                        bank[7][:, 0:2 * P].rearrange("p (j t) -> p j t", j=2)[:, :, 0:64]), m)
                else:
                    sa = V.do(lambda: v_.tensor_copy(saz, xg), V.now(), ctl.last("end_p"))
                    V.do(lambda: v_.memset(OS[:, :, 0:64], 0.0))
                both = copied[h] = A.do(lambda: s_.copy(SA[rows, tb, :], SAz[rows, h, :]), sa)
                if c < 3:
                    P_.wait(sa)
                    for j in range(2):
                        o = bank[6][:, P * j:P * j + P]
                        P_.quiet(self.mm(o, self.ident[:, :], ST[:, j, :], True, False))
                        P_.quiet(self.mm(o, tok[:, 1, 2 * j + tb, :], SAz[:, h, P * j:P * j + P],
                                         False, False))
                        m = P_.do(self.mm(o, tok[:, 2, 2 * j + tb, :], Vz[:, h, 2 * j + tb, :],
                                          False, True))
                    for j in range(2):
                        for e in range(2):
                            rw = slice(64 * e, 64 * e + 64)
                            st = V.do(lambda: v_.tensor_scalar(
                                ST[rw, j, 64 * e:64 * e + 64], bank[6][rw, P * j + 64 * e:P * j + 64 * e + 64],
                                wi[rw, j, 64 * c + 63:64 * c + 64], None, MUL), m)
            P_.wait(both)
            for u in range(8):
                j, e, tb = unit(u)
                o = bank[u // 4][64 * e:64 * e + 64, P * (2 * (u // 4 - u // 4) + tb):P * tb + P]
                P_.quiet(self.mm(o, SA[:, tb, P * j + 64 * e:P * j + 64 * e + 64], NQ[:, u, P:2 * P],
                                 True, False))
                m = P_.do(self.mm(o, tok[:, 0, 2 * j + tb, 64 * e:64 * e + 64], AQ[:, u, P:2 * P],
                                  False, True))
            for j in range(2):
                V.do(lambda: tt(O[:, j, :], OS[:, j, :], bank[j][:, 0:T], ADD), m, os_)
            m = P_.do(self.mm(bank[4][:, :], self.blk64[:, :], flat(O), True, True), V.now())
            V.do(lambda: tt(bo[:, :, :], r, kp[:, :, :], MUL))
            for j in range(2):
                V.do(lambda: v_.tensor_scalar(bo[:, j, :], bo[:, j, :], self.col("r_k", i * 2 + j), None, MUL),
                     V.now())
            mb = P_.do(self.mm(bank[5][:, :], self.blk64[:, :], flat(bo), True, True), V.now())
            V.do(lambda: v_.scalar_tensor_tensor(flat(O), bank[4][:, :], -1.0 / 64, flat(O), MUL, ADD), m)
            s = A.do(lambda: s_.activation(sq[:, :, :], O[:, :, :], ACT.Square), V.now())
            m = P_.do(self.mm(bank[6][:, :], self.blk64[:, :], flat(sq), True, True), s)
            rs = flat(wx)
            self.rstd(rs, bank[6][:, :], 1.0 / 64, GN_EPS, m)
            V.do(lambda: tt(flat(O), flat(O), rs, MUL), V.now())
            for j in range(2):
                V.do(lambda: v_.tensor_scalar(O[:, j, :], O[:, j, :], self.col("lnx_g", i * 2 + j),
                                              self.col("lnx_b", i * 2 + j), MUL, ADD), V.now())
            V.do(lambda: tt(bo[:, :, :], v, bank[5][:, :].rearrange("p (j t) -> p j t", j=2), MUL), mb)
            V.do(lambda: tt(O[:, :, :], O[:, :, :], bo[:, :, :], ADD), V.now())
            sz = A.do(lambda: s_.activation(OS[:, :, :], z, ACT.Silu), V.now())
            f = V.do(lambda: tt(Y[:, two, :], O[:, :, :], OS[:, :, :], MUL), sz)
            ctl.note("end_v", f)
            ctl.note("end_a", A.now())
            ctl.note("end_p", P_.now())
            ctl.note("end_g", Gq.now())

        ctl.loop_over(4, [ENG.PE, ENG.DVE, ENG.Activation, ENG.Pool], heads)
        self.bounds()

    def stage_v(self, src, dst):
        m = self.V.do(lambda: self.nc.vector.tensor_copy(dst, src))
        self.P.wait(m)
        return dst


    def ada_products(self, count, group, banks=(6, 7)):
        P_, ctl = self.P, self.ctl
        for u in range(self.ada_at, self.ada_at + count):
            g, k, b = u // 8, u % 8, u // 8 % 2
            out, row = self.bank[banks[b]][0:2, :], self.row[0:2, :]
            if k % 4 == 0:
                self.ada_w = self.take()
            if k == 0:
                P_.wait(ctl.last(f"row_read{b}"))
            make = self.mm(out, self.cond[:, k, :], self.ada_w[:, 512 * (k % 4):512 * (k % 4) + 512],
                           k == 0, k == 7)
            m = self.give(make) if k % 4 == 3 else P_.quiet(make)
            if k == 7:
                m = self.A.do(lambda: self.nc.scalar.copy(row, out), m, ctl.last("row_sent"))
                ctl.note(f"row_read{b}", m)
                ctl.note("row_sent", self.sent.start(
                    self.G, self.t["mods"][:, bass.ds((group + g) * 512, 512)], row, m))
        self.ada_at += count

    def ada(self):
        P_, V, A, G_, nc, ctl = self.P, self.V, self.A, self.G, self.nc, self.ctl
        v_ = nc.vector
        tmp = Arena(self.arena, self.arena_size)
        tiles = DEPTH2 * 9 * KT
        most, rest = tmp(2, P), tmp(2, P)
        self.misc.start(G_, self.H[:, :, T:2 * T], self.t["ctx"])
        G_.wait(ctl.last("row_sent"))
        mods = self.t["mods"]
        for n in range(2):
            self.misc.start(G_, most[:, n, :], mods[n, 0:P * P].rearrange("(m f) -> m f", f=P))
            got = self.misc.start(G_, rest[0:tiles - P, n, :],
                                  mods[n, P * P:tiles * P].rearrange("(m f) -> m f", f=P))
        for q in (V, P_, A):
            q.wait(got)
        m = self.mod[:, :].rearrange("p (m n) -> p n m", n=2)
        for b, (src, at, rows) in enumerate(((most, 0, P), (rest, P, tiles - P))):
            for n in range(2):
                tr = P_.do(lambda: nc.tensor.transpose(self.bank[b][:, rows * n:rows * n + rows],
                                                       src[0:rows, n, :], self.ident[0:rows, 0:rows]))
            bias = bc(self.cols[:, COLS["ada_b"] + at:COLS["ada_b"] + at + rows], 2)
            V.do(lambda: v_.tensor_tensor(m[:, :, at:at + rows], self.bank[b][:, 0:2 * rows].rearrange(
                "p (n m) -> p n m", n=2), bias, ADD), tr)
        m5 = self.mod[:, :].rearrange("p (l w k n) -> p l w k n", l=DEPTH2, w=9, k=KT)
        V.wait(V.now())
        for l in range(DEPTH2):
            for s in range(3):
                at = COLS["norm_g"] + KT * (3 * l + s)
                g = bc_in(self.cols[:, at:at + KT], 2)
                sl = m5[:, l, 3 * s + 1, :, :]
                V.do(lambda: v_.scalar_tensor_tensor(sl, sl, 1.0, g, ADD, MUL))
                if s != 1:
                    gt = m5[:, l, 3 * s + 2, :, :]
                    V.do(lambda: v_.tensor_scalar(gt, gt, 0.5, None, MUL))
        self.bounds()

    def mod_col(self, l, which, k, n):
        return self.mod[:, bass.ds((k * 2) + ((l * 9 + which) * KT * 2 + n), 1)]

    def modulated(self, l, s, dst, sq, nt):
        V, A, nc, H = self.V, self.A, self.nc, self.H
        m = A.do(lambda: nc.scalar.activation(sq[:, :, 0:nt], H[:, :, 0:nt], ACT.Square))
        m = self.colsum(self.bank[0][:, 0:nt], lambda k: sq[:, k, 0:nt], KT, after=[m])
        rs = sq[:, 0, 0:nt]
        m = self.rstd(rs, self.bank[0][:, 0:nt], 1.0 / D, RMS_EPS, m)
        V.do(lambda: nc.vector.tensor_tensor(dst[:, :, 0:nt], H[:, :, 0:nt], bc(rs, KT), MUL), m)
        V.wait(V.now())
        for k in range(KT):
            for n in range(nt // T):
                d = dst[:, k, n * T:n * T + T]
                m = V.do(lambda: nc.vector.tensor_scalar(
                    d, d, self.mod_col(l, 3 * s + 1, k, n), self.mod_col(l, 3 * s, k, n), MUL, ADD))
        self.P.wait(m)

    def gated_sum(self, o, l, which, m, nt, done):
        for n in range(nt // T):
            h = self.H[:, bass.ds(m, 1), n * T:n * T + T].rearrange("p a t -> p (a t)")
            f = self.V.do(lambda: self.nc.vector.scalar_tensor_tensor(
                h, o[:, n * T:n * T + T], self.mod_col(l, which, m, n), h, MUL, ADD), done)
        return f

    def rest_of(self, x_hi, x_lo, y, shift, k, half, hi):
        return self.V.do(lambda: self.nc.vector.scalar_tensor_tensor(
            fr(x_lo[:, k, half]), y, shift, x_hi[:, k, half], ADD, SUB), hi)

    def ffn(self, l, s):
        P_, V, A, nc, ctl = self.P, self.V, self.A, self.nc, self.ctl
        nt = T if (l, s) == (DEPTH2 - 1, 1) else 2 * T
        x_hi, x_lo, u_hi, u_lo = (self.box[n] for n in ("x_hi", "x_lo", "u_hi", "u_lo"))
        tmp = Arena(self.arena, self.arena_size)
        rs, ut, act = tmp(nt), tmp(2, 2 * T), tmp(4, 2 * T)
        up, dn = (KT, KT), ((FT // 2 + 1) // 2, FT // 2 // 2)
        H = self.H
        first = self.split_part(0, up, 0)
        free = [None] * 4
        for k in range(KT):
            sq, h = act[:, k % 4, 0:nt], H[:, k, 0:nt]
            m = V.do(lambda: nc.vector.tensor_tensor(sq, h, h, MUL), free[k % 4]) if k % 2 else \
                A.do(lambda: nc.scalar.activation(sq, h, ACT.Square), free[k % 4])
            m = free[k % 4] = P_.do(self.mm(self.bank[0][:, 0:nt], self.ones[:, :], sq,
                                            k == 0, k == KT - 1), m)
        m = self.rstd(rs, self.bank[0][:, 0:nt], 1.0 / D, RMS_EPS, m)
        V.wait(m)
        lo, read = [None] * 4, {}
        for k in range(KT):
            for n in range(nt // T):
                half, y = slice(n * T, n * T + T), act[:, k % 4, n * T:n * T + T]
                scale, shift = (self.mod_col(l, 6 * s + w, k, n) for w in (1, 0))
                m = V.do(lambda: nc.vector.scalar_tensor_tensor(y, H[:, k, half], scale, rs[:, half],
                                                                MUL, MUL), read.get((k - 4, n)))
                hi = A.do(lambda: nc.scalar.activation(fr(x_hi[:, k, half]), y, ACT.Identity, bias=shift), m)
                lo = lo[1:] + [(y, shift, k, half, hi)]
                if lo[0]:
                    read[lo[0][2], lo[0][3].start // T] = self.rest_of(x_hi, x_lo, *lo[0])
        for part in lo[1:]:
            self.rest_of(x_hi, x_lo, *part)
        lo = [None, V.now()]
        P_.wait(lo[1])
        V.wait(A.now())
        A.wait(V.now())
        halves = lambda hi, lo, k: (hi[:, k, 0:nt], lo[:, k, 0:nt])

        def pair(m, j):
            P_.wait(ctl.last(f"u{j}"))
            a, b = self.bank[2 * j][:, 0:nt], self.bank[2 * j + 1][:, 0:nt]
            self.split_part(0, up, 1)
            self.product_split(a, 0, KT, lambda k: halves(x_hi, x_lo, k))
            am = P_.now()
            self.split_part(1, up if m is not last else dn, 0)
            done = self.product_split(b, 1, KT, lambda k: halves(x_hi, x_lo, k))
            g = A.do(lambda: nc.scalar.activation(act[:, j, 0:nt], a, ACT.Silu), am, ctl.last(f"u{j}"))
            u, e = ut[:, j % 2, 0:nt], j % 2
            uh, ul = (y[:, bass.ds(m, 1), 0:nt].rearrange("p a t -> p (a t)") for y in (u_hi, u_lo))
            f = V.do(lambda: nc.vector.tensor_tensor(u, act[:, j, 0:nt], b, MUL), g, done)
            ctl.note(f"u{j}", f)
            f = V.do(lambda: nc.vector.tensor_copy(fr(uh), u), f)
            return V.do(lambda: nc.vector.tensor_tensor(fr(ul), u, uh, SUB), f)

        full, last = FT // NS, None
        P_.wait(first)
        ctl.loop_over(full, [ENG.PE, ENG.DVE, ENG.Activation],
                      lambda i: [pair(i * NS + j, j) for j in range(NS)])
        for j in range(FT % NS):
            tile = full * NS + j
            last = tile if tile == FT - 1 else None
            m = pair(tile, j)
        P_.wait(m)
        A.wait(self.freed())

        def down(i, end=False):
            for j in range(2):
                P_.wait(ctl.last(f"d{j}"))
                o = self.bank[j][:, 0:nt]
                for c in range(2):
                    u = lambda k: halves(u_hi, u_lo, c * (FT // 2) + k)
                    self.split_part(0, dn, 1)
                    self.product_split(o, 0, dn[0], u, c == 0, False)
                    if not (end and j == c == 1):
                        self.split_part(1, dn, 0)
                    done = self.product_split(o, 1, dn[1], lambda k: u(dn[0] + k), False, c == 1)
                ctl.note(f"d{j}", self.gated_sum(o, l, 6 * s + 2, i * 2 + j, nt, done))

        ctl.loop_over(KT // 2 - 1, [ENG.PE, ENG.DVE, ENG.Activation], down)
        P_.wait(V.now())
        A.wait(self.freed())
        down(KT // 2 - 1, True)
        self.bounds()

    def softmax_units(self, units, scale, sc, on_pair):
        P_, V, A, nc = self.P, self.V, self.A, self.nc
        v_, s_ = nc.vector, nc.scalar
        ctl = self.ctl
        pr, pt, st, sb = sc

        def scores(n):
            qs, ks, nk, _, _, bias, _ = units[n]
            d = n % 2
            b = self.bank[d]
            P_.wait(ctl.last(f"s{d}"))
            for c, (q, k) in enumerate(zip(qs, ks)):
                mk = self.mm(b[:, 0:nk], q, k, c == 0, c == len(qs) - 1)
                m = P_.do(mk) if c == len(qs) - 1 else P_.quiet(mk)
            mx, ng, sm, rc = (st[:, d, k:k + 1] for k in range(4))
            src, sscale = b[:, 0:nk], scale
            V.wait(ctl.last(f"p{d}"))
            if bias is not None:
                V.do(lambda: v_.scalar_tensor_tensor(sb[:, d, 0:T], b[:, 0:T], scale, bias, MUL, ADD), m)
                V.do(lambda: v_.tensor_scalar(sb[:, d, T:nk], b[:, T:nk], scale, None, MUL))
                ctl.note(f"s{d}", V.now())
                src, sscale = sb[:, d, 0:nk], 1.0
            V.do(lambda: v_.reduce_max(mx, src, AX), m, V.now() if bias is not None else None)
            m = V.do(lambda: v_.tensor_scalar(ng, mx, -sscale, None, MUL), V.now())
            A.wait(ctl.last(f"t{d}"))
            m = A.do(lambda: s_.activation(pr[:, d, 0:nk], src, ACT.Exp, bias=ng, scale=sscale,
                                           accum_out=sm), m)
            if bias is None:
                ctl.note(f"s{d}", m)
            return m

        def probabilities(n, m):
            nk, d = units[n][2], n % 2
            sm, rc = st[:, d, 2:3], st[:, d, 3:4]
            V.do(lambda: v_.reciprocal(rc, sm), m)
            m = V.do(lambda: v_.tensor_scalar(pr[:, d, 0:nk], pr[:, d, 0:nk], rc, None, MUL), V.now())
            tb = self.bank[2 + d]
            P_.wait(ctl.last(f"e{d}"))
            P_.wait(m)
            for k in range(nk // P):
                m = P_.do(lambda: nc.tensor.transpose(tb[:, P * k:P * k + P], pr[:, d, P * k:P * k + P],
                                                      self.ident[:, :]))
            ctl.note(f"t{d}", m)
            ctl.note(f"p{d}", m)
            A.wait(ctl.last(f"o{d}"))
            m = A.do(lambda: s_.copy(pt[:, d, 0:nk], tb[:, 0:nk]), m)
            ctl.note(f"e{d}", m)
            return m

        def values(n, m):
            _, _, nk, vs, out, _, close = units[n]
            d, nb = n % 2, nk // P
            P_.wait(m)
            if close == "first":
                P_.wait(ctl.last("pair"))
            for k in range(nb):
                m = P_.do(self.mm(out, vs[k], pt[:, d, P * k:P * k + P], k == 0, k == nb - 1))
            ctl.note(f"o{d}", m)
            if close == "last":
                on_pair(n, m)

        done = {}
        for n in range(len(units) + 2):
            if n < len(units):
                done[n] = scores(n)
            if 0 <= n - 2:
                values(n - 2, done[n - 2])
            if 0 <= n - 1 < len(units):
                done[n - 1] = probabilities(n - 1, done[n - 1])

    def headnorm(self, tile, sums, gain, div, nt, tmp, rope=None, dst=None, squares=None):
        P_, V, A, nc, ctl = self.P, self.V, self.A, self.nc, self.ctl
        v_ = nc.vector
        n = self.hn = (self.hn + 1) % 2
        bank, rs, rot = self.bank[4 + n], tmp[n][:, 0:nt], tmp[n][:, 0:T]
        dst = tile if dst is None else dst
        P_.wait(ctl.last(f"hn{n}"))
        for k, (mat, sqr) in enumerate(sums):
            mk = self.mm(bank[:, 0:nt], mat, sqr, k == 0, k == len(sums) - 1)
            m = P_.do(mk, squares) if k == len(sums) - 1 else P_.quiet(mk, squares)
        V.wait(V.now())
        m = self.rstd(rs, bank[:, 0:nt], 1.0 / div, RMS_EPS, m)
        m = V.do(lambda: v_.scalar_tensor_tensor(dst, tile, gain, rs, MUL, MUL), m)
        if rope:
            mat, cos, sin = rope
            m = P_.do(self.mm(bank[:, 0:T], mat, dst[:, 0:T], True, True), m)
            V.do(lambda: v_.tensor_tensor(rot, bank[:, 0:T], sin, MUL), m)
            V.do(lambda: v_.tensor_tensor(dst[:, 0:T], dst[:, 0:T], cos, MUL))
            m = V.do(lambda: v_.tensor_tensor(dst[:, 0:T], dst[:, 0:T], rot, ADD), V.now())
        ctl.note(f"hn{n}", m)
        return m

    def mixer_ab(self):
        P_, V, A, nc, ctl, t = self.P, self.V, self.A, self.nc, self.ctl, self.t
        v_, s_ = nc.vector, nc.scalar
        N = 2 * T
        self.hn = 0
        tmp = Arena(self.arena, self.arena_size)
        hm, sq = tmp(KT, N), tmp(KT, N)
        AQ, AK, BQN, BQR, KV, KR = (tmp(n, N) for n in (4, 1, 4, 2, 2, 1))
        BKN, BKR = tmp(4, N), tmp(2, N)
        AV, BV = tmp(4, P), tmp(4, 512)
        con = tmp(128 * 7 + 4 * T)
        nt2 = [tmp(N) for _ in range(2)]
        got = self.misc.start(self.G, con, t["ab_consts"][:, :])
        blk32, E0, E1, F0, F1, RA, RB = (con[:, P * k:P * k + P] for k in range(7))
        cosA, sinA, cosB, sinB = (con[:, 896 + T * k:896 + T * k + T] for k in range(4))
        self.modulated(0, 1, hm, sq, N)
        tiles_ = [AQ[:, k, :] for k in range(4)] + [AK[:, 0, :]] + [BQN[:, k, :] for k in range(4)] + \
            [BQR[:, k, :] for k in range(2)] + [KV[:, k, :] for k in range(2)] + [KR[:, 0, :]]
        free = [None] * 8
        for c in range(7):
            w = self.take()
            for e in range(2):
                m = 2 * c + e
                b = m % 8
                P_.wait(free[b])
                done = self.product(self.bank[b][:, :], w, KT, lambda k: hm[:, k, :], e * KT, e == 1)
                q = V if e else A
                cp = (lambda: v_.tensor_copy(tiles_[m], self.bank[b][:, :])) if e else \
                    (lambda: s_.copy(tiles_[m], self.bank[b][:, :]))
                free[b] = q.do(cp, done)
        w = self.take()
        P_.wait(free[6])
        for tb in range(4):
            for k in range(KT):
                mk = self.mm(self.bank[6][:, P * tb:P * tb + P], hm[:, k, P * tb:P * tb + P],
                             w[:, P * k:P * k + P], k == 0, k == KT - 1)
                if (tb, k) == (3, KT - 1):
                    m = self.give(mk)
                else:
                    P_.quiet(mk)
        A.do(lambda: s_.copy(AV.rearrange("p a b -> p (a b)"), self.bank[6][:, :]), m)
        for q in (V, P_, A):
            q.wait(got)
        self.bounds()
        A.do(lambda: s_.activation(sq[:, 0:2, :], KV[:, :, :], ACT.Square))
        m = A.do(lambda: s_.activation(sq[:, 2, :], KR[:, 0, :], ACT.Square))
        both = [(self.ones[:, :], sq[:, k, :]) for k in range(2)]
        for k in range(2):
            m2 = self.headnorm(KV[:, k, :], both, self.col("kvn", k), 256, N, nt2, squares=m)
        w = self.take()
        P_.wait(m2)
        for k in range(4):
            b = self.bank[k]
            for c in range(2):
                mk = self.mm(b[:, :], w[:, P * (2 * k + c):P * (2 * k + c + 1)], KV[:, c, :],
                             c == 0, c == 1)
                m3 = P_.do(mk) if c else P_.quiet(mk)
            A.do(lambda: s_.copy(BKN[:, k, :], b[:, :]), m3)
        P_.wait(A.now())
        for tb in range(4):
            for c in range(2):
                mk = self.mm(self.bank[tb][:, :], KV[:, c, P * tb:P * tb + P],
                             w[:, 1024 + 512 * c:1536 + 512 * c], c == 0, c == 1)
                if (tb, c) == (3, 1):
                    m3 = self.give(mk)
                else:
                    m3 = P_.do(mk) if c else P_.quiet(mk)
            V.do(lambda: v_.tensor_copy(BV[:, tb, :], self.bank[tb][:, :]), m3)
        blk64 = self.blk64[:, :]
        m = A.do(lambda: s_.activation(sq[:, 3:7, :], BKN[:, :, :], ACT.Square), A.now())
        rb = (RB, cosB, sinB)
        for k in range(4):
            self.headnorm(BKN[:, k, :], [(blk64, sq[:, 3 + k, :]), ((E0, E1)[k % 2], sq[:, 2, :])],
                          self.col("bkn"), 96, N, nt2, squares=m)
        for k in range(2):
            self.headnorm(KR[:, 0, :], [(blk32, sq[:, 2, :]), (F0, sq[:, 3 + 2 * k, :]),
                                        (F1, sq[:, 4 + 2 * k, :])],
                          self.col("bkr"), 96, N, nt2, rope=rb, dst=BKR[:, k, :])
        A.wait(P_.now())
        A.do(lambda: s_.activation(sq[:, 0:4, :], BQN[:, :, :], ACT.Square))
        m = A.do(lambda: s_.activation(sq[:, 4:6, :], BQR[:, :, :], ACT.Square))
        for k in range(4):
            self.headnorm(BQN[:, k, :], [(blk64, sq[:, k, :]), ((E0, E1)[k % 2], sq[:, 4 + k // 2, :])],
                          self.col("bqn"), 96, N, nt2, squares=m)
        for k in range(2):
            self.headnorm(BQR[:, k, :], [(blk32, sq[:, 4 + k, :]), (F0, sq[:, 2 * k, :]),
                                         (F1, sq[:, 2 * k + 1, :])],
                          self.col("bqr"), 96, N, nt2, rope=rb)
        A.wait(P_.now())
        A.do(lambda: s_.activation(sq[:, 0:4, :], AQ[:, :, :], ACT.Square))
        m = A.do(lambda: s_.activation(sq[:, 4, :], AK[:, 0, :], ACT.Square))
        ra = (RA, cosA, sinA)
        for k in range(4):
            self.headnorm(AQ[:, k, :], [(blk64, sq[:, k, :])], self.col("aqn"), 64, N, nt2, rope=ra,
                          squares=m)
        self.headnorm(AK[:, 0, :], [(blk64, sq[:, 4, :])], self.col("akn"), 64, N, nt2, rope=ra)
        self.bounds()

        wk = Arena(self.arena, self.arena_size)
        att = wk(KT, N)
        qm, kn, kr, vb = wk(2, 2, N), wk(N), wk(N), wk(4, P)
        sc = (tmp(2, N), tmp(2, N), tmp(2, 4), None)
        assert wk.at <= 2 * KT * N

        def streams(e, q, k, v, bank):
            for qb in range(4):
                k0, tb0 = (0, 0) if qb < 2 else (T, 2)
                yield (tuple(a[:, P * qb:P * qb + P] for a in q), tuple(a[:, k0:N] for a in k), N - k0,
                       [v[:, tb, 64 * e:64 * e + 64] for tb in range(tb0, 4)],
                       bank[64 * e:64 * e + 64, P * qb:P * qb + P], None,
                       {(0, 0): "first", (1, 3): "last"}.get((e, qb)))

        def heads(i, first, Q, rope):
            for q in (V, A):
                q.wait(ctl.last("pair_p"))
            qt = Q[:, bass.ds(i, 1), :].rearrange("p a t -> p (a t)")
            for e in range(2):
                V.do(lambda: v_.tensor_scalar(qm[:, 0, e, :], qt, self.col("half", e), None, MUL))
            if rope is not None:
                r, p = rope
                qr = BQR[:, bass.ds(r, 1), :].rearrange("p a t -> p (a t)")
                for e in range(2):
                    V.do(lambda: v_.tensor_scalar(qm[:, 1, e, :], qr, self.col("quart", 2 * p + e),
                                                  None, MUL))
                V.do(lambda: v_.tensor_copy(kn, BKN[:, bass.ds(i, 1), :].rearrange("p a t -> p (a t)")))
                V.do(lambda: v_.tensor_copy(kr, BKR[:, bass.ds(r, 1), :].rearrange("p a t -> p (a t)")))
                V.do(lambda: v_.tensor_copy(vb[:, :, :], BV[:, :, bass.ds(i * P, P)]))
            P_.wait(V.now())
            units = []
            for e in range(2):
                if rope is None:
                    units += streams(e, (qm[:, 0, e, :],), (AK[:, 0, :],), AV, self.bank[6])
                else:
                    units += streams(e, (qm[:, 0, e, :], qm[:, 1, e, :]), (kn, kr), vb, self.bank[6])

            def pair(n, m):
                out = att[:, bass.ds(i + first, 1), :].rearrange("p a t -> p (a t)")
                ctl.note("pair", A.do(lambda: s_.copy(out, self.bank[6][:, :]), m))

            self.softmax_units(units, (64 if rope is None else 96) ** -0.5, sc, pair)
            ctl.note("pair_p", P_.now())

        engines = [ENG.PE, ENG.DVE, ENG.Activation]
        ctl.straight.clear()
        ctl.loop_over(4, engines, lambda i: heads(i, 0, AQ, None))
        self.bounds()
        ctl.loop_over(2, engines, lambda r: [heads(r * 2 + p, 4, BQN, (r, p)) for p in range(2)])
        self.bounds()
        self.mixer_out(0, att, N)

    def mixer_out(self, l, att, nt):
        for c in range(4):
            w = self.take()
            for e in range(2):
                m = 2 * c + e
                o = self.bank[m][:, 0:nt]
                done = self.product(o, w, KT, lambda k: att[:, k, 0:nt], e * KT, e == 1)
                self.gated_sum(o, l, 5, m, nt, done)
        self.bounds()


    def mixer_cd(self):
        P_, V, A, Gq, nc, ctl, t = self.P, self.V, self.A, self.G, self.nc, self.ctl, self.t
        v_, s_, tt, bank = nc.vector, nc.scalar, nc.vector.tensor_tensor, self.bank
        N = 2 * T
        self.hn = 0
        tmp = Arena(self.arena, self.arena_size)
        DQ, DK, IV, DV = tmp(4, T), tmp(4, N), tmp(4, 512), tmp(4, 512)
        Q, GT, ZF, ZB = tmp(4, T), tmp(4, T), tmp(4, N), tmp(4, N)
        att = tmp(KT, T)
        base = tmp.at
        hm, sq = tmp(KT, N), tmp(KT, N)
        self.modulated(1, 1, hm, sq, N)
        places = [(ZF[:, k, :], N) for k in range(4)] + [(ZB[:, k, :], N) for k in range(4)] + \
            [(DK[:, k, :], N) for k in range(4)] + [(Q[:, k, :], T) for k in range(4)] + \
            [(GT[:, k, :], T) for k in range(4)] + [(DQ[:, k, :], T) for k in range(4)]
        free = [None] * 8
        for c in range(12):
            w = self.take()
            for e in range(2):
                m = 2 * c + e
                b, (dst, n) = m % 8, places[m]
                P_.wait(free[b])
                done = self.product(bank[b][:, 0:n], w, KT, lambda k: hm[:, k, 0:n], e * KT, e == 1)
                if 12 <= m < 20:
                    free[b] = A.do(lambda: s_.activation(dst, bank[b][:, 0:n], ACT.Silu), done)
                else:
                    free[b] = V.do(lambda: v_.tensor_copy(dst, bank[b][:, 0:n]), done)
        for f in free:
            P_.wait(f)
        for n, dst in enumerate((IV, DV)):
            for h in range(2):
                w = self.take()
                for tb in range(4):
                    for k in range(4):
                        mk = self.mm(bank[4 * n + tb][:, :], hm[:, 4 * h + k, P * tb:P * tb + P],
                                     w[:, 512 * k:512 * k + 512], h + k == 0, h == 1 and k == 3)
                        if (tb, k) == (3, 3):
                            m = self.give(mk)
                        else:
                            P_.quiet(mk)
            for tb in range(4):
                A.do(lambda: s_.copy(dst[:, tb, :], bank[4 * n + tb][:, :]), m)
        self.bounds()

        wk = Arena(self.arena, self.arena_size)
        wk.at = base
        masks = wk(16, P)
        got = self.misc.start(Gq, masks.rearrange("p a b -> p (a b)"), t["h_masks"][:, :])
        for q in (V, P_, A):
            q.wait(got)
        KY, PS, SS = wk(4, N), wk(4, N), wk(4, N)
        M, Mq = wk(4, T), wk(4, T)
        AT = wk(16, P)
        khT = wk(3, 4, P)
        ST, lbt, zero = wk(4, P), wk(8), wk(512)
        flat = lambda ap: ap.rearrange("p a b -> p (a b)")
        V.do(lambda: v_.memset(zero, 0.0))
        d = self.cols[:, COLS["lb1"]:COLS["lb1"] + 8]
        d0 = self.cols[:, COLS["lb0"]:COLS["lb0"] + 8]
        lb, ol = wk(8), wk(8)
        V.do(lambda: tt(lbt, d, d0, SUB))
        A.do(lambda: s_.activation(lb, lbt, ACT.Sigmoid), V.now())
        m = A.do(lambda: s_.activation(ol, lbt, ACT.Sigmoid, scale=-1.0))
        V.wait(m)
        P_.wait(V.now())
        OB = [bank[6], bank[7]]
        for b in OB:
            P_.quiet(lambda: nc.tensor.matmul(b[:, :], zero[:, 0:P], zero, start=True, stop=False,
                                              skip_group_check=True))
        outp = lambda i, e, tb: OB[i // 2][64 * e:64 * e + 64, T * (i % 2) + P * tb:T * (i % 2) + P * tb + P]

        def add(out, lhsT, rhs):
            return lambda: nc.tensor.matmul(out, lhsT, rhs, start=False, stop=False,
                                            skip_group_check=True)

        for dr, Z in enumerate((ZF, ZB)):
            a1 = A.do(lambda: s_.activation(flat(PS), flat(Z), ACT.Sigmoid), V.now(), P_.now())
            a2 = A.do(lambda: s_.activation(flat(KY), flat(Z), ACT.Sigmoid, scale=-1.0))
            for k in range(4):
                c = 4 * dr + k
                V.do(lambda: v_.tensor_scalar(PS[:, k, :], PS[:, k, :], ol[:, c:c + 1], lb[:, c:c + 1],
                                              MUL, ADD), a1)
            for k in range(4):
                c = 4 * dr + k
                V.do(lambda: v_.tensor_scalar(KY[:, k, :], KY[:, k, :], ol[:, c:c + 1], None, MUL), a2)
            V.do(lambda: v_.tensor_scalar(flat(PS), flat(PS), 1.1e-19, None, MAX), V.now())
            m = A.do(lambda: s_.activation(flat(PS), flat(PS), ACT.Ln), V.now())
            V.do(lambda: v_.memset(flat(SS), 0.0))
            V.wait(m)
            A.wait(V.now())
            tg, so = (1, 0) if dr == 0 else (0, 1)

            def score(units, mask, lhs, rhs, after):
                P_.wait(after)
                for e in range(2):
                    rows = slice(64 * e, 64 * e + 64)
                    for i in range(4):
                        for tb in range(2):
                            u, tk = i * 2 + tb, slice(P * tb, P * tb + P)
                            o = bank[2 * e + u // 4][:, P * (u % 4):P * (u % 4) + P]
                            m = P_.do(self.mm(o, lhs[rows, i, tk], rhs[rows, i, tk], True, True))
                V.wait(m)
                for q in range(4):
                    a = V.do(lambda: tt(AT[:, 4 * q:4 * q + 4, :],
                                        bank[q][:, :].rearrange("p (u t) -> p u t", u=4),
                                        bc(masks[:, mask, :], 4), MUL))
                P_.wait(a)
                for e in range(2):
                    for i in range(4):
                        for tb in range(2):
                            m = P_.do(add(outp(i, e, tb), IV[:, tb, P * i + 64 * e:P * i + 64 * e + 64],
                                          AT[:, 8 * e + 2 * i + tb, :]))
                return m

            used = score(16, 14, KY, Q, V.now())
            for lv in range(7):
                h = 1 << lv
                halves = lambda ap, n: ap.rearrange("p a (b two h) -> p (a b) two h", two=2, h=h) \
                    if n == N else ap[:, :, 0:T].rearrange("p a (b two h) -> p a b two h", two=2, h=h)
                x4 = lambda ap, w: halves(ap, T)[:, :, :, w, :]
                A.wait(used)
                A.do(lambda: s_.activation(x4(M, tg), x4(PS, tg), ACT.Exp), V.now())
                m = A.do(lambda: s_.activation(x4(M, so), x4(SS, so), ACT.Exp))
                V.do(lambda: tt(x4(M, tg), x4(M, tg), x4(Q, tg), MUL), m)
                mq = V.do(lambda: tt(x4(M, so), x4(M, so), x4(KY, so), MUL))
                p, s = halves(PS, N), halves(SS, N)
                last = (h - 1) if dr == 0 else 0
                n = 4 * N // (2 * h)
                tot = lambda w: p[:, :, w, last:last + 1].broadcast_to([P, n, h])
                V.do(lambda: tt(s[:, :, so, :], s[:, :, so, :], tot(tg), ADD))
                V.do(lambda: tt(p[:, :, tg, :], p[:, :, tg, :], tot(so), ADD), V.now())
                used = score(16, lv + 7 * dr, M, M, mq)
            V.wait(V.now())
            m = A.do(lambda: s_.activation(flat(SS), flat(SS), ACT.Exp), V.now())
            a1 = A.do(lambda: s_.activation(M[:, :, :], PS[:, :, 0:T], ACT.Exp), used)
            kh = V.do(lambda: tt(flat(SS), flat(SS), flat(KY), MUL), m)
            qh = V.do(lambda: tt(flat(Mq), flat(M), flat(Q), MUL), a1)
            order = (2, 3, 0, 1) if dr == 0 else (3, 2, 1, 0)
            P_.wait(kh)
            for n, b in enumerate(order[:3]):
                for i in range(4):
                    m = P_.do(lambda: nc.tensor.transpose(bank[n][:, P * i:P * i + P],
                                                          SS[:, i, P * b:P * b + P], self.ident[:, :]))
                A.do(lambda: s_.copy(flat(khT[:, n, :, :]), bank[n][:, :]), m)
            P_.wait(A.now())
            for n, b in enumerate(order[:3]):
                for i in range(4):
                    m = P_.do(self.mm(bank[3 + n][:, P * i:P * i + P], khT[:, n, i, :],
                                      IV[:, b, P * i:P * i + P], True, True))
            V.do(lambda: v_.memset(flat(ST), 0.0), m)
            V.wait(V.now())
            for n, b in enumerate(order):
                end = P * b + (P - 1 if dr == 0 else 0)
                if n >= 1:
                    pb = order[n - 1]
                    pe = P * pb + (P - 1 if dr == 0 else 0)
                    if n == 1:
                        V.do(lambda: v_.memset(zero[:, 0:8], 0.0))
                    for i in range(4):
                        V.do(lambda: v_.tensor_copy(lbt[:, i:i + 1], PS[:, i, pe:pe + 1]), V.now())
                    w = A.do(lambda: s_.activation(lbt[:, 4:8], lbt[:, 0:4], ACT.Exp), V.now())
                    V.wait(P_.now())
                    for e in range(2):
                        rw = slice(64 * e, 64 * e + 64)
                        for i in range(4):
                            sd = ST[rw, i, 64 * e:64 * e + 64]
                            u = bank[2 + n][rw, P * i + 64 * e:P * i + 64 * e + 64]
                            V.do(lambda: v_.scalar_tensor_tensor(sd, sd, lbt[rw, 4 + i:5 + i], u, MUL, ADD), w)
                if n >= 2:
                    P_.wait(V.now())
                    for i in range(4):
                        o = OB[i // 2][:, T * (i % 2) + P * b:T * (i % 2) + P * b + P]
                        m = P_.do(add(o, ST[:, i, :], Mq[:, i, P * b:P * b + P]))
            self.bounds()
        for b in OB:
            m = P_.do(lambda: nc.tensor.matmul(b[:, :], zero[:, 0:P], zero, start=False, stop=True,
                                               skip_group_check=True))
        O = M
        for k in range(2):
            V.do(lambda: v_.tensor_copy(flat(O[:, 2 * k:2 * k + 2, :]), OB[k][:, :]), m)
        m = A.do(lambda: s_.activation(flat(Mq), flat(O), ACT.Square), V.now())
        hn = [AT[:, 4 * k:4 * k + 4, :].rearrange("p a b -> p (a b)") for k in range(2)]
        for k in range(4):
            g = self.headnorm(O[:, k, :], [(self.blk64[:, :], Mq[:, k, :])], self.col("cgn"), 64, T, hn,
                              squares=m)
            V.do(lambda: tt(att[:, k, :], O[:, k, :], GT[:, k, :], MUL), g)
        m = A.do(lambda: s_.activation(flat(Mq), flat(DQ), ACT.Square), P_.now())
        for k in range(4):
            self.headnorm(DQ[:, k, :], [(self.blk64[:, :], Mq[:, k, :])], self.col("dqn"), 64, T, hn,
                          squares=m)
        m = A.do(lambda: s_.activation(flat(KY), flat(DK), ACT.Square))
        for k in range(4):
            self.headnorm(DK[:, k, :], [(self.blk64[:, :], KY[:, k, :])], self.col("dkn"), 64, N, hn,
                          squares=m)
        self.bounds()
        wk = Arena(self.arena, self.arena_size)
        wk.at = base
        bias, nm = wk(8, 2, T), wk(2, T)
        qm, kn, vb, bi = wk(2, T), wk(N), wk(4, P), wk(2, 2, T)
        sc = (wk(2, N), wk(2, N), wk(2, 4), wk(2, N))
        self.misc.start(Gq, bias.rearrange("p a b c -> p (a b c)"), t["d_bias"][:, :], V.now())
        got = self.misc.start(Gq, nm.rearrange("p b c -> p (b c)"), t["d_mask"][:, :])
        V.wait(got)
        V.do(lambda: tt(bias.rearrange("p a b c -> p a (b c)"), bias.rearrange("p a b c -> p a (b c)"),
                        bc(nm.rearrange("p b c -> p (b c)"), 8), ADD))
        V.wait(V.now())

        def heads(i):
            for q in (V, A):
                q.wait(ctl.last("pair_p"))
            V.wait(ctl.last("pair"))
            qt = DQ[:, bass.ds(i, 1), :].rearrange("p a t -> p (a t)")
            for e in range(2):
                V.do(lambda: v_.tensor_scalar(qm[:, e, :], qt, self.col("half", e), None, MUL))
            V.do(lambda: v_.tensor_copy(kn, DK[:, bass.ds(i, 1), :].rearrange("p a t -> p (a t)")))
            V.do(lambda: v_.tensor_copy(vb[:, :, :], DV[:, :, bass.ds(i * P, P)]))
            V.do(lambda: v_.tensor_copy(bi[:, :, :, :], bias[:, bass.ds(i * 2, 2), :, :]))
            P_.wait(V.now())
            V.wait(V.now())
            units = [((qm[:, e, P * qb:P * qb + P],), (kn,), N,
                      [vb[:, tb, 64 * e:64 * e + 64] for tb in range(4)],
                      bank[6][64 * e:64 * e + 64, P * qb:P * qb + P], bi[:, e, qb, :],
                      {(0, 0): "first", (1, 1): "last"}.get((e, qb)))
                     for e in range(2) for qb in range(2)]

            def pair(n, m):
                out = att[:, bass.ds(i + 4, 1), :].rearrange("p a t -> p (a t)")
                ctl.note("pair", A.do(lambda: s_.copy(out, bank[6][:, 0:T]), m))

            self.softmax_units(units, 64 ** -0.5, sc, pair)
            ctl.note("pair_p", P_.now())

        ctl.straight.clear()
        ctl.loop_over(4, [ENG.PE, ENG.DVE, ENG.Activation], heads)
        self.bounds()
        self.mixer_out(1, att, T)


def build(nc, t, parts, dumps=()):
    with ExitStack() as es:
        m = Machine(nc, t, es)
        g = m.G
        first = Load(m.ctl, m.sem("s_first"), "first")
        for dst, name in ((m.cols, "cols"), (m.ident, "ident"), (m.ones, "ones"), (m.blk64, "blk64")):
            got = first.start(g, dst[:, :], t[name][:, :])
        got = first.start(g, m.H[:, :, 0:T], t["x"])
        for q in (m.P, m.V, m.A, g):
            q.wait(got)
        names = [s for p in parts for s in PART_STAGES[p]]
        m.feed(names)
        for p in parts:
            kind, l = p[:-1], int(p[-1])
            if kind == "ffn":
                with m.scope(w_hi=(2, SLOT // 2), w_lo=(2, SLOT // 2), x_hi=(KT, 2 * T), x_lo=(KT, 2 * T),
                             u_hi=(FT, 2 * T), u_lo=(FT, 2 * T)):
                    m.ffn(l // 2, l % 2)
            elif kind == "conv":
                with m.scope(**m.BOXES):
                    m.conv_layer(l)
            else:
                with m.scope():
                    {"ssm": lambda: m.ssm_layer(l),
                     "rwkv": lambda: m.rwkv_layer(l), "ada": m.ada, "ab": m.mixer_ab,
                     "cd": m.mixer_cd}[kind]()
                if kind in ("ssm", "rwkv"):
                    with m.scope(**m.BOXES):
                        m.tail(l, "sc" if kind == "ssm" else None)
        m.bounds(m.S)
        s_out = m.sem("s_out")
        m.S.eng.dma_start(t["out"], m.H[:, :, 0:T]).then_inc(s_out, 16)
        m.S.eng.wait_ge(s_out, 16)
        for n, (name, ap) in enumerate(m.dumps if dumps else ()):
            m.S.eng.dma_start(t[name], ap).then_inc(s_out, 16)
            m.S.eng.wait_ge(s_out, 16 * (n + 2))


PART_STAGES = {
    "conv0": ["conv_in0", "out0", "ple0"], "ssm1": ["ssm_in", "ada_s", "glu", "out1", "ple1"],
    "rwkv2": ["lora", "rkvz", "ada_r", "out2", "ple2"], "conv3": ["conv_in3", "out3", "ple3"], "ada0": [],
    "ffn0": ["f00a", "f00b"], "ab0": ["ab_in", "ab_av", "ukv", "ab_out"], "ffn1": ["f01a", "f01b"],
    "ffn2": ["f10a", "f10b"], "cd0": ["cd_in", "cd_v", "cd_out"], "ffn3": ["f11a", "f11b"],
}
PARTS = ["conv0", "ssm1", "rwkv2", "conv3", "ada0", "ffn0", "ab0", "ffn1", "ffn2", "cd0", "ffn3"]


def tiles(w, order):
    return np.concatenate([w[k * P:(k + 1) * P, m * P:(m + 1) * P] for k, m in order], axis=1)


def whole(w, per=2):
    nk, nm = w.shape[0] // P, w.shape[1] // P
    return np.stack([tiles(w, [(k, m) for m in range(c, c + per) for k in range(nk)])
                     for c in range(0, nm, per)])


def fcol(v):
    return np.ascontiguousarray(v.reshape(-1, P).T)


def fmajor(a):
    return np.ascontiguousarray(a.T.reshape(-1, P, a.shape[0]).transpose(1, 0, 2))


def lay_out(inp):
    o = {}
    o["x"] = fmajor(inp["x"][0])
    o["p"] = np.stack([fmajor(inp["p"][l, 0]) for l in range(DEPTH1)])
    for l in (0, 3):
        w = inp["conv_w_in"][l // 3]
        bg, cg, h, z = (w[:, k * D:(k + 1) * D] for k in range(4))
        o[f"conv_in{l}"] = np.concatenate([
            np.stack([np.concatenate([tiles(a, [(k, m) for k in range(KT)]) for a in ab], axis=1)
                      for ab in ((cg, h), (bg, z))]) for m in range(KT)])
        o[f"out{l}"] = whole(inp["conv_w_out"][l // 3])
    for l in range(DEPTH1):
        o[f"ple{l}"] = np.stack([np.concatenate([
            tiles(inp["ple_gate"][l], [(k, m) for k in range(KT)]),
            tiles(inp["ple_proj"][l], [(k, m) for k in range(2)])], axis=1) for m in range(KT)])
    c = np.zeros((P, NCOL), np.float32)

    def put(name, a):
        c[:, COLS[name]:COLS[name] + a.shape[1]] = a

    put("conv_k", np.concatenate([fcol(inp["conv_k"][j, s]) for j in range(2) for s in range(3)], 1))
    put("ln_g", np.concatenate([fcol(inp["ln_g"][l]) for l in range(4)], 1))
    put("ln_b", np.concatenate([fcol(inp["ln_b"][l]) for l in range(4)], 1))
    lay_out_more(inp, o, put)
    o["cols"] = c
    o["ident"] = np.eye(P, dtype=np.float32)
    o["ones"] = np.ones((P, P), np.float32)
    o["blk64"] = np.kron(np.eye(2), np.ones((64, 64))).astype(np.float32)
    return o


def lay_out_more(inp, o, put):
    o["ssm_in"], o["glu"] = whole(inp["ssm_w_in"][0]), whole(inp["ssm_w_glu"][0])
    o["out1"] = whole(inp["ssm_w_out"][0])
    twice = lambda a: np.ascontiguousarray(np.concatenate([a.T, a.T]))
    o["s_lre"], o["s_lim"] = twice(inp["ssm_lam_re"][0]), twice(inp["ssm_lam_im"][0])
    o["s_ldt"] = np.ascontiguousarray(np.broadcast_to(inp["ssm_log_dt"][0][None], (P, G)))
    br, bi = (inp[n][0].transpose(1, 0, 2).reshape(NP_, G * GH) for n in ("ssm_b_re", "ssm_b_im"))
    cr, ci = (inp[n][0].transpose(2, 0, 1).reshape(NP_, G * GH) for n in ("ssm_c_re", "ssm_c_im"))
    o["s_b1"], o["s_b2"] = np.concatenate([br, bi]), np.concatenate([bi, br])
    o["s_c1"], o["s_c2"] = np.concatenate([cr, ci]), np.concatenate([ci, cr])
    put("ssm_d", fcol(inp["ssm_d"][0]))
    put("b_glu", fcol(inp["ssm_b_glu"][0]))
    put("sgn", np.concatenate([-np.ones((64, 1)), np.ones((64, 1))]))
    o["rkvz"] = np.concatenate([whole(inp["rwkv_w_rkvz"][0, n]) for n in range(4)])
    o["out2"] = whole(inp["rwkv_w_out"][0])
    low = lambda w: w.reshape(KT, P, 64).transpose(1, 0, 2).reshape(P, 512)
    o["lora"] = np.concatenate([low(inp["rwkv_w1"][0]), low(inp["rwkv_a1"][0]),
                                np.concatenate([inp["rwkv_w2"][0], inp["rwkv_a2"][0]])], axis=1)[None]
    put("mu", np.concatenate([fcol(inp["rwkv_mu"][0, n]) for n in range(6)], 1))
    for name in ("w0", "a0", "k_k", "k_a", "r_k", "lnx_g", "lnx_b"):
        put(name, fcol(inp["rwkv_" + name][0]))
    put("half", np.kron(np.eye(2), np.ones((64, 1))))
    s_, t_ = np.meshgrid(np.arange(P), np.arange(P), indexing="ij")
    chunk = s_ // 64 == t_ // 64

    def joins(lv):
        return (s_ >> (lv + 1) == t_ >> (lv + 1)) & ((t_ >> lv) % 2 == 1) & ((s_ >> lv) % 2 == 0)

    o["r_masks"] = np.concatenate(
        [chunk & (s_ < t_), chunk & (s_ <= t_), (chunk & (s_ < t_)).T, joins(0).T, joins(0)]
        + [joins(lv) for lv in range(1, 6)], axis=1).astype(np.float32)
    o["ctx"] = fmajor(inp["ctx_2"][0])
    c2 = np.stack([inp["c_2"][0].reshape(KT, P), inp["c_ctx_2"].reshape(KT, P)], axis=-1)
    put("c", c2.transpose(1, 0, 2).reshape(P, 2 * KT))
    ada = np.concatenate([inp["ada_w_2"][l].reshape(2, 4, P, -1, 512).transpose(3, 0, 2, 1, 4)
                          .reshape(-1, P, 2048) for l in range(DEPTH2)])
    o["ada_s"], o["ada_r"] = ada[:2 * ADA_SSM], ada[2 * ADA_SSM:]
    put("ada_b", np.concatenate([fcol(inp["ada_b_2"][l]) for l in range(DEPTH2)], 1))
    put("norm_g", np.concatenate([fcol(inp["norm_g_2"][l, s]) for l in range(2) for s in range(3)], 1))
    for l in range(DEPTH2):
        for s in range(2):
            w1, w3, w2 = (inp[n][l, s] for n in ("ffn_w1_2", "ffn_w3_2", "ffn_w2_2"))
            o[f"f{l}{s}a"] = np.concatenate([whole(w1, 1), whole(w3, 1)], axis=2)
            o[f"f{l}{s}b"] = whole(w2, 1).reshape(KT, P, 2, FT // 2 * P).transpose(0, 2, 1, 3).reshape(
                2 * KT, P, FT // 2 * P)
    w = inp["ab_w_in_2"][0]
    ab = {}
    at = 0
    for name, n in (("aq", 512), ("ak", 128), ("av", 128), ("bq", 768), ("bkv", 256), ("bkr", 32)):
        ab[name] = w[:, at:at + n]
        at += n
    perm = [h for i in range(4) for h in (i, i + 4)]
    aq = ab["aq"].reshape(D, 8, 64)[:, perm].reshape(D, 512)
    bq = ab["bq"].reshape(D, 8, 96)
    o["ab_in"] = whole(np.concatenate([aq, ab["ak"], bq[:, :, :64].reshape(D, 512),
                                       bq[:, :, 64:].reshape(D, 256), ab["bkv"],
                                       np.tile(ab["bkr"], (1, 4))], axis=1))
    o["ab_av"] = moving(ab["av"])[None]
    u = inp["ab_b_wukv_2"][0].reshape(256, 8, 128)
    o["ukv"] = np.concatenate([tiles(u[:, :, :64].reshape(256, 512), [(k, m) for m in range(4) for k in (0, 1)]),
                               moving(u[:, :, 64:].reshape(256, 512))], axis=1)[None]
    wo = inp["ab_w_out_2"][0]
    o["ab_out"] = whole(np.concatenate([wo[:512].reshape(8, 64, D)[perm].reshape(512, D), wo[512:]]))
    put("aqn", np.tile(inp["ab_a_qn_2"][0], 2)[:, None])
    put("akn", np.tile(inp["ab_a_kn_2"][0], 2)[:, None])
    for name, g in (("bq", inp["ab_b_qn_2"][0]), ("bk", inp["ab_b_kn_2"][0])):
        put(name + "n", np.tile(g[:64], 2)[:, None])
        put(name + "r", np.tile(g[64:], 4)[:, None])
    put("kvn", fcol(inp["ab_b_kvn_2"][0]))
    put("quart", np.kron(np.eye(4), np.ones((32, 1))))
    f = np.arange(P)
    E = [(f[:, None] // 32 == 2 * p + f[None] // 64) for p in range(2)]

    def rotate(hb):
        r = np.zeros((P, P))
        for d in range(P):
            if d % hb < hb // 2:
                r[d + hb // 2, d] = -1
            else:
                r[d - hb // 2, d] = 1
        return r

    def rope(dim):
        inv = np.float32(10000.0) ** (-np.arange(0, dim // 2, 2, dtype=np.float32) / np.float32(dim // 2))
        pos = np.arange(T)
        ang = np.concatenate([np.concatenate([a, a], 1) for a in
                              ((pos // 64)[:, None] * inv[None], (pos % 64)[:, None] * inv[None])], 1)
        ang = np.tile(ang.astype(np.float32).T, (P // dim, 1))
        return [np.cos(ang), np.sin(ang)]

    o["ab_consts"] = np.concatenate(
        [f[:, None] // 32 == f[None] // 32, E[0], E[1], E[0].T, E[1].T, rotate(32), rotate(16)]
        + rope(64) + rope(32), axis=1).astype(np.float32)

    w = inp["cd_w_in_2"][0]
    q, zf, zb, iv, gate, dq, dk, dv = (w[:, 512 * k:512 * k + 512] for k in range(8))
    o["cd_in"] = whole(np.concatenate([zf, zb, dk, q, gate, dq], axis=1))
    o["cd_v"] = np.concatenate([moving(a).reshape(P, 2, 4 * 512).transpose(1, 0, 2) for a in (iv, dv)])
    o["cd_out"] = whole(inp["cd_w_out_2"][0])
    for n in range(2):
        put(f"lb{n}", np.concatenate([fcol(inp["hgrn_lb_2"][n, d]) for d in range(2)], 1))
    for name, key in (("cgn", "cd_c_gn_2"), ("dqn", "cd_d_qn_2"), ("dkn", "cd_d_kn_2")):
        put(name, np.tile(inp[key][0], 2)[:, None])
    none = np.zeros((P, P))
    o["h_masks"] = np.concatenate([joins(lv) for lv in range(7)] + [joins(lv).T for lv in range(7)]
                                  + [np.eye(P), none], axis=1).astype(np.float32)
    tok = np.arange(T)
    row, col = tok // 64, tok % 64
    start = np.clip(col - 8, 0, 48)
    inside = (col[None] >= start[:, None]) & (col[None] < start[:, None] + 16)
    dr = row[None] - row[:, None] + 7
    dc = np.where(inside, col[None] - col[:, None] + 15, 0)
    rpb = np.where(inside[None], inp["cd_d_rpb_2"][0][:, dr, dc], np.float32(0))
    o["d_bias"] = np.ascontiguousarray(rpb.reshape(8, 2, P, T).transpose(2, 0, 1, 3).reshape(P, -1))
    o["d_mask"] = np.where(inside, 0, NEG).astype(np.float32).reshape(2, P, T).transpose(
        1, 0, 2).reshape(P, -1)


def moving(w):
    return np.ascontiguousarray(w.reshape(-1, P, w.shape[1]).transpose(1, 0, 2).reshape(P, -1))


def kernel(**inputs):
    import concourse.bacc as bacc
    from concourse.bass_utils import run_bass_kernel_spmd

    arrays = lay_out({k: np.asarray(v) for k, v in inputs.items()})
    nc = bacc.Bacc("TRN2", target_bir_lowering=False, num_devices=1)
    t, send = {}, {}
    for name, a in arrays.items():
        send["in_" + name] = np.ascontiguousarray(a)
        t[name] = nc.dram_tensor("in_" + name, a.shape, F32, kind="ExternalInput").ap()
    for name in ("scratch_u", "scratch_y"):
        t[name] = nc.dram_tensor(name, (D * T,), F32, kind="Internal").ap()
    t["mods"] = nc.dram_tensor("mods", (2, DEPTH2 * 9 * D), F32, kind="Internal").ap()
    t["out"] = nc.dram_tensor("out_x", (P, KT, T), F32, kind="ExternalOutput").ap()
    build(nc, t, PARTS)
    got = run_bass_kernel_spmd(nc, [send], core_ids=[0]).results[0]["out_x"]
    return np.ascontiguousarray(got.transpose(1, 0, 2).reshape(D, T).T)[None]
```

```python
from contextlib import ExitStack, contextmanager

import numpy as np

import concourse.bass as bass
from concourse import mybir

F32, F32R = mybir.dt.float32, mybir.dt.float32r
ALU = mybir.AluOpType
ACT = mybir.ActivationFunctionType
AX = mybir.AxisListType.X
ENG = mybir.EngineType
MUL, ADD, SUB, MAX, MIN, BYP = ALU.mult, ALU.add, ALU.subtract, ALU.max, ALU.min, ALU.bypass

P = 128
D = 1024
KT = D // P
T = 256
DEPTH1, DEPTH2 = 4, 2
ALPHA = (2 * DEPTH1) ** 0.25
LN_EPS, GN_EPS, RMS_EPS = 1e-5, 64e-5, 1e-6
FF = 2816
FT = FF // P
G, NP_, GH = 64, 64, 16
SL = 8
SC = T // SL
NS = 4
SLOT = 16 * P
ADA = DEPTH2 * 9 * D // 512
ADA_SSM = 20
START = 4000
NEG = -1e30
NSEL, ROWS = 17, 32

COLS = {}


def _cols():
    at = 0
    for name, n in (("conv_k", 48), ("ssm_d", 8), ("b_glu", 8), ("mu", 48), ("w0", 8), ("a0", 8),
                    ("k_k", 8), ("k_a", 8), ("r_k", 8), ("lnx_g", 8), ("lnx_b", 8), ("ln_g", 32),
                    ("ln_b", 32), ("norm_g", 48), ("ada_b", 144), ("c", 16), ("aqn", 1), ("akn", 1),
                    ("bqn", 1), ("bqr", 1), ("bkn", 1), ("bkr", 1), ("kvn", 2), ("lb0", 8),
                    ("lb1", 8), ("cgn", 1), ("dqn", 1), ("dkn", 1), ("sgn", 1), ("half", 2), ("quart", 4)):
        COLS[name] = at
        at += n
    return at


NCOL = _cols()

STAGES = {}


def _stages():
    for l in range(DEPTH1):
        if l % 3 == 0:
            STAGES[f"conv_in{l}"] = (16, 2048)
        elif l == 1:
            STAGES["ssm_in"] = (8, 2048)
            STAGES["glu"] = (4, 2048)
        else:
            STAGES["rkvz"] = (16, 2048)
            STAGES["lora"] = (1, 2048)
        STAGES[f"out{l}"] = (4, 2048)
        STAGES[f"ple{l}"] = (8, 1280)
    STAGES["ada_s"] = (2 * ADA_SSM, 2048)
    STAGES["ada_r"] = (2 * (ADA - ADA_SSM), 2048)
    for l in range(DEPTH2):
        STAGES[f"f{l}0a"] = (22, 2048)
        STAGES[f"f{l}0b"] = (16, 1408)
        if l == 0:
            STAGES["ab_in"] = (7, 2048)
            STAGES["ab_av"] = (1, 1024)
            STAGES["ukv"] = (1, 2048)
            STAGES["ab_out"] = (4, 2048)
        else:
            STAGES["cd_in"] = (12, 2048)
            STAGES["cd_v"] = (4, 2048)
            STAGES["cd_out"] = (4, 2048)
        STAGES[f"f{l}1a"] = (22, 2048)
        STAGES[f"f{l}1b"] = (16, 1408)


_stages()


class Mark:

    def __init__(self, sem, key, v, loop=None):
        self.sem, self.key, self.v, self.loop = sem, key, v, loop


class Loop:
    def __init__(self, i, per, n):
        self.i, self.per, self.n, self.notes = i, per, n, {}


class Queue:

    def __init__(self, ctl, eng, sem, name):
        self.ctl, self.eng, self.sem, self.name = ctl, eng, sem, name
        self.n = START
        self.met = {}

    def now(self):
        return Mark(self.sem, self.name, self.n, self.ctl.loop)

    def wait(self, m):
        loop = self.ctl.loop
        if m is None or self.ctl.dry:
            return
        if m.loop is None or m.loop is not loop:
            v = m.v if m.loop is None else m.v + (m.loop.n - 1) * m.loop.per[m.key]
            if self.met.get(m.key, -1) >= v:
                return
            if loop is None:
                self.met[m.key] = v
            self.eng.wait_ge(m.sem, v)
        else:
            per = m.loop.per[m.key]
            assert m.v > 0
            if self.met.get((m.key, "loop"), -1) >= m.v:
                return
            self.met[(m.key, "loop")] = m.v
            self.eng.wait_ge(m.sem, loop.i * per + m.v if per else m.v)

    def do(self, make, *after):
        for m in after:
            self.wait(m)
        self.n += 1
        if not self.ctl.dry:
            make().then_inc(self.sem, 1)
        return self.now()

    def quiet(self, make, *after):
        for m in after:
            self.wait(m)
        if not self.ctl.dry:
            make()


class Control:
    def __init__(self, nc):
        self.nc, self.loop, self.dry = nc, None, False
        self.queues, self.straight = [], {}

    def note(self, name, mark):
        (self.straight if self.loop is None else self.loop.notes)[name] = mark

    def last(self, name):
        if self.dry:
            return None
        if self.loop is None:
            return self.straight.get(name)
        if name in self.loop.notes:
            return self.loop.notes[name]
        m = self.loop.before[name]
        return Mark(m.sem, m.key, m.v - self.loop.per[m.key], self.loop)

    def loop_over(self, n, engines, body):
        base = {q.name: q.n for q in self.queues}
        counts = [(c, c.n) for c in self.counters]
        self.dry, self.loop = True, Loop(0, {}, n)
        body(0)
        notes = self.loop.notes
        per = {q.name: q.n - base[q.name] for q in self.queues}
        for c, v in counts:
            per[c.key] = (c.n - v) * c.unit
            c.n = v
        for q in self.queues:
            q.n = base[q.name]
        self.dry = False
        with self.nc.Fori(0, n, engines=engines) as i:
            self.loop = Loop(i, per, n)
            self.loop.before = notes
            for q in self.queues:
                q.met = {k: v for k, v in q.met.items() if not isinstance(k, tuple)}
            body(i)
            self.straight.update(self.loop.notes)
            self.loop = None
        for q in self.queues:
            q.met = {k: v for k, v in q.met.items() if not isinstance(k, tuple)}
            q.n = base[q.name] + n * per[q.name]
        for c, v in counts:
            c.n = v + n * per[c.key] // c.unit


class Load:

    unit = 16

    def __init__(self, ctl, sem, key):
        self.ctl, self.sem, self.key, self.n = ctl, sem, key, 0
        ctl.counters.append(self)

    def start(self, q, dst, src, *after):
        for m in after:
            q.wait(m)
        self.n += 1
        if not self.ctl.dry:
            q.eng.dma_start(dst, src).then_inc(self.sem, 16)
        return Mark(self.sem, self.key, 16 * self.n, self.ctl.loop)


def bc(ap, n):
    return ap.unsqueeze(1).broadcast_to([ap.shape[0], n, ap.shape[1]])


def bc_in(ap, n):
    return ap.unsqueeze(2).broadcast_to([ap.shape[0], ap.shape[1], n])


def fr(ap):
    return ap.bitcast(F32R)


class Arena:

    def __init__(self, tensor, size):
        self.t, self.size, self.at = tensor, size, 0

    def __call__(self, *shape):
        n = int(np.prod(shape))
        ap = self.t[:, self.at:self.at + n]
        self.at += n
        assert self.at <= self.size, (self.at, self.size)
        if len(shape) == 1:
            return ap
        names = "abcde"[:len(shape)]
        return ap.rearrange(f"p ({' '.join(names)}) -> p {' '.join(names)}",
                            **{c: s for c, s in zip(names[1:], shape[1:])})


class Machine:

    def __init__(self, nc, t, es):
        self.nc, self.t, self.es = nc, t, es
        self.ctl = ctl = Control(nc)
        ctl.counters = []
        self.P = Queue(ctl, nc.tensor, self.sem("s_pe"), "P")
        self.V = Queue(ctl, nc.vector, self.sem("s_dve"), "V")
        self.A = Queue(ctl, nc.scalar, self.sem("s_act"), "A")
        self.G = Queue(ctl, nc.gpsimd, self.sem("s_pool"), "G")
        self.S = Queue(ctl, nc.sync, self.sem("s_sp"), "S")
        ctl.queues = [self.P, self.V, self.A, self.G, self.S]
        for q in ctl.queues[:4]:
            q.eng.sem_inc(q.sem, START)
        self.slot_sem = [self.sem(f"s_slot{k}") for k in range(NS)]
        self.s_free = self.sem("s_free")
        self.P.eng.sem_inc(self.s_free, START)
        self.n, self.key, self.unit = 0, "free", 1
        ctl.counters.append(self)
        self.loaded = 0
        self.ring = self.sbuf("ring", NS, SLOT)
        self.H = self.sbuf("H", KT, 2 * T)
        self.cols = self.sbuf("cols", NCOL)
        self.ident = self.sbuf("ident", P)
        self.ones = self.sbuf("ones", P)
        self.blk64 = self.sbuf("blk64", P)
        self.cond = self.sbuf("cond", KT, 2)
        self.row = self.sbuf("row", 512)
        self.mod = self.sbuf("mod", DEPTH2 * 9 * KT * 2)
        self.left, self.scopes = 39200, 0
        self.box, self.arena, self.arena_size = {}, None, 0
        self.bank = [es.enter_context(nc.psum_tensor(f"bank{k}", [P, 512], F32)) for k in range(8)]
        self.misc = Load(ctl, self.sem("s_misc"), "misc")
        self.shuffle = Load(ctl, self.sem("s_shuffle"), "shuffle")
        self.sent = Load(ctl, self.sem("s_sent"), "sent")
        self.moved = Load(ctl, self.sem("s_moved"), "moved")
        self.moved.n = SL + 1
        nc.scalar.sem_inc(self.moved.sem, 16 * self.moved.n)

    @contextmanager
    def scope(self, total=None, **boxes):
        before = self.box, self.arena, self.arena_size, self.left
        total = total or self.left
        self.left, self.scopes, self.box = self.left - total, self.scopes + 1, {}
        boxes["arena"] = (total - sum(int(np.prod(s)) for s in boxes.values()),)
        with ExitStack() as es:
            for name, shape in boxes.items():
                self.box[name] = es.enter_context(
                    self.nc.sbuf_tensor(f"{name}_{self.scopes}", [P, *shape], F32))
            self.arena, self.arena_size = self.box["arena"], boxes["arena"][0]
            yield
        self.box, self.arena, self.arena_size, self.left = before

    def sem(self, name):
        return self.es.enter_context(self.nc.semaphore(name))

    def sbuf(self, name, *shape):
        return self.es.enter_context(self.nc.sbuf_tensor(name, [P, *shape], F32))

    def col(self, name, k=0):
        return self.cols[:, bass.ds(k + COLS[name], 1)]

    def bounds(self, *queues):
        marks = [q.now() for q in (self.P, self.V, self.A, self.G)] + [self.freed()]
        for q in queues or (self.P, self.V, self.A, self.G, self.S):
            for m in marks:
                if not (q is self.P and m.key in ("P", "free")):
                    q.wait(m)

    def feed(self, names):
        sp = self.nc.sync
        for name in names:
            nch, width = STAGES[name]
            src, b = self.t[name], self.loaded

            def put(j, at, ahead):
                k = (b + j) % NS
                sp.wait_ge(self.s_free, ahead + (START + b + j - NS + 1))
                sp.dma_start(self.ring[:, k, 0:width], src[at, :, :].rearrange("a p n -> (a p) n")
                             if at is not j else src[j, :, :]).then_inc(self.slot_sem[k], 16)

            full = nch // NS if nch >= 2 * NS else 0
            if full:
                with self.nc.Fori(0, full, engines=[ENG.SP]) as i:
                    for j in range(NS):
                        put(j, bass.ds(i * NS + j, 1), i * NS)
            for j in range(full * NS, nch):
                put(j, j, 0)
            self.loaded += nch

    def take(self):
        n, k = self.n, self.n % NS
        loop = self.ctl.loop
        if not self.ctl.dry:
            v = 16 * (n // NS + 1)
            if loop is None:
                self.P.eng.wait_ge(self.slot_sem[k], v)
            else:
                assert loop.per["free"] % NS == 0
                self.P.eng.wait_ge(self.slot_sem[k], loop.i * (16 * loop.per["free"] // NS) + v)
        return self.ring[:, k, :]

    def freed(self):
        return Mark(self.s_free, "free", START + self.n, self.ctl.loop)

    def give(self, make):
        self.n += 1
        if not self.ctl.dry:
            make().then_inc(self.s_free, 1)
        return self.freed()

    def mm(self, out, lhsT, rhs, start, stop):
        return lambda: self.nc.tensor.matmul(out, lhsT, rhs, start=start, stop=stop)

    def product(self, out, w, nk, rhs, tile0=0, last=True, start=True, stop=True):
        m = None
        for k in range(nk):
            make = self.mm(out, w[:, (tile0 + k) * P:(tile0 + k + 1) * P], rhs(k),
                           start and k == 0, stop and k == nk - 1)
            if k < nk - 1:
                self.P.quiet(make)
            elif last:
                m = self.give(make)
            else:
                m = self.P.do(make)
        return m

    def w_buffer(self, n, part):
        return (2 * n + part) % self.box["w_hi"].shape[1]

    def split_part(self, ahead, tiles, part):
        nc, n = self.nc, self.n + ahead
        k, loop, buf = n % NS, self.ctl.loop, self.w_buffer(n, part)
        raw = self.ring[:, k, part * tiles[0] * P:(part * tiles[0] + tiles[part]) * P]
        hi, lo = (self.box[x][:, buf, 0:tiles[part] * P] for x in ("w_hi", "w_lo"))
        if part == 0 and not self.ctl.dry:
            v = 16 * (n // NS + 1)
            self.A.eng.wait_ge(self.slot_sem[k],
                               v if loop is None else loop.i * (16 * loop.per["free"] // NS) + v)
        m = self.A.do(lambda: nc.scalar.copy(fr(hi), raw), self.ctl.last(f"used{buf}"))
        m = self.V.do(lambda: nc.vector.tensor_tensor(fr(lo), raw, hi, SUB), m)
        self.ctl.note(f"split{buf}", m)
        return m

    def product_split(self, out, part, nk, rhs, start=True, stop=True):
        buf = self.w_buffer(self.n, part)
        self.P.wait(self.ctl.last(f"split{buf}"))
        for k in range(nk):
            at = slice(k * P, (k + 1) * P)
            wh, wl = (fr(self.box[n][:, buf, at]) for n in ("w_hi", "w_lo"))
            xh, xl = (fr(x) for x in rhs(k))
            for n, (a, b) in enumerate(((wh, xh), (wh, xl), (wl, xh))):
                end = k == nk - 1 and n == 2
                make = self.mm(out, a, b, start and k == 0 and n == 0, stop and end)
                if not end:
                    self.P.quiet(make)
        m = self.give(make) if part else self.P.do(make)
        self.ctl.note(f"used{buf}", m)
        return m

    def values_split(self, part, nk, out, x, start, stop, last):
        buf, width = self.w_buffer(self.n, part), SLOT // 2 // nk
        self.P.wait(self.ctl.last(f"split{buf}"))
        for tb in range(4):
            for k in range(nk):
                at = slice(k * width, (k + 1) * width)
                wh, wl = (fr(self.box[n][:, buf, at]) for n in ("w_hi", "w_lo"))
                xh, xl = (fr(a) for a in x(k, tb))
                for n, (a, b) in enumerate(((xh, wh), (xh, wl), (xl, wh))):
                    make = self.mm(out(tb), a, b, start and k == 0 and n == 0,
                                   stop and k == nk - 1 and n == 2)
                    if (tb, k, n) != (3, nk - 1, 2):
                        self.P.quiet(make)
        m = self.give(make) if last else self.P.do(make)
        self.ctl.note(f"used{buf}", m)
        return m

    def colsum(self, out, src, nk, mat=None, after=()):
        for m in after:
            self.P.wait(m)
        mat = self.ones if mat is None else mat
        for k in range(nk):
            make = self.mm(out, mat[:, :], src(k), k == 0, k == nk - 1)
            m = self.P.do(make) if k == nk - 1 else self.P.quiet(make)
        return m

    def rstd(self, out, var, scale, eps, after):
        m = self.V.do(lambda: self.nc.vector.tensor_scalar(out, var, scale, eps, MUL, ADD), after)
        m = self.A.do(lambda: self.nc.scalar.activation(out, out, ACT.Sqrt), m)
        return self.V.do(lambda: self.nc.vector.reciprocal(out, out), m)

    def layer_norm(self, R, l, dst, tmp, after):
        P_, V, A, nc = self.P, self.V, self.A, self.nc
        dev, sq, rs = tmp(KT, T), tmp(KT, T), tmp(T)
        mean, var = self.bank[0][:, 0:T], self.bank[1][:, 0:T]
        m = self.colsum(mean, lambda k: R[:, k, :], KT, after=[after])
        m = V.do(lambda: nc.vector.scalar_tensor_tensor(dev[:, :, :], bc(mean, KT), -1.0 / D, R, MUL, ADD), m)
        s = A.do(lambda: nc.scalar.activation(sq[:, :, :], dev[:, :, :], ACT.Square), m)
        m = self.colsum(var, lambda k: sq[:, k, :], KT, after=[s])
        m = self.rstd(rs, var, 1.0 / D, LN_EPS, m)
        m = V.do(lambda: nc.vector.tensor_tensor(dev[:, :, :], dev[:, :, :], bc(rs, KT), MUL), m)
        for k in range(KT):
            g, b = self.col("ln_g", 8 * l + k), self.col("ln_b", 8 * l + k)
            V.do(lambda: nc.vector.tensor_scalar(dst[:, k, :], dev[:, k, :], g, b, MUL, ADD), m)

    BOXES = dict(w_hi=(4, SLOT // 2), w_lo=(4, SLOT // 2), x_hi=(KT, T), x_lo=(KT, T),
                 y_hi=(KT, T), y_lo=(KT, T), p_hi=(2, T), p_lo=(2, T))
    IN_BOXES = dict(w_hi=(2, SLOT // 2), w_lo=(2, SLOT // 2), x_hi=(KT, 2 * T), x_lo=(KT, 2 * T))
    EIGHTS = (KT, KT)

    def halves(self, name):
        hi, lo = self.box[name + "_hi"], self.box[name + "_lo"]
        return lambda k: (hi[:, k, :], lo[:, k, :])

    def split_input(self, name, x, n, after):
        hi, lo = self.box[name + "_hi"], self.box[name + "_lo"]
        for k in range(0, n, 4):
            at = slice(k, min(k + 4, n))
            m = self.A.do(lambda: self.nc.scalar.copy(fr(hi[:, at, :]), x[:, at, :]), after)
            m = self.V.do(lambda: self.nc.vector.tensor_tensor(fr(lo[:, at, :]), x[:, at, :],
                                                               hi[:, at, :], SUB), m)
        return m

    def tail(self, l, order=None, ahead=False):
        P_, V, A, nc, X = self.P, self.V, self.A, self.nc, self.H
        tmp = Arena(self.arena, self.arena_size)
        R, R2, sig, pT = tmp(KT, T), tmp(KT, T), tmp(2, T), tmp(2, T)
        r_hi, r_lo = self.box["x_hi"], self.box["x_lo"]
        got = self.misc.start(self.G, pT[:, :, :], self.t["p"][l])
        gates = (KT, 2)
        if not ahead:
            for part in range(2):
                self.split_part(0, self.EIGHTS, part)
        P_.wait(self.split_input("y", X[:, :, T:2 * T], KT, V.now()))
        y_at, r_at, p_at = (self.halves(n) for n in "yxp")
        free = [None] * 8
        for m in range(8):
            e = m % 2
            y = self.bank[m][:, 0:T]
            self.split_part(1, self.EIGHTS if m < 6 else gates, e)
            if m == 3:
                A.wait(got)
                self.split_input("p", pT, 2, None)
            done = self.product_split(y, e, KT, y_at)
            x, r = X[:, m, 0:T], R[:, m, :]
            if order == "sc":
                y = y.rearrange("p (s c) -> p c s", s=SL)
                x, r = (a.rearrange("p (c s) -> p c s", s=SL) for a in (x, r))
            f = V.do(lambda: nc.vector.scalar_tensor_tensor(r, x, ALPHA, y, MUL, ADD), done)
            free[m] = f
            f = V.do(lambda: nc.vector.tensor_copy(fr(r_hi[:, m, :]), R[:, m, :]), f)
            rdy = V.do(lambda: nc.vector.tensor_tensor(fr(r_lo[:, m, :]), R[:, m, :], r_hi[:, m, :], SUB), f)
        P_.wait(rdy)
        for m in range(KT):
            bg, bp, e = m % 4, 4 + m % 4, m % 2
            gate, proj = self.bank[bg][:, 0:T], self.bank[bp][:, 0:T]
            P_.wait(free[bg])
            P_.wait(free[bp])
            for part in range(2 if m < KT - 1 else 0):
                self.split_part(1, gates, part)
            self.product_split(gate, 0, KT, r_at)
            done = self.product_split(proj, 1, 2, p_at)
            s = A.do(lambda: nc.scalar.activation(sig[:, e, :], gate, ACT.Sigmoid), done, free[bp])
            v = V.do(lambda: nc.vector.tensor_tensor(sig[:, e, :], sig[:, e, :], proj, MUL), s)
            free[bg] = free[bp] = v
            V.do(lambda: nc.vector.tensor_tensor(R2[:, m, :], R[:, m, :], sig[:, e, :], ADD), v)
            if e == 1:
                A.wait(V.now())
        self.bounds(P_)
        self.layer_norm(R2, l, X[:, :, 0:T], tmp, V.now())
        self.bounds()

    def conv_layer(self, l):
        P_, V, A, nc, X, ctl = self.P, self.V, self.A, self.nc, self.H, self.ctl
        tmp = Arena(self.arena, self.arena_size)
        U = [tmp(T + 2) for _ in range(2)]
        hs, sz, cv = ([tmp(T) for _ in range(2)] for _ in range(3))
        for e in range(2):
            V.do(lambda: nc.vector.memset(U[e][:, 0:2], 0.0))
        V.wait(V.now())
        kofs, up = 24 * (l // 3), self.EIGHTS
        x_at = self.halves("x")
        for part in range(2):
            self.split_part(0, up, part)
        P_.wait(self.split_input("x", X[:, :, 0:T], KT, None))

        def pair(i):
            for e in range(2):
                b = self.bank[4 * e:4 * e + 4]
                u = U[e]
                P_.wait(ctl.last(f"free{e}"))
                self.split_part(1, up, 0)
                self.product_split(b[0][:, 0:T], 0, KT, x_at)
                self.split_part(1, up, 1)
                hm = self.product_split(b[1][:, 0:T], 1, KT, x_at)
                self.split_part(1, up, 0)
                A.wait(ctl.last(f"free{e}"))
                a = A.do(lambda: nc.scalar.copy(hs[e], b[1][:, 0:T]), hm)
                V.do(lambda: nc.vector.tensor_tensor(u[:, 2:T + 2], b[0][:, 0:T], hs[e], MUL), a)
                taps = [self.col("conv_k", i * 2 + (kofs + 8 * tap + e)) for tap in range(3)]
                V.do(lambda: nc.vector.tensor_scalar(cv[e], u[:, 0:T], taps[0], None, MUL), V.now())
                for tap in (1, 2):
                    V.do(lambda: nc.vector.scalar_tensor_tensor(
                        cv[e], u[:, tap:T + tap], taps[tap], cv[e], MUL, ADD), V.now())
                taps_done = V.now()
                cm = self.product_split(b[2][:, 0:T], 0, KT, x_at)
                self.split_part(1, up, 1)
                zm = self.product_split(b[3][:, 0:T], 1, KT, x_at)
                z = A.do(lambda: nc.scalar.activation(sz[e], b[3][:, 0:T], ACT.Silu), zm)
                V.do(lambda: nc.vector.tensor_tensor(cv[e], cv[e], b[2][:, 0:T], MUL), taps_done, cm)
                y = X[:, bass.ds(i * 2 + e, 1), T:2 * T].rearrange("p a t -> p (a t)")
                f = V.do(lambda: nc.vector.tensor_tensor(y, cv[e], sz[e], MUL), V.now(), z)
                ctl.note(f"free{e}", f)

        ctl.loop_over(4, [ENG.PE, ENG.DVE, ENG.Activation], pair)
        self.bounds()
        self.tail(l, ahead=True)

    def ssm_layer(self, l):
        P_, V, A, Gq, nc, X, ctl, t = self.P, self.V, self.A, self.G, self.nc, self.H, self.ctl, self.t
        v_, bank = nc.vector, self.bank
        tmp = Arena(self.arena, self.arena_size)
        UF, UP, ZZ = tmp(KT, SL, SC), tmp(G, SC), tmp(SC, 2, G)
        TT, CA = tmp(G, P), tmp(G, SL + 1, GH)
        Zs = X[:, :, T:2 * T]
        AB, ABT = tmp(16, SL, GH), tmp(16, P)
        t2 = tmp(16 * (SL + 1) * GH)
        B1, B2, C1, C2 = (tmp(G, GH) for _ in range(4))
        small = tmp(10 * G)
        lre, lim, ldt, th, er, ar, ai, w1, w2, w3 = (small[:, G * k:G * k + G] for k in range(10))
        PWr, PWi = tmp(SL + 1, G), tmp(SL + 1, G)
        A8r, A8i = tmp(2, G), tmp(2, G)
        q1, q2 = (small[:, 128 * k:128 * k + 128].rearrange("p (r g) -> p r g", g=G) for k in range(2))
        b1, b2 = t2[:, 0:1024], t2[:, 1024:2048]
        for dst, name in ((lre, "s_lre"), (lim, "s_lim"), (ldt, "s_ldt")):
            self.misc.start(Gq, dst[:, :], t[name][:, :])
        for dst, name in ((b1, "s_b1"), (b2, "s_b2"), (C1, "s_c1"), (C2, "s_c2")):
            flat = dst if name in ("s_b1", "s_b2") else dst.rearrange("p g h -> p (g h)")
            got = self.misc.start(Gq, flat, t[name][:, :])
        b1, b2 = (b.rearrange("p (g h) -> p g h", g=G) for b in (b1, b2))

        free = [None] * 8
        for c in range(8):
            w = self.take()
            for e in range(2):
                m = 2 * c + e
                b = m % 8
                P_.wait(free[b])
                o = bank[b][:, 0:T]
                done = self.product(o, w, KT, lambda k: X[:, k, 0:T], e * KT, e == 1)
                o = o.rearrange("p (c s) -> p s c", s=SL)
                if m < 8:
                    free[b] = V.do(lambda: v_.tensor_copy(UF[:, m, :, :], o), done)
                else:
                    z = Zs[:, m - 8, :].rearrange("p (s c) -> p s c", s=SL)
                    free[b] = A.do(lambda: nc.scalar.activation(z, o, ACT.Silu), done)
            if c == 3:
                u_ready = V.now()
        c = self.cols[:, COLS["c"]:COLS["c"] + 2 * KT].rearrange("p (k n) -> p k n", n=2)
        P_.wait(A.do(lambda: nc.scalar.activation(self.cond[:, :, :], c, ACT.Silu)))
        for b in (6, 7):
            P_.wait(free[b])
        sc1, sc2 = t["scratch_u"], t["scratch_y"]
        wrote = self.shuffle.start(Gq, sc1.rearrange("(p n) -> p n", p=P),
                                   UF.rearrange("p m s c -> p (m s c)"), u_ready)
        Gq.wait(wrote)
        for s in range(SL):
            src = bass.AP(tensor=sc1.tensor, offset=s * SC,
                          ap=[[KT * T, GH], [T, KT], [GH * KT * T, 8], [1, SC]])
            u_in = self.shuffle.start(Gq, UP[s * GH:(s + 1) * GH, :, :]
                                      .rearrange("h (m g) c -> h m g c", g=8), src)

        V.wait(got)
        A.wait(got)
        dt = w1
        d = A.do(lambda: nc.scalar.activation(dt, ldt, ACT.Exp))
        V.do(lambda: v_.tensor_tensor(er, lre, dt, MUL), d)
        V.do(lambda: v_.tensor_tensor(th, lim, dt, MUL))
        d = V.now()
        A.do(lambda: nc.scalar.activation(er, er, ACT.Exp), d)
        V.do(lambda: v_.tensor_scalar(w2, th, 1 / (2 * np.pi), 12582912.0, MUL, ADD), V.now())
        V.do(lambda: v_.tensor_scalar(w2, w2, -12582912.0, None, ADD), V.now())
        for part in (6.28125, 1.9340515136718750e-3, 1.2556659418 * 1e-6):
            V.do(lambda: v_.scalar_tensor_tensor(th, w2, -part, th, MUL, ADD), V.now())
        V.do(lambda: v_.tensor_scalar(th, th, 3.1415925, -3.1415925, MIN, MAX), V.now())
        V.do(lambda: v_.scalar_tensor_tensor(w2, th, -1.0, th, MUL, MAX), V.now())
        V.do(lambda: v_.tensor_scalar(w2, w2, -1.0, np.pi / 2, MUL, ADD), V.now())
        A.do(lambda: nc.scalar.activation(w2, w2, ACT.Sin), V.now())
        A.do(lambda: nc.scalar.activation(th, th, ACT.Sin))
        V.do(lambda: v_.tensor_tensor(ar, er, w2, MUL), A.now())
        V.do(lambda: v_.tensor_tensor(ai, er, th, MUL))
        fr, fi, n = w1, w2, w3
        V.do(lambda: v_.tensor_tensor(fr, lre, lre, MUL))
        V.do(lambda: v_.tensor_tensor(fi, lim, lim, MUL), V.now())
        V.do(lambda: v_.tensor_tensor(th, fr, fi, ADD), V.now())
        V.do(lambda: v_.reciprocal(th, th), V.now())
        V.do(lambda: v_.tensor_scalar(n, ar, -1.0, None, ADD))

        def cross(out, x, y, z, w, op):
            V.do(lambda: v_.tensor_tensor(er, z, w, MUL), V.now())
            V.do(lambda: v_.tensor_tensor(out, x, y, MUL))
            V.do(lambda: v_.tensor_tensor(out, out, er, op), V.now())

        cross(fr, n, lre, ai, lim, ADD)
        cross(fi, ai, lre, n, lim, SUB)
        V.do(lambda: v_.tensor_tensor(fr, fr, th, MUL), V.now())
        V.do(lambda: v_.tensor_tensor(fi, fi, th, MUL), V.now())
        sgn = self.col("sgn")
        V.do(lambda: v_.tensor_scalar(fi, fi, sgn, None, MUL), V.now())
        V.do(lambda: v_.tensor_tensor(B1[:, :, :], b1, bc_in(fr, GH), MUL), V.now())
        V.do(lambda: v_.tensor_tensor(B2[:, :, :], b2, bc_in(fi, GH), MUL))
        V.do(lambda: v_.tensor_tensor(B1[:, :, :], B1[:, :, :], B2[:, :, :], ADD), V.now())
        V.do(lambda: v_.tensor_tensor(B2[:, :, :], b2, bc_in(fr, GH), MUL), V.now())
        V.do(lambda: v_.tensor_tensor(b1, b1, bc_in(fi, GH), MUL))
        V.do(lambda: v_.tensor_tensor(B2[:, :, :], B2[:, :, :], b1, SUB), V.now())
        V.do(lambda: v_.tensor_scalar(C1[:, :, :], C1[:, :, :], sgn, -1.0, MUL, MUL))
        V.do(lambda: v_.tensor_scalar(C2[:, :, :], C2[:, :, :], -1.0, None, MUL))
        V.do(lambda: v_.memset(PWr[:, 0, :], 1.0))
        V.do(lambda: v_.memset(PWi[:, 0, :], 0.0))
        V.do(lambda: v_.tensor_copy(PWr[:, 1, :], ar))
        V.do(lambda: v_.tensor_copy(PWi[:, 1, :], ai))
        p1 = t2[:, 0:4 * G].rearrange("p (a g) -> p a g", g=G)
        for k in (1, 2, 4):
            lr, li = PWr[:, 1:1 + k, :], PWi[:, 1:1 + k, :]
            hr, hi = bc(PWr[:, k, :], k), bc(PWi[:, k, :], k)
            orr, oi, s = PWr[:, 1 + k:1 + 2 * k, :], PWi[:, 1 + k:1 + 2 * k, :], p1[:, 0:k, :]
            for out, x, y, op in ((orr, hr, hi, SUB), (oi, hi, hr, ADD)):
                V.do(lambda: v_.tensor_tensor(s, li, y, MUL), V.now())
                V.do(lambda: v_.tensor_tensor(out, lr, x, MUL))
                V.do(lambda: v_.tensor_tensor(out, out, s, op), V.now())
        for h in range(2):
            V.do(lambda: v_.tensor_copy(A8r[:, h, :], PWr[:, SL, :]), V.now())
            V.do(lambda: v_.tensor_scalar(A8i[:, h, :], PWi[:, SL, :], sgn, 1.0 - 2 * h, MUL, MUL))
        RPr, RPi = tmp(SL, G), tmp(SL, G)
        US = small[:, 0:16 * SC].rearrange("p (g c) -> p g c", g=16)
        for s in range(SL):
            V.do(lambda: v_.tensor_copy(RPr[:, s, :], PWr[:, SL - 1 - s, :]))
            V.do(lambda: v_.tensor_scalar(RPi[:, s, :], PWi[:, SL - 1 - s, :], sgn, None, MUL))
        self.ada_at = 0
        self.ada_products(32, 0)
        V.do(lambda: v_.memset(TT[:, :, :], 0.0))
        V.do(lambda: v_.memset(ZZ[:, 0, :, :], 0.0))
        P_.wait(u_in)
        V.wait(u_in)
        self.bounds()

        KS = ABT

        def block(i):
            V.wait(ctl.last("pe"))
            Gq.wait(ctl.last("pe"))
            g16 = bass.ds(i * 16, 16)
            back = lambda pw: pw[:, :, g16].rearrange("p s g -> p g s").unsqueeze(3).broadcast_to(
                [P, 16, SL, GH])
            over = lambda b, n: b[:, g16, :].unsqueeze(2).broadcast_to([P, 16, n, GH])
            s2 = t2[:, 0:16 * SL * GH].rearrange("p (g s h) -> p g s h", g=16, s=SL)
            Gq.wait(V.now())
            y = Gq.do(lambda: nc.gpsimd.tensor_tensor(s2, back(RPi), over(B2, SL), MUL))
            V.do(lambda: v_.tensor_tensor(AB, back(RPr), over(B1, SL), MUL))
            ab = V.do(lambda: v_.tensor_tensor(AB, AB, s2, ADD), y, V.now())
            us = V.do(lambda: v_.tensor_copy(US[:, :, :], UP[:, g16, :]))
            P_.wait(ctl.last("k_read"))
            self.ada_at, ada = 0, lambda n: self.ada_products(n, i * 2 + 4, (6, 2))
            ada(8)
            P_.wait(ctl.last("row_read1"))
            P_.wait(us)
            for g in range(16):
                tr = P_.do(lambda: nc.tensor.transpose(
                    bank[g // 4][:, P * (g % 4):P * (g % 4 + 1)],
                    AB[:, g, :, :].rearrange("p s h -> p (s h)"), self.ident[:, :]), ab)
            A.wait(ctl.last("toeplitz"))
            for b in range(4):
                copy = lambda: nc.scalar.copy(ABT[:, 4 * b:4 * b + 4, :].rearrange("p g n -> p (g n)"),
                                              bank[b][:, :])
                abt = A.do(copy, tr)
            for g in range(16):
                u = US[:, g, :]
                o0, o1 = bank[0][:, 32 * g:32 * g + 32], bank[1][:, 32 * g:32 * g + 32]
                P_.quiet(self.mm(o0, ABT[:, g, :], u, True, True), abt)
                P_.quiet(self.mm(o1[0:64, :], ABT[:, g, 64:128], u, True, True))
                vm = P_.do(self.mm(o1[64:128, :], ABT[:, g, 0:64], u, True, True))
            for h in range(2):
                zo = ZZ[:, 1:SC, h, g16]
                vr = V.do(lambda: v_.tensor_copy(
                    zo, bank[h][:, :].rearrange("p (g c) -> p c g", g=16)[:, 0:SC - 1, :]), vm)
            ada(8)
            P_.wait(ctl.last("row_read0"))
            n = SL + 1
            s9 = t2[:, 0:16 * n * GH].rearrange("p (g s h) -> p g s h", g=16, s=n)
            pw = lambda p: p[:, :, g16].rearrange("p s g -> p g s").unsqueeze(3).broadcast_to(
                [P, 16, n, GH])
            y = Gq.do(lambda: nc.gpsimd.tensor_tensor(s9, pw(PWi), over(C2, n), MUL), ab)
            c = CA[:, g16, :, :]
            V.do(lambda: v_.tensor_tensor(c, pw(PWr), over(C1, n), MUL))
            bs = AB[:, 0:2, :, :].rearrange("p a s h -> p (a s) h")
            V.do(lambda: v_.tensor_copy(bs, B1[:, g16, :]), tr)
            ca = V.do(lambda: v_.tensor_tensor(c, c, s9, ADD), y, V.now())
            for g in range(16):
                rhs = CA[:, bass.ds(i * 16 + g, 1), 0:SL, :].rearrange("p a s h -> p (a s h)")
                km = P_.do(self.mm(bank[4 + g // 4][0:GH, P * (g % 4):P * (g % 4 + 1)],
                                   bs[:, g, :], rhs, True, True), ca)
            for b in range(4):
                copy = lambda: nc.scalar.copy(KS[0:GH, 4 * b:4 * b + 4, :]
                                              .rearrange("p g n -> p (g n)"), bank[4 + b][0:GH, :])
                ks = A.do(copy, km, vr)
            ctl.note("k_read", ks)
            ctl.note("pe", km)
            for s in range(SL):
                toe = self.moved.start(
                    A, TT[s * GH:(s + 1) * GH, g16, s * GH:P], KS[0:GH, :, 0:(SL - s) * GH], ks)
            ctl.note("toeplitz", toe)

        ctl.loop_over(4, [ENG.PE, ENG.DVE, ENG.Activation, ENG.Pool], block)
        self.bounds(P_, V)
        for q in (P_, A):
            q.wait(ctl.last("toeplitz"))

        def steps(i):
            for h in range(2):
                old, new = (ZZ[:, bass.ds(i * 2 + (1 + h + e), 1), :, :].rearrange("p a r g -> p (a r) g")
                            for e in range(2))
                V.do(lambda: v_.tensor_tensor(q1[:, :, :], old, A8r[:, :, :], MUL), V.now())
                for r in range(2):
                    V.do(lambda: v_.tensor_tensor(q2[:, r, :], old[:, 1 - r, :], A8i[:, r, :], MUL))
                V.do(lambda: v_.tensor_tensor(q1[:, :, :], q1[:, :, :], q2[:, :, :], ADD), V.now())
                V.do(lambda: v_.tensor_tensor(new, new, q1[:, :, :], ADD), V.now())

        ctl.loop_over((SC - 2) // 2, [ENG.DVE], steps)

        def meanwhile(i):
            self.ada_at = 0
            self.ada_products(16, i * 2 + 12)

        ctl.loop_over(4, [ENG.PE, ENG.Activation, ENG.Pool], meanwhile)
        P_.wait(V.now())
        YP = AB.rearrange("p g s h -> p (g s h)").rearrange("p (g c) -> p g c", g=G)
        for g in range(G):
            o = bank[g // 16][:, 32 * (g % 16):32 * (g % 16) + 32]
            P_.quiet(self.mm(o, TT[:, g, :], UP[:, g, :], True, False))
            ym = P_.do(self.mm(o, CA[:, g, 1:SL + 1, :].rearrange("p s h -> p (s h)"),
                               ZZ[:, 0:SC, 0, g], False, True))
            if g % 16 == 15:
                b = g // 16
                cp = A.do(lambda: nc.scalar.copy(YP[:, 16 * b:16 * b + 16, :]
                                                 .rearrange("p g c -> p (g c)"), bank[b][:, :]), ym)
        wrote = self.moved.start(A, sc2.rearrange("(p n) -> p n", p=P),
                                   YP.rearrange("p g c -> p (g c)"), cp)
        A.wait(wrote)
        YF = ABT.rearrange("p g n -> p (g n)").rearrange("p (m s c) -> p m s c", m=KT, s=SL)
        for s in range(SL):
            src = bass.AP(tensor=sc2.tensor, offset=s * GH * KT * T,
                          ap=[[SC, 8], [KT * T, GH], [T, KT], [1, SC]])
            back = self.moved.start(A, YF[:, :, s, :], src)
        yf = YF.rearrange("p m s c -> p m (s c)")
        uf = UF.rearrange("p m s c -> p m (s c)")
        V.wait(back)
        for k in range(KT):
            V.do(lambda: v_.scalar_tensor_tensor(yf[:, k, :], uf[:, k, :], self.col("ssm_d", k),
                                                 yf[:, k, :], MUL, ADD))
        ge = A.do(lambda: nc.scalar.activation(yf, yf, ACT.Gelu_apprx_tanh), V.now())
        P_.wait(ge)
        for c in range(4):
            w = self.take()
            for e in range(2):
                m = 2 * c + e
                o = bank[m][:, 0:T]
                done = self.product(o, w, KT, lambda k: yf[:, k, :], e * KT, e == 1)
                sg = uf[:, m, :]
                a = A.do(lambda: nc.scalar.activation(sg, o, ACT.Sigmoid, bias=self.col("b_glu", m)), done)
                V.do(lambda: v_.tensor_tensor(sg, sg, yf[:, m, :], MUL), a)
                V.do(lambda: v_.tensor_tensor(Zs[:, m, :], sg, Zs[:, m, :], MUL), V.now())
        self.bounds()

    def rwkv_layer(self, l):
        P_, V, A, Gq, nc, X, ctl, t = self.P, self.V, self.A, self.G, self.nc, self.H, self.ctl, self.t
        v_, s_, bank, tt = nc.vector, nc.scalar, self.bank, nc.vector.tensor_tensor
        keep = Arena(self.arena, self.arena_size)
        RKVZ, LD, AA, Y = keep(4, KT, T), keep(KT, T), keep(KT, T), X[:, :, T:2 * T]
        masks = keep(1280)
        tmp = Arena(self.arena, self.arena_size)
        tmp.at = keep.at
        dx, XS = tmp(KT, T), tmp(6, KT, T)
        gm = self.misc.start(Gq, masks, t["r_masks"][:, :])
        x = X[:, :, 0:T]
        V.do(lambda: tt(dx[:, :, 1:T], x[:, :, 0:T - 1], x[:, :, 1:T], SUB))
        V.do(lambda: v_.tensor_scalar(dx[:, :, 0:1], x[:, :, 0:1], -1.0, None, MUL))
        V.wait(V.now())
        mixed = {}
        for n in (4, 5, 0, 1, 2, 3):
            for k in range(KT):
                V.do(lambda: v_.scalar_tensor_tensor(XS[:, n, k, :], dx[:, k, :],
                                                     self.col("mu", 8 * n + k), x[:, k, :], MUL, ADD))
            mixed[n] = V.now()
        w = self.take()
        lw, la = bank[0][0:64, 0:T], bank[1][64:128, 0:T]
        hw, ha = tmp(T), tmp(T)
        P_.wait(mixed[5])
        for k in range(KT):
            P_.quiet(self.mm(lw, w[:, 64 * k:64 * k + 64], XS[:, 4, k, :], k == 0, k == KT - 1))
        for k in range(KT):
            mk = self.mm(la, w[:, 512 + 64 * k:576 + 64 * k], XS[:, 5, k, :], k == 0, k == KT - 1)
            m = P_.do(mk) if k == KT - 1 else P_.quiet(mk)
        A.do(lambda: s_.activation(hw[0:64, :], lw, ACT.Tanh), m)
        m = A.do(lambda: s_.copy(ha[64:128, :], la))
        P_.wait(m)
        for k in range(KT):
            for e, (h, dst, bias) in enumerate(((hw, LD, "w0"), (ha, AA, "a0"))):
                b, r = bank[(2 * k + e) % 8], slice(64 * e, 64 * e + 64)
                if k >= 4:
                    P_.wait(freed[2 * k + e - 8])
                mk = self.mm(b[:, 0:T], w[r, 1024 + P * k:1024 + P * (k + 1)], h[r, :], True, True)
                m = self.give(mk) if (k, e) == (KT - 1, 1) else P_.do(mk)
                m = A.do(lambda: s_.activation(dst[:, k, :], b[:, 0:T], ACT.Sigmoid,
                                               bias=self.col(bias, k)), m)
                freed = [m] if (k, e) == (0, 0) else freed + [m]
        V.do(lambda: v_.tensor_scalar(LD[:, :, :], LD[:, :, :], -float(np.exp(-0.5)), None, MUL), m)
        self.bounds(P_, A)

        def project(n):
            for c in range(4):
                w = self.take()
                for e in range(2):
                    m = 2 * c + e
                    P_.wait(ctl.last(f"b{m}"))
                    o = bank[m][:, 0:T]
                    done = self.product(
                        o, w, KT, lambda k: XS[:, bass.ds(n, 1), k, :].rearrange("p a t -> p (a t)"),
                        e * KT, e == 1)
                    dst = RKVZ[:, bass.ds(n, 1), m, :].rearrange("p a t -> p (a t)")
                    if e:
                        f = A.do(lambda: s_.copy(dst, o), done)
                    else:
                        f = V.do(lambda: v_.tensor_copy(dst, o), done)
                    ctl.note(f"b{m}", f)

        ctl.loop_over(4, [ENG.PE, ENG.DVE, ENG.Activation], project)
        for q in (P_, V, A, Gq):
            q.wait(gm)
        self.bounds()

        tmp = Arena(self.arena, self.arena_size)
        tmp.at = keep.at
        kk, kp, cu, wi, wv, wx, bt, kt, sq, O, OS, bo = (tmp(2, T) for _ in range(12))
        AR = tmp(2, 2, 2, P)
        NQ, AQ = tmp(8, 2 * P), tmp(8, 2 * P)
        NN, XX, XT, YY = (tmp(8, P) for _ in range(4))
        MMs = [tmp(8, P) for _ in range(2)]
        tok = tmp(4, 4, P)
        Vz = tmp(2, 4, P)
        Gs, XG, XA, SAz, SA = tmp(8, 64), tmp(8, 64), tmp(4, P), tmp(2, 2 * P), tmp(2, 2 * P)
        ST = tmp(2, P)
        mask2 = masks[:, 0:256]
        mN, m0, m0T = (masks[:, 256 + P * k:384 + P * k] for k in range(3))
        level = [masks[:, 640 + P * k:768 + P * k] for k in range(5)]
        Z0 = V.do(lambda: v_.memset(SAz[:, :, :], 0.0))
        V.wait(Z0)

        def heads(i):
            two = bass.ds(i * 2, 2)
            self.ada_at, ada = 0, lambda n: self.ada_products(n, i * 4 + ADA_SSM)
            r, k, v, z = (RKVZ[:, n, two, :] for n in range(4))
            a, ld = AA[:, two, :], LD[:, two, :]
            flat = lambda ap: ap.rearrange("p j t -> p (j t)")
            V.do(lambda: v_.memset(ST[:, :, :], 0.0), ctl.last("end_p"))
            for j in range(2):
                kj = RKVZ[:, 1, bass.ds(i * 2 + j, 1), :].rearrange("p a t -> p (a t)")
                aj = AA[:, bass.ds(i * 2 + j, 1), :].rearrange("p a t -> p (a t)")
                V.do(lambda: v_.tensor_scalar(kk[:, j, :], kj, self.col("k_k", i * 2 + j), None, MUL),
                     ctl.last("end_p"), ctl.last("end_a"), ctl.last("end_g"))
                V.do(lambda: v_.tensor_scalar(kp[:, j, :], aj, -1.0, self.col("k_a", i * 2 + j), ADD, MUL))
            s = A.do(lambda: s_.activation(sq[:, :, :], kk[:, :, :], ACT.Square), V.now(), ctl.last("end_v"))
            V.do(lambda: v_.scalar_tensor_tensor(kp[:, :, :], kp[:, :, :], 1.0, k, ADD, MUL), V.now())
            P_.wait(ctl.last("norm_read"))
            ada(8)
            m = P_.do(self.mm(bank[7][:, :], self.blk64[:, :], flat(sq), True, True), s, ctl.last("end_v"))
            m = A.do(lambda: s_.activation(flat(sq), bank[7][:, :], ACT.Sqrt), m)
            P_.wait(m)
            ada(8)
            V.do(lambda: v_.tensor_copy(cu[:, :, :], ld))
            for lv in range(6):
                h = 1 << lv
                c = flat(cu).rearrange("p (b two h) -> p b two h", two=2, h=h)
                carry = c[:, :, 0, h - 1:h].broadcast_to([P, 2 * T // (2 * h), h])
                V.do(lambda: tt(c[:, :, 1, :], c[:, :, 1, :], carry, ADD), V.now())
            e1 = A.do(lambda: s_.activation(wi[:, :, :], cu[:, :, :], ACT.Exp), V.now())
            e2 = A.do(lambda: s_.activation(wv[:, :, :], cu[:, :, :], ACT.Exp, scale=-1.0))
            V.do(lambda: tt(wx[:, :, :], cu[:, :, :], ld, SUB), V.now())
            e3 = A.do(lambda: s_.activation(wx[:, :, :], wx[:, :, :], ACT.Exp), V.now())
            V.do(lambda: v_.tensor_scalar(sq[:, :, :], sq[:, :, :], 1e-12, None, MAX), m)
            V.do(lambda: v_.reciprocal(sq[:, :, :], sq[:, :, :]), V.now())
            V.do(lambda: tt(kk[:, :, :], kk[:, :, :], sq[:, :, :], MUL), V.now())
            ar = lambda which: AR[:, :, :, which, :].rearrange("p j b t -> p (j b) t")
            at4 = lambda ap: ap.rearrange("p j (b t) -> p (j b) t", t=P)
            V.do(lambda: tt(kt[:, :, :], kp[:, :, :], wv[:, :, :], MUL), e2)
            V.do(lambda: tt(ar(1), at4(r), at4(wi), MUL), e1)
            V.do(lambda: tt(bt[:, :, :], kk[:, :, :], a, MUL), V.now())
            V.do(lambda: v_.scalar_tensor_tensor(ar(0), at4(kk), -1.0, at4(wx), MUL, MUL), e3)
            pre = V.do(lambda: tt(bt[:, :, :], bt[:, :, :], wv[:, :, :], MUL), V.now())
            for j in range(2):
                if j:
                    P_.wait(masked)
                for e in range(2):
                    rows = slice(64 * e, 64 * e + 64)
                    for tb in range(2):
                        tk = slice(P * tb, P * tb + P)
                        both = AR[rows, j, tb, :, :].rearrange("p w t -> p (w t)")
                        half = slice(256 * tb, 256 * tb + 256)
                        P_.quiet(self.mm(bank[2 * e][:, half], bt[rows, j, tk], both, True, True), pre)
                        P_.quiet(self.mm(bank[2 * e + 1][:, half], kt[rows, j, tk], both, True, True))
                        m = P_.do(self.mm(bank[4 + e][:, tk], AR[rows, j, tb, 0, :], bt[rows, j, tk],
                                          True, True))
                for e in range(2):
                    u = slice(4 * j + 2 * e, 4 * j + 2 * e + 2)
                    q = lambda b: b[:, :].rearrange("p (b t) -> p b t", b=2)
                    V.do(lambda: tt(NQ[:, u, :], q(bank[2 * e]), bc(mask2, 2), MUL), m)
                    V.do(lambda: tt(AQ[:, u, :], q(bank[2 * e + 1]), bc(mask2, 2), MUL))
                    masked = V.do(lambda: tt(NN[:, u, :], bank[4 + e][:, 0:256]
                                             .rearrange("p (b t) -> p b t", b=2), bc(mN, 2), MUL))
            P_.wait(masked)
            for n in range(4):
                for jb in range(4):
                    j, tk = jb // 2, slice(P * (jb % 2), P * (jb % 2) + P)
                    if n == 0:
                        src = RKVZ[:, 2, bass.ds(i * 2 + j, 1), tk].rearrange("p a t -> p (a t)")
                        src = self.stage_v(src, O[:, j, tk])
                    else:
                        src = (bt[:, j, tk], kt[:, j, tk], AR[:, j, jb % 2, 0, :])[n - 1]
                    m = P_.do(lambda: nc.tensor.transpose(bank[n][:, P * jb:P * jb + P], src,
                                                          self.ident[:, :]))
            for n in range(4):
                cp = A.do(lambda: s_.copy(tok[:, n, :, :].rearrange("p a b -> p (a b)"), bank[n][:, :]), m)
            P_.wait(cp)
            NT = NQ[:, :, 0:P]
            V.do(lambda: tt(XX[:, :, :], NN[:, :, :], bc(m0, 8), MUL), V.now())
            V.do(lambda: tt(XT[:, :, :], NT, bc(m0T, 8), MUL))
            V.do(lambda: tt(XX[:, :, :], XX[:, :, :], bc(self.ident[:, :], 8), ADD), V.now())
            xx = V.do(lambda: tt(XT[:, :, :], XT[:, :, :], bc(self.ident[:, :], 8), ADD))
            join = lambda lv, after: Gq.do(lambda: nc.gpsimd.tensor_tensor(
                MMs[lv % 2][:, :, :], NT, bc(level[lv], 8), MUL), masked, after)
            p1, xt, joins = None, xx, join(0, None)
            for lv in range(5):
                MM = MMs[lv % 2]
                P_.wait(joins)
                if lv < 4:
                    joins = join(lv + 1, p1)
                P_.wait(xx)
                for u in range(8):
                    p1 = P_.do(self.mm(bank[4 + u // 4][:, P * (u % 4):P * (u % 4) + P], MM[:, u, :],
                                       XX[:, u, :], True, True))
                ada(2 if lv < 4 else 0)
                for b in range(2):
                    y = A.do(lambda: s_.copy(YY[:, 4 * b:4 * b + 4, :].rearrange("p u t -> p (u t)"),
                                             bank[4 + b][:, :]), p1)
                P_.wait(y)
                mx = None
                P_.wait(xt)
                if lv < 4:
                    for u in range(8):
                        c = slice(P * (u % 4), P * (u % 4) + P)
                        mx = P_.do(self.mm(bank[2 + u // 4][:, c], XT[:, u, :], YY[:, u, :], True, True))
                for u in range(8):
                    c = slice(P * (u % 4), P * (u % 4) + P)
                    m = P_.do(self.mm(bank[u // 4][:, c], YY[:, u, :], XT[:, u, :], True, True))
                ada(2 if lv < 4 else 0)
                for out, first, mark in (((XX, 2, mx),) if lv < 4 else ()) + ((XT, 0, m),):
                    for b in range(2):
                        u4 = slice(4 * b, 4 * b + 4)
                        xt = V.do(lambda: tt(out[:, u4, :], out[:, u4, :],
                                             bank[first + b][:, :].rearrange("p (u t) -> p u t", u=4), ADD),
                                  mark)
                    if out is XX:
                        xx = xt
            xx = xt
            unit = lambda u: (u // 4, (u // 2) % 2, u % 2)
            for u in range(8):
                j, e, tb = unit(u)
                m = P_.do(self.mm(bank[4][:, 64 * u:64 * u + 64], AQ[:, u, 0:P],
                                  tok[:, 0, 2 * j + tb, 64 * e:64 * e + 64], True, True))
            g = A.do(lambda: s_.copy(Gs.rearrange("p u v -> p (u v)"), bank[4][:, :]), m)
            for h in range(2):
                vz = A.do(lambda: s_.activation(Vz[:, h, :, :], tok[:, 0, :, :], ACT.Copy,
                                                scale=self.col("half", h)), cp)
            P_.wait(xx)
            for u in range(8):
                j, e, tb = unit(u)
                P_.quiet(self.mm(bank[6][64 * e:64 * e + 64, P * (2 * j + tb):P * (2 * j + tb) + P],
                                 tok[:, 3, 2 * j + tb, 64 * e:64 * e + 64], XT[:, u, :], True, True))
            P_.wait(g)
            for u in range(8):
                m = P_.do(self.mm(bank[5][:, 64 * u:64 * u + 64], XT[:, u, :], Gs[:, u, :], True, True))
            xa = A.do(lambda: s_.copy(XA.rearrange("p u t -> p (u t)"), bank[6][:, :]), m)
            V.do(lambda: v_.tensor_copy(XG.rearrange("p u v -> p (u v)"), bank[5][:, :]), m)
            P_.wait(xa)
            P_.wait(vz)
            for b in range(2):
                P_.wait(ctl.last(f"row_read{b}"))
            xgb = XG.rearrange("p (je tb) v -> p tb je v", tb=2)
            st, os_, copied = V.now(), None, [None, None]
            for c in range(4):
                tb, h = c // 2, c % 2
                rows, bk = slice(64 * h, 64 * h + 64), bank[4 + (c % 2)]
                saz = SAz[rows, h, :].rearrange("p (je v) -> p je v", je=4)
                xg = xgb[rows, tb, :, :]
                P_.wait(st)
                if c:
                    for j in range(2):
                        m = P_.do(self.mm(bk[rows, P * j:P * j + P], XA[:, 2 * j + tb, rows], ST[:, j, :],
                                          True, True))
                    sa = V.do(lambda: tt(saz, xg, bk[rows, 0:2 * P].rearrange("p (je v) -> p je v", je=4),
                                         ADD), m, copied[h])
                    P_.wait(os_)
                    for j in range(2):
                        m = P_.do(self.mm(bank[7][:, P * j + 0:P * j + 64], ST[:, j, :],
                                          AR[:, j, tb, 1, rows], True, True))
                    os_ = A.do(lambda: s_.copy(
                        OS[:, :, 64 * c:64 * c + 64],
                        bank[7][:, 0:2 * P].rearrange("p (j t) -> p j t", j=2)[:, :, 0:64]), m)
                else:
                    sa = V.do(lambda: v_.tensor_copy(saz, xg), V.now(), ctl.last("end_p"))
                    V.do(lambda: v_.memset(OS[:, :, 0:64], 0.0))
                both = copied[h] = A.do(lambda: s_.copy(SA[rows, tb, :], SAz[rows, h, :]), sa)
                if c < 3:
                    P_.wait(sa)
                    for j in range(2):
                        o = bank[6][:, P * j:P * j + P]
                        P_.quiet(self.mm(o, self.ident[:, :], ST[:, j, :], True, False))
                        P_.quiet(self.mm(o, tok[:, 1, 2 * j + tb, :], SAz[:, h, P * j:P * j + P],
                                         False, False))
                        m = P_.do(self.mm(o, tok[:, 2, 2 * j + tb, :], Vz[:, h, 2 * j + tb, :],
                                          False, True))
                    for j in range(2):
                        for e in range(2):
                            rw = slice(64 * e, 64 * e + 64)
                            st = V.do(lambda: v_.tensor_scalar(
                                ST[rw, j, 64 * e:64 * e + 64], bank[6][rw, P * j + 64 * e:P * j + 64 * e + 64],
                                wi[rw, j, 64 * c + 63:64 * c + 64], None, MUL), m)
            P_.wait(both)
            for u in range(8):
                j, e, tb = unit(u)
                o = bank[u // 4][64 * e:64 * e + 64, P * (2 * (u // 4 - u // 4) + tb):P * tb + P]
                P_.quiet(self.mm(o, SA[:, tb, P * j + 64 * e:P * j + 64 * e + 64], NQ[:, u, P:2 * P],
                                 True, False))
                m = P_.do(self.mm(o, tok[:, 0, 2 * j + tb, 64 * e:64 * e + 64], AQ[:, u, P:2 * P],
                                  False, True))
            for j in range(2):
                V.do(lambda: tt(O[:, j, :], OS[:, j, :], bank[j][:, 0:T], ADD), m, os_)
            m = P_.do(self.mm(bank[4][:, :], self.blk64[:, :], flat(O), True, True), V.now())
            V.do(lambda: tt(bo[:, :, :], r, kp[:, :, :], MUL))
            for j in range(2):
                V.do(lambda: v_.tensor_scalar(bo[:, j, :], bo[:, j, :], self.col("r_k", i * 2 + j), None, MUL),
                     V.now())
            mb = P_.do(self.mm(bank[5][:, :], self.blk64[:, :], flat(bo), True, True), V.now())
            V.do(lambda: v_.scalar_tensor_tensor(flat(O), bank[4][:, :], -1.0 / 64, flat(O), MUL, ADD), m)
            s = A.do(lambda: s_.activation(sq[:, :, :], O[:, :, :], ACT.Square), V.now())
            m = P_.do(self.mm(bank[6][:, :], self.blk64[:, :], flat(sq), True, True), s)
            rs = flat(wx)
            ctl.note("norm_read", self.rstd(rs, bank[6][:, :], 1.0 / 64, GN_EPS, m))
            V.do(lambda: tt(flat(O), flat(O), rs, MUL), V.now())
            for j in range(2):
                V.do(lambda: v_.tensor_scalar(O[:, j, :], O[:, j, :], self.col("lnx_g", i * 2 + j),
                                              self.col("lnx_b", i * 2 + j), MUL, ADD), V.now())
            V.do(lambda: tt(bo[:, :, :], v, bank[5][:, :].rearrange("p (j t) -> p j t", j=2), MUL), mb)
            V.do(lambda: tt(O[:, :, :], O[:, :, :], bo[:, :, :], ADD), V.now())
            sz = A.do(lambda: s_.activation(OS[:, :, :], z, ACT.Silu), V.now())
            f = V.do(lambda: tt(Y[:, two, :], O[:, :, :], OS[:, :, :], MUL), sz)
            ctl.note("end_v", f)
            ctl.note("end_a", A.now())
            ctl.note("end_p", P_.now())
            ctl.note("end_g", Gq.now())

        ctl.loop_over(4, [ENG.PE, ENG.DVE, ENG.Activation, ENG.Pool], heads)
        self.bounds()

    def stage_v(self, src, dst):
        m = self.V.do(lambda: self.nc.vector.tensor_copy(dst, src))
        self.P.wait(m)
        return dst


    def ada_products(self, count, group, banks=(6, 7)):
        P_, ctl = self.P, self.ctl
        for u in range(self.ada_at, self.ada_at + count):
            g, k, b = u // 8, u % 8, u // 8 % 2
            out, row = self.bank[banks[b]][0:2, :], self.row[0:2, :]
            if k % 4 == 0:
                self.ada_w = self.take()
            if k == 0:
                P_.wait(ctl.last(f"row_read{b}"))
            make = self.mm(out, self.cond[:, k, :], self.ada_w[:, 512 * (k % 4):512 * (k % 4) + 512],
                           k == 0, k == 7)
            m = self.give(make) if k % 4 == 3 else P_.quiet(make)
            if k == 7:
                m = self.A.do(lambda: self.nc.scalar.copy(row, out), m, ctl.last("row_sent"))
                ctl.note(f"row_read{b}", m)
                ctl.note("row_sent", self.sent.start(
                    self.G, self.t["mods"][:, bass.ds((group + g) * 512, 512)], row, m))
        self.ada_at += count

    def ada(self):
        P_, V, A, G_, nc, ctl = self.P, self.V, self.A, self.G, self.nc, self.ctl
        v_ = nc.vector
        tmp = Arena(self.arena, self.arena_size)
        tiles = DEPTH2 * 9 * KT
        most, rest = tmp(2, P), tmp(2, P)
        self.misc.start(G_, self.H[:, :, T:2 * T], self.t["ctx"])
        G_.wait(ctl.last("row_sent"))
        mods = self.t["mods"]
        for n in range(2):
            self.misc.start(G_, most[:, n, :], mods[n, 0:P * P].rearrange("(m f) -> m f", f=P))
            got = self.misc.start(G_, rest[0:tiles - P, n, :],
                                  mods[n, P * P:tiles * P].rearrange("(m f) -> m f", f=P))
        for q in (V, P_, A):
            q.wait(got)
        m = self.mod[:, :].rearrange("p (m n) -> p n m", n=2)
        for b, (src, at, rows) in enumerate(((most, 0, P), (rest, P, tiles - P))):
            for n in range(2):
                tr = P_.do(lambda: nc.tensor.transpose(self.bank[b][:, rows * n:rows * n + rows],
                                                       src[0:rows, n, :], self.ident[0:rows, 0:rows]))
            bias = bc(self.cols[:, COLS["ada_b"] + at:COLS["ada_b"] + at + rows], 2)
            V.do(lambda: v_.tensor_tensor(m[:, :, at:at + rows], self.bank[b][:, 0:2 * rows].rearrange(
                "p (n m) -> p n m", n=2), bias, ADD), tr)
        m5 = self.mod[:, :].rearrange("p (l w k n) -> p l w k n", l=DEPTH2, w=9, k=KT)
        V.wait(V.now())
        for l in range(DEPTH2):
            for s in range(3):
                at = COLS["norm_g"] + KT * (3 * l + s)
                g = bc_in(self.cols[:, at:at + KT], 2)
                sl = m5[:, l, 3 * s + 1, :, :]
                V.do(lambda: v_.scalar_tensor_tensor(sl, sl, 1.0, g, ADD, MUL))
                if s != 1:
                    gt = m5[:, l, 3 * s + 2, :, :]
                    V.do(lambda: v_.tensor_scalar(gt, gt, 0.5, None, MUL))
        self.bounds()

    def mod_col(self, l, which, k, n):
        return self.mod[:, bass.ds((k * 2) + ((l * 9 + which) * KT * 2 + n), 1)]

    def modulated_split(self, l, s, nt, act, rs):
        P_, V, A, nc, H = self.P, self.V, self.A, self.nc, self.H
        x_hi, x_lo = self.box["x_hi"], self.box["x_lo"]
        free = [None] * 4
        for k in range(KT):
            sq, h = act[:, k % 4, 0:nt], H[:, k, 0:nt]
            m = V.do(lambda: nc.vector.tensor_tensor(sq, h, h, MUL), free[k % 4]) if k % 2 else \
                A.do(lambda: nc.scalar.activation(sq, h, ACT.Square), free[k % 4])
            m = free[k % 4] = P_.do(self.mm(self.bank[0][:, 0:nt], self.ones[:, :], sq,
                                            k == 0, k == KT - 1), m)
        m = self.rstd(rs, self.bank[0][:, 0:nt], 1.0 / D, RMS_EPS, m)
        V.wait(m)
        lo, read = [None] * 4, {}
        for k in range(KT):
            for n in range(nt // T):
                half, y = slice(n * T, n * T + T), act[:, k % 4, n * T:n * T + T]
                scale, shift = (self.mod_col(l, 3 * s + w, k, n) for w in (1, 0))
                m = V.do(lambda: nc.vector.scalar_tensor_tensor(y, H[:, k, half], scale, rs[:, half],
                                                                MUL, MUL), read.get((k - 4, n)))
                hi = A.do(lambda: nc.scalar.activation(fr(x_hi[:, k, half]), y, ACT.Identity, bias=shift), m)
                lo = lo[1:] + [(y, shift, k, half, hi)]
                if lo[0]:
                    read[lo[0][2], lo[0][3].start // T] = self.rest_of(x_hi, x_lo, *lo[0])
        for part in lo[1:]:
            self.rest_of(x_hi, x_lo, *part)
        lo = [None, V.now()]
        P_.wait(lo[1])
        V.wait(A.now())
        A.wait(V.now())

    def gated_sum(self, o, l, which, m, nt, done):
        for n in range(nt // T):
            h = self.H[:, bass.ds(m, 1), n * T:n * T + T].rearrange("p a t -> p (a t)")
            f = self.V.do(lambda: self.nc.vector.scalar_tensor_tensor(
                h, o[:, n * T:n * T + T], self.mod_col(l, which, m, n), h, MUL, ADD), done)
        return f

    def rest_of(self, x_hi, x_lo, y, shift, k, half, hi):
        return self.V.do(lambda: self.nc.vector.scalar_tensor_tensor(
            fr(x_lo[:, k, half]), y, shift, x_hi[:, k, half], ADD, SUB), hi)

    def ffn(self, l, s):
        P_, V, A, nc, ctl = self.P, self.V, self.A, self.nc, self.ctl
        nt = T if (l, s) == (DEPTH2 - 1, 1) else 2 * T
        x_hi, x_lo, u_hi, u_lo = (self.box[n] for n in ("x_hi", "x_lo", "u_hi", "u_lo"))
        tmp = Arena(self.arena, self.arena_size)
        rs, ut, act = tmp(nt), tmp(2, 2 * T), tmp(4, 2 * T)
        up, dn = (KT, KT), ((FT // 2 + 1) // 2, FT // 2 // 2)
        first = self.split_part(0, up, 0)
        self.modulated_split(l, 2 * s, nt, act, rs)
        halves = lambda hi, lo, k: (hi[:, k, 0:nt], lo[:, k, 0:nt])

        def pair(m, j):
            P_.wait(ctl.last(f"u{j}"))
            a, b = self.bank[2 * j][:, 0:nt], self.bank[2 * j + 1][:, 0:nt]
            self.split_part(0, up, 1)
            self.product_split(a, 0, KT, lambda k: halves(x_hi, x_lo, k))
            am = P_.now()
            self.split_part(1, up if m is not last else dn, 0)
            done = self.product_split(b, 1, KT, lambda k: halves(x_hi, x_lo, k))
            g = A.do(lambda: nc.scalar.activation(act[:, j, 0:nt], a, ACT.Silu), am, ctl.last(f"u{j}"))
            u, e = ut[:, j % 2, 0:nt], j % 2
            uh, ul = (y[:, bass.ds(m, 1), 0:nt].rearrange("p a t -> p (a t)") for y in (u_hi, u_lo))
            f = V.do(lambda: nc.vector.tensor_tensor(u, act[:, j, 0:nt], b, MUL), g, done)
            ctl.note(f"u{j}", f)
            f = V.do(lambda: nc.vector.tensor_copy(fr(uh), u), f)
            return V.do(lambda: nc.vector.tensor_tensor(fr(ul), u, uh, SUB), f)

        full, last = FT // NS, None
        P_.wait(first)
        ctl.loop_over(full, [ENG.PE, ENG.DVE, ENG.Activation],
                      lambda i: [pair(i * NS + j, j) for j in range(NS)])
        for j in range(FT % NS):
            tile = full * NS + j
            last = tile if tile == FT - 1 else None
            m = pair(tile, j)
        P_.wait(m)
        A.wait(self.freed())

        def down(i, end=False):
            for j in range(2):
                P_.wait(ctl.last(f"d{j}"))
                o = self.bank[j][:, 0:nt]
                for c in range(2):
                    u = lambda k: halves(u_hi, u_lo, c * (FT // 2) + k)
                    self.split_part(0, dn, 1)
                    self.product_split(o, 0, dn[0], u, c == 0, False)
                    if not (end and j == c == 1):
                        self.split_part(1, dn, 0)
                    done = self.product_split(o, 1, dn[1], lambda k: u(dn[0] + k), False, c == 1)
                ctl.note(f"d{j}", self.gated_sum(o, l, 6 * s + 2, i * 2 + j, nt, done))

        ctl.loop_over(KT // 2 - 1, [ENG.PE, ENG.DVE, ENG.Activation], down)
        P_.wait(V.now())
        A.wait(self.freed())
        down(KT // 2 - 1, True)
        self.bounds()

    def softmax_units(self, units, scale, sc, on_pair):
        P_, V, A, nc = self.P, self.V, self.A, self.nc
        v_, s_ = nc.vector, nc.scalar
        ctl = self.ctl
        pr, pt, st, sb = sc

        def scores(n):
            qs, ks, nk, _, _, bias, _ = units[n]
            d = n % 2
            b = self.bank[d]
            P_.wait(ctl.last(f"s{d}"))
            for c, (q, k) in enumerate(zip(qs, ks)):
                mk = self.mm(b[:, 0:nk], q, k, c == 0, c == len(qs) - 1)
                m = P_.do(mk) if c == len(qs) - 1 else P_.quiet(mk)
            mx, ng, sm, rc = (st[:, d, k:k + 1] for k in range(4))
            src, sscale = b[:, 0:nk], scale
            V.wait(ctl.last(f"p{d}"))
            if bias is not None:
                V.do(lambda: v_.scalar_tensor_tensor(sb[:, d, 0:T], b[:, 0:T], scale, bias, MUL, ADD), m)
                V.do(lambda: v_.tensor_scalar(sb[:, d, T:nk], b[:, T:nk], scale, None, MUL))
                ctl.note(f"s{d}", V.now())
                src, sscale = sb[:, d, 0:nk], 1.0
            V.do(lambda: v_.reduce_max(mx, src, AX), m, V.now() if bias is not None else None)
            m = V.do(lambda: v_.tensor_scalar(ng, mx, -sscale, None, MUL), V.now())
            A.wait(ctl.last(f"t{d}"))
            m = A.do(lambda: s_.activation(pr[:, d, 0:nk], src, ACT.Exp, bias=ng, scale=sscale,
                                           accum_out=sm), m)
            if bias is None:
                ctl.note(f"s{d}", m)
            return m

        def divided(n, m):
            nk, d = units[n][2], n % 2
            sm, rc = st[:, d, 2:3], st[:, d, 3:4]
            V.do(lambda: v_.reciprocal(rc, sm), m)
            return V.do(lambda: v_.tensor_scalar(pr[:, d, 0:nk], pr[:, d, 0:nk], rc, None, MUL), V.now())

        def probabilities(n, m):
            nk, d = units[n][2], n % 2
            tb = self.bank[2 + d]
            P_.wait(ctl.last(f"e{d}"))
            P_.wait(m)
            for k in range(nk // P):
                m = P_.do(lambda: nc.tensor.transpose(tb[:, P * k:P * k + P], pr[:, d, P * k:P * k + P],
                                                      self.ident[:, :]))
            ctl.note(f"t{d}", m)
            ctl.note(f"p{d}", m)
            A.wait(ctl.last(f"o{d}"))
            m = A.do(lambda: s_.copy(pt[:, d, 0:nk], tb[:, 0:nk]), m)
            ctl.note(f"e{d}", m)
            return m

        def values(n, m):
            _, _, nk, vs, out, _, close = units[n]
            d, nb = n % 2, nk // P
            P_.wait(m)
            if close and close[0] == "first":
                P_.wait(ctl.last(f"pair{close[1]}"))
            for k in range(nb):
                m = P_.do(self.mm(out, vs[k], pt[:, d, P * k:P * k + P], k == 0, k == nb - 1))
            ctl.note(f"o{d}", m)
            if close and close[0] == "last":
                on_pair(close[1], m)

        done = {}
        for n in range(len(units) + 2):
            if 0 <= n - 1 < len(units):
                done[n - 1] = divided(n - 1, done[n - 1])
            if n < len(units):
                done[n] = scores(n)
            if 0 <= n - 1 < len(units):
                done[n - 1] = probabilities(n - 1, done[n - 1])
            if 0 <= n - 2:
                values(n - 2, done[n - 2])

    def headnorms(self, nt, squares, outs, scale, con, rs, rot, after):
        P_, V, A, nc, v_ = self.P, self.V, self.A, self.nc, self.nc.vector
        sel, back = con[:, 0:NSEL * ROWS], con[:, NSEL * ROWS:NSEL * (ROWS + P)]
        for k, (t, sq) in enumerate(squares):
            mk = self.mm(self.bank[4][0:ROWS, 0:nt], sel[:, ROWS * t:ROWS * t + ROWS], sq,
                         k == 0, k == len(squares) - 1)
            m = P_.do(mk, after) if k == len(squares) - 1 else P_.quiet(mk, after)
        rs = rs[0:ROWS, 0:nt]
        m = self.rstd(rs, self.bank[4][0:ROWS, 0:nt], scale, RMS_EPS, m)
        free, turned = [None] * 3, [None] * 2

        def bring(i):
            b, t = self.bank[i % 3][:, 0:nt], outs[i][0]
            return P_.do(self.mm(b, back[0:ROWS, P * t:P * t + P], rs, True, True), m, free[i % 3])

        def turn(i, tm):
            _, _, _, dst, (_, cos, sin), _ = outs[i]
            r = rot[i % 2][:, 0:T]
            turned[i % 2] = V.do(lambda: v_.tensor_tensor(r, self.bank[5 + i % 2][:, 0:T], sin, MUL), tm)
            V.do(lambda: v_.tensor_tensor(dst[:, 0:T], dst[:, 0:T], cos, MUL))
            V.do(lambda: v_.tensor_tensor(dst[:, 0:T], dst[:, 0:T], r, ADD), V.now())

        here, late = bring(0), None
        for i, (t, tile, gain, dst, rope, then) in enumerate(outs):
            there = bring(i + 1) if i + 1 < len(outs) else None
            b = self.bank[i % 3][:, 0:nt]
            f = free[i % 3] = V.do(lambda: v_.scalar_tensor_tensor(dst, tile, gain, b, MUL, MUL), here)
            if then:
                then(f)
            if rope:
                tm = P_.do(self.mm(self.bank[5 + i % 2][:, 0:T], rope[0], dst[:, 0:T], True, True),
                           f, turned[i % 2])
            if late:
                turn(*late)
            late, here = (i, tm) if rope else None, there
        if late:
            turn(*late)

    def mixer_ab(self):
        P_, V, A, nc, ctl, t = self.P, self.V, self.A, self.nc, self.ctl, self.t
        v_, s_ = nc.vector, nc.scalar
        N = 2 * T
        tmp = Arena(self.arena, self.arena_size)
        att = tmp(KT, N)
        AQ, AK, BQN, BQR, KV, KR = (tmp(n, N) for n in (4, 1, 4, 2, 2, 1))
        BKN, BKR = tmp(4, N), tmp(2, N)
        AV, BV = tmp(4, P), tmp(4, 512)
        con, sel = tmp(128 * 2 + 4 * T), tmp(NSEL * (ROWS + P) + 1)
        nt2, rs = [tmp(N) for _ in range(2)], tmp(N)
        self.misc.start(self.G, con, t["ab_consts"][:, :])
        got = self.misc.start(self.G, sel, t["selectors"][:, :])
        RA, RB = (con[:, P * k:P * k + P] for k in range(2))
        cosA, sinA, cosB, sinB = (con[:, 256 + T * k:256 + T * k + T] for k in range(4))
        tiles_ = [AQ[:, k, :] for k in range(4)] + [AK[:, 0, :]] + [BQN[:, k, :] for k in range(4)] + \
            [BQR[:, k, :] for k in range(2)] + [KV[:, k, :] for k in range(2)] + [KR[:, 0, :]]
        with self.scope(**self.IN_BOXES):
            act = Arena(self.arena, self.arena_size)(4, N)
            up, x_at = self.EIGHTS, self.halves("x")
            self.split_part(0, up, 0)
            self.modulated_split(0, 1, N, act, rs)
            free = [None] * 8
            for m in range(14):
                b, e = m % 8, m % 2
                P_.wait(free[b])
                self.split_part(e, up, 1 - e)
                done = self.product_split(self.bank[b][:, :], e, KT, x_at)
                q = V if e else A
                cp = (lambda: v_.tensor_copy(tiles_[m], self.bank[b][:, :])) if e else \
                    (lambda: s_.copy(tiles_[m], self.bank[b][:, :]))
                free[b] = q.do(cp, done)
            P_.wait(free[6])
            m = self.values_split(0, KT, lambda tb: self.bank[6][:, P * tb:P * tb + P],
                                  lambda k, tb: (a[:, P * tb:P * tb + P] for a in x_at(k)), True, True, True)
            A.do(lambda: s_.copy(AV.rearrange("p a b -> p (a b)"), self.bank[6][:, :]), m)
            for q in (V, P_, A):
                q.wait(got)
            self.bounds()
        with self.scope():
            self.attention_ab(att, (AQ, AK, BQN, BQR, KV, KR, BKN, BKR, AV, BV), sel, rs, nt2,
                              (RA, RB, cosA, sinA, cosB, sinB))
        self.mixer_out(0, att, N)

    def attention_ab(self, att, tiles, sel, rs, nt2, turns):
        P_, V, A, nc, ctl = self.P, self.V, self.A, self.nc, self.ctl
        v_, s_, N = nc.vector, nc.scalar, 2 * T
        AQ, AK, BQN, BQR, KV, KR, BKN, BKR, AV, BV = tiles
        RA, RB, cosA, sinA, cosB, sinB = turns
        tmp = Arena(self.arena, self.arena_size)
        S = tmp(2 * KT, N)
        m = A.do(lambda: s_.activation(S[:, 0:2, :], KV[:, :, :], ACT.Square))
        m2 = self.colsum(self.bank[4][:, :], lambda k: S[:, k, :], 2, after=[m])
        m2 = self.rstd(rs, self.bank[4][:, :], 1.0 / 256, RMS_EPS, m2)
        for k in range(2):
            m2 = V.do(lambda: v_.scalar_tensor_tensor(KV[:, k, :], KV[:, k, :], self.col("kvn", k), rs,
                                                      MUL, MUL), m2)
        for k, src in ((2, AQ), (6, AK), (7, BQN), (11, BQR), (13, KR)):
            A.do(lambda: s_.activation(S[:, k:k + src.shape[1], :], src[:, :, :], ACT.Square))
        w = self.take()
        P_.wait(m2)
        for k in range(4):
            b = self.bank[k]
            for c in range(2):
                mk = self.mm(b[:, :], w[:, P * (2 * k + c):P * (2 * k + c + 1)], KV[:, c, :],
                             c == 0, c == 1)
                m3 = P_.do(mk) if c else P_.quiet(mk)
            A.do(lambda: s_.copy(BKN[:, k, :], b[:, :]), m3)
        P_.wait(A.now())
        for tb in range(4):
            for c in range(2):
                mk = self.mm(self.bank[tb][:, :], KV[:, c, P * tb:P * tb + P],
                             w[:, 1024 + 512 * c:1536 + 512 * c], c == 0, c == 1)
                if (tb, c) == (3, 1):
                    m3 = self.give(mk)
                else:
                    m3 = P_.do(mk) if c else P_.quiet(mk)
            V.do(lambda: v_.tensor_copy(BV[:, tb, :], self.bank[tb][:, :]), m3)
        A.do(lambda: s_.activation(S[:, 14:16, :], BKN[:, 0:2, :], ACT.Square), A.now(), m2)
        m = A.do(lambda: s_.activation(S[:, 0:2, :], BKN[:, 2:4, :], ACT.Square))
        V.wait(V.now())
        ra, rb, col = (RA, cosA, sinA), (RB, cosB, sinB), self.col
        squares = [(k, S[:, 2 + k, :]) for k in range(5)] + [(11 + k, S[:, 7 + k, :]) for k in range(6)] + \
            [(9, S[:, 13, :]), (10, S[:, 13, :])] + [(5 + k, S[:, (14, 15, 0, 1)[k], :]) for k in range(4)]
        outs = [(k, AQ[:, k, :], col("aqn"), AQ[:, k, :], ra, None) for k in range(4)] + \
            [(4, AK[:, 0, :], col("akn"), AK[:, 0, :], ra, None)] + \
            [(5 + k, BKN[:, k, :], col("bkn"), BKN[:, k, :], None, None) for k in range(4)] + \
            [(9 + k, KR[:, 0, :], col("bkr"), BKR[:, k, :], rb, None) for k in range(2)] + \
            [(11 + k, BQN[:, k, :], col("bqn"), BQN[:, k, :], None, None) for k in range(4)] + \
            [(15 + k, BQR[:, k, :], col("bqr"), BQR[:, k, :], rb, None) for k in range(2)]
        self.headnorms(N, squares, outs, sel[0:ROWS, NSEL * (ROWS + P):], sel, rs, nt2, m)
        self.bounds()

        wk = Arena(self.arena, 2 * KT * N)
        qm, kn, kr, vb = tmp(2, 2, 2, N), wk(2, N), wk(N), wk(2, 4, P)
        sc = (tmp(2, N), tmp(2, N), tmp(2, 4), None)

        def streams(p, e, q, k, v):
            bank = self.bank[6 + p]
            for qb in range(4):
                k0, tb0 = (0, 0) if qb < 2 else (T, 2)
                yield (tuple(a[:, P * qb:P * qb + P] for a in q), tuple(a[:, k0:N] for a in k), N - k0,
                       [v[:, tb, 64 * e:64 * e + 64] for tb in range(tb0, 4)],
                       bank[64 * e:64 * e + 64, P * qb:P * qb + P], None,
                       {(0, 0): ("first", p), (1, 3): ("last", p)}.get((e, qb)))

        def heads(r, first, Q, rope):
            for q in (V, A):
                q.wait(ctl.last("pair_p"))
            tile = lambda x, i: x[:, bass.ds(i, 1), :].rearrange("p a t -> p (a t)")
            if rope:
                V.do(lambda: v_.tensor_copy(kr, tile(BKR, r)))
            units = []
            for p in range(2):
                for e in range(2):
                    V.do(lambda: v_.tensor_scalar(qm[:, p, 0, e, :], tile(Q, r * 2 + p),
                                                  self.col("half", e), None, MUL))
                    if rope:
                        V.do(lambda: v_.tensor_scalar(qm[:, p, 1, e, :], tile(BQR, r),
                                                      self.col("quart", 2 * p + e), None, MUL))
                if rope:
                    V.do(lambda: v_.tensor_copy(kn[:, p, :], tile(BKN, r * 2 + p)))
                    V.do(lambda: v_.tensor_copy(vb[:, p, :, :], BV[:, :, bass.ds((r * 2 + p) * P, P)]))
                for e in range(2):
                    q, k, v = ((qm[:, p, 0, e, :],), (AK[:, 0, :],), AV) if not rope else \
                        ((qm[:, p, 0, e, :], qm[:, p, 1, e, :]), (kn[:, p, :], kr), vb[:, p, :, :])
                    units += streams(p, e, q, k, v)
            P_.wait(V.now())

            def pair(p, m):
                out = att[:, bass.ds(r * 2 + p + first, 1), :].rearrange("p a t -> p (a t)")
                ctl.note(f"pair{p}", A.do(lambda: s_.copy(out, self.bank[6 + p][:, :]), m))

            self.softmax_units(units, (96 if rope else 64) ** -0.5, sc, pair)
            ctl.note("pair_p", P_.now())

        engines = [ENG.PE, ENG.DVE, ENG.Activation]
        ctl.straight.clear()
        ctl.loop_over(2, engines, lambda r: heads(r, 0, AQ, False))
        self.bounds()
        ctl.loop_over(2, engines, lambda r: heads(r, 4, BQN, True))
        self.bounds()

    def mixer_out(self, l, att, nt):
        up = self.EIGHTS
        with self.scope(w_hi=(4, SLOT // 2), w_lo=(4, SLOT // 2), x_hi=(KT, nt), x_lo=(KT, nt)):
            self.split_part(0, up, 0)
            self.P.wait(self.split_input("x", att, KT, None))
            self.split_part(0, up, 1)
            for m in range(KT):
                o, e = self.bank[m][:, 0:nt], m % 2
                if m < KT - 2:
                    self.split_part(1, up, e)
                done = self.product_split(o, e, KT, self.halves("x"))
                self.gated_sum(o, l, 5, m, nt, done)
            self.bounds()

    def mixer_cd(self):
        P_, V, A, Gq, nc, ctl, t = self.P, self.V, self.A, self.G, self.nc, self.ctl, self.t
        v_, s_, tt, bank = nc.vector, nc.scalar, nc.vector.tensor_tensor, self.bank
        N = 2 * T
        tmp = Arena(self.arena, self.arena_size)
        DQ, DK, IV, DV = tmp(4, T), tmp(4, N), tmp(4, 512), tmp(4, 512)
        Q, GT, ZF, ZB = tmp(4, T), tmp(4, T), tmp(4, N), tmp(4, N)
        att = tmp(KT, T)
        sel, rs = (self.arena[:, self.arena_size - n:][:, 0:w] for n, w in
                   ((NSEL * (ROWS + P) + 1 + N, NSEL * (ROWS + P) + 1), (N, N)))
        self.misc.start(self.G, sel, t["selectors"][:, :])
        up = Arena(self.arena, self.arena_size)
        up.at = self.arena_size - (NSEL * (ROWS + P) + 1 + N) - 9 * N
        bias, nm = up(8, 2, T), up(2, T)
        self.misc.start(Gq, bias.rearrange("p a b c -> p (a b c)"), t["d_bias"][:, :])
        self.misc.start(Gq, nm.rearrange("p b c -> p (b c)"), t["d_mask"][:, :])
        places = [(ZF[:, k, :], N) for k in range(4)] + [(ZB[:, k, :], N) for k in range(4)] + \
            [(DK[:, k, :], N) for k in range(4)] + [(Q[:, k, :], T) for k in range(4)] + \
            [(GT[:, k, :], T) for k in range(4)] + [(DQ[:, k, :], T) for k in range(4)]
        with self.scope(**self.IN_BOXES):
            act = Arena(self.arena, self.arena_size)(4, N)
            up, x_at = self.EIGHTS, self.halves("x")
            self.split_part(0, up, 0)
            self.modulated_split(1, 1, N, act, rs)
            free = [None] * 8
            for m in range(24):
                b, e, (dst, n) = m % 8, m % 2, places[m]
                P_.wait(free[b])
                self.split_part(e, up, 1 - e)
                done = self.product_split(bank[b][:, 0:n], e, KT, lambda k: (a[:, 0:n] for a in x_at(k)))
                if 12 <= m < 20:
                    free[b] = A.do(lambda: s_.activation(dst, bank[b][:, 0:n], ACT.Silu), done)
                else:
                    free[b] = V.do(lambda: v_.tensor_copy(dst, bank[b][:, 0:n]), done)
            for f in free:
                P_.wait(f)
            for m in range(8):
                n, q, e = m // 4, m % 4, m % 2
                if m < 7:
                    self.split_part(e, up, 1 - e)
                done = self.values_split(
                    e, 2, lambda tb: bank[4 * n + tb][:, :],
                    lambda k, tb: (a[:, P * tb:P * tb + P] for a in x_at(2 * q + k)), q == 0, q == 3, e == 1)
                if q == 3:
                    for tb in range(4):
                        A.do(lambda: s_.copy((IV, DV)[n][:, tb, :], bank[4 * n + tb][:, :]), done)
            self.bounds()
        with self.scope():
            self.attention_cd(att, (DQ, DK, IV, DV, Q, GT, ZF, ZB), sel, rs, bias, nm)
        self.mixer_out(1, att, T)

    def attention_cd(self, att, tiles, sel, rs, bias, nm):
        P_, V, A, Gq, nc, ctl, t = self.P, self.V, self.A, self.G, self.nc, self.ctl, self.t
        v_, s_, tt, bank = nc.vector, nc.scalar, nc.vector.tensor_tensor, self.bank
        N = 2 * T
        DQ, DK, IV, DV, Q, GT, ZF, ZB = tiles
        wk = Arena(self.arena, self.arena_size)
        masks = wk(16, P)
        got = self.misc.start(Gq, masks.rearrange("p a b -> p (a b)"), t["h_masks"][:, :])
        for q in (V, P_, A):
            q.wait(got)
        KY, PS, SS = wk(4, N), wk(4, N), wk(4, N)
        M, Mq = wk(4, T), wk(4, T)
        AT = wk(16, P)
        khT = wk(3, 4, P)
        ST, lbt, zero = wk(4, P), wk(8), wk(512)
        flat = lambda ap: ap.rearrange("p a b -> p (a b)")
        V.do(lambda: v_.memset(zero, 0.0))
        d = self.cols[:, COLS["lb1"]:COLS["lb1"] + 8]
        d0 = self.cols[:, COLS["lb0"]:COLS["lb0"] + 8]
        lb, ol = wk(8), wk(8)
        V.do(lambda: tt(lbt, d, d0, SUB))
        A.do(lambda: s_.activation(lb, lbt, ACT.Sigmoid), V.now())
        m = A.do(lambda: s_.activation(ol, lbt, ACT.Sigmoid, scale=-1.0))
        V.wait(m)
        P_.wait(V.now())
        OB = [bank[6], bank[7]]
        for b in OB:
            P_.quiet(lambda: nc.tensor.matmul(b[:, :], zero[:, 0:P], zero, start=True, stop=False,
                                              skip_group_check=True))
        outp = lambda i, e, tb: OB[i // 2][64 * e:64 * e + 64, T * (i % 2) + P * tb:T * (i % 2) + P * tb + P]

        def add(out, lhsT, rhs):
            return lambda: nc.tensor.matmul(out, lhsT, rhs, start=False, stop=False,
                                            skip_group_check=True)

        for dr, Z in enumerate((ZF, ZB)):
            a1 = A.do(lambda: s_.activation(flat(PS), flat(Z), ACT.Sigmoid), V.now(), P_.now())
            a2 = A.do(lambda: s_.activation(flat(KY), flat(Z), ACT.Sigmoid, scale=-1.0))
            for k in range(4):
                c = 4 * dr + k
                V.do(lambda: v_.tensor_scalar(PS[:, k, :], PS[:, k, :], ol[:, c:c + 1], lb[:, c:c + 1],
                                              MUL, ADD), a1)
            for k in range(4):
                c = 4 * dr + k
                V.do(lambda: v_.tensor_scalar(KY[:, k, :], KY[:, k, :], ol[:, c:c + 1], None, MUL), a2)
            V.do(lambda: v_.tensor_scalar(flat(PS), flat(PS), 1.1e-19, None, MAX), V.now())
            m = A.do(lambda: s_.activation(flat(PS), flat(PS), ACT.Ln), V.now())
            V.do(lambda: v_.memset(flat(SS), 0.0))
            V.wait(m)
            A.wait(m)
            A.wait(V.now())
            tg, so = (1, 0) if dr == 0 else (0, 1)

            def prepare(lv, before):
                h, W = 1 << lv, (M, Mq)[lv % 2]
                halves = lambda ap, n: ap.rearrange("p a (b two h) -> p (a b) two h", two=2, h=h) \
                    if n == N else ap[:, :, 0:T].rearrange("p a (b two h) -> p a b two h", two=2, h=h)
                x4 = lambda ap, w: halves(ap, T)[:, :, :, w, :]
                A.wait(before)
                A.do(lambda: s_.activation(x4(W, tg), x4(PS, tg), ACT.Exp), V.now())
                m = A.do(lambda: s_.activation(x4(W, so), x4(SS, so), ACT.Exp))
                V.do(lambda: tt(x4(W, tg), x4(W, tg), x4(Q, tg), MUL), m)
                mq = V.do(lambda: tt(x4(W, so), x4(W, so), x4(KY, so), MUL))
                p, s = halves(PS, N), halves(SS, N)
                last = (h - 1) if dr == 0 else 0
                n = 4 * N // (2 * h)
                tot = lambda w: p[:, :, w, last:last + 1].broadcast_to([P, n, h])
                V.do(lambda: tt(s[:, :, so, :], s[:, :, so, :], tot(tg), ADD))
                V.do(lambda: tt(p[:, :, tg, :], p[:, :, tg, :], tot(so), ADD), V.now())
                return mq

            def score(mask, lhs, rhs, after, meanwhile):
                P_.wait(after)
                scored, masked = [], []
                for e in range(2):
                    rows = slice(64 * e, 64 * e + 64)
                    for i in range(4):
                        for tb in range(2):
                            u, tk = i * 2 + tb, slice(P * tb, P * tb + P)
                            o = bank[2 * e + u // 4][:, P * (u % 4):P * (u % 4) + P]
                            m = P_.do(self.mm(o, lhs[rows, i, tk], rhs[rows, i, tk], True, True))
                    scored.append(m)
                ready = meanwhile()
                for e in range(2):
                    for q in (2 * e, 2 * e + 1):
                        a = V.do(lambda: tt(AT[:, 4 * q:4 * q + 4, :],
                                            bank[q][:, :].rearrange("p (u t) -> p u t", u=4),
                                            bc(masks[:, mask, :], 4), MUL), scored[e])
                    masked.append(a)
                for e in range(2):
                    P_.wait(masked[e])
                    for i in range(4):
                        for tb in range(2):
                            m = P_.do(add(outp(i, e, tb), IV[:, tb, P * i + 64 * e:P * i + 64 * e + 64],
                                          AT[:, 8 * e + 2 * i + tb, :]))
                return scored[1], m, ready

            before, used, ready = score(14, KY, Q, V.now(), lambda: prepare(0, P_.now()))
            for lv in range(7):
                W, seen = (M, Mq)[lv % 2], before
                following = (lambda: prepare(lv + 1, seen)) if lv < 6 else lambda: None
                before, used, ready = score(lv + 7 * dr, W, W, ready, following)
            V.wait(V.now())
            m = A.do(lambda: s_.activation(flat(SS), flat(SS), ACT.Exp), V.now())
            a1 = A.do(lambda: s_.activation(M[:, :, :], PS[:, :, 0:T], ACT.Exp), used)
            kh = V.do(lambda: tt(flat(SS), flat(SS), flat(KY), MUL), m)
            qh = V.do(lambda: tt(flat(Mq), flat(M), flat(Q), MUL), a1)
            order = (2, 3, 0, 1) if dr == 0 else (3, 2, 1, 0)
            P_.wait(kh)
            for n, b in enumerate(order[:3]):
                for i in range(4):
                    m = P_.do(lambda: nc.tensor.transpose(bank[n][:, P * i:P * i + P],
                                                          SS[:, i, P * b:P * b + P], self.ident[:, :]))
                A.do(lambda: s_.copy(flat(khT[:, n, :, :]), bank[n][:, :]), m)
            P_.wait(A.now())
            for n, b in enumerate(order[:3]):
                for i in range(4):
                    m = P_.do(self.mm(bank[3 + n][:, P * i:P * i + P], khT[:, n, i, :],
                                      IV[:, b, P * i:P * i + P], True, True))
            V.do(lambda: v_.memset(flat(ST), 0.0), m)
            V.wait(V.now())
            for n, b in enumerate(order):
                end = P * b + (P - 1 if dr == 0 else 0)
                if n >= 1:
                    pb = order[n - 1]
                    pe = P * pb + (P - 1 if dr == 0 else 0)
                    if n == 1:
                        V.do(lambda: v_.memset(zero[:, 0:8], 0.0))
                    for i in range(4):
                        V.do(lambda: v_.tensor_copy(lbt[:, i:i + 1], PS[:, i, pe:pe + 1]), V.now())
                    w = A.do(lambda: s_.activation(lbt[:, 4:8], lbt[:, 0:4], ACT.Exp), V.now())
                    V.wait(P_.now())
                    for e in range(2):
                        rw = slice(64 * e, 64 * e + 64)
                        for i in range(4):
                            sd = ST[rw, i, 64 * e:64 * e + 64]
                            u = bank[2 + n][rw, P * i + 64 * e:P * i + 64 * e + 64]
                            V.do(lambda: v_.scalar_tensor_tensor(sd, sd, lbt[rw, 4 + i:5 + i], u, MUL, ADD), w)
                if n >= 2:
                    P_.wait(V.now())
                    for i in range(4):
                        o = OB[i // 2][:, T * (i % 2) + P * b:T * (i % 2) + P * b + P]
                        m = P_.do(add(o, ST[:, i, :], Mq[:, i, P * b:P * b + P]))
            self.bounds()
        for b in OB:
            m = P_.do(lambda: nc.tensor.matmul(b[:, :], zero[:, 0:P], zero, start=False, stop=True,
                                               skip_group_check=True))
        O = M
        for k in range(2):
            V.do(lambda: v_.tensor_copy(flat(O[:, 2 * k:2 * k + 2, :]), OB[k][:, :]), m)
        V.wait(V.now())
        gated = lambda k: lambda f: V.do(lambda: tt(att[:, k, :], O[:, k, :], GT[:, k, :], MUL), f)
        sqq = [AT[:, 4 * k:4 * k + 4, :].rearrange("p a b -> p (a b)") for k in range(2)]
        A.do(lambda: s_.activation(flat(Mq), flat(O), ACT.Square), V.now(), P_.now())
        for k in range(2):
            m = A.do(lambda: s_.activation(sqq[k], flat(DQ[:, 2 * k:2 * k + 2, :]), ACT.Square))
        self.headnorms(T, [(5 + k, Mq[:, k, :]) for k in range(4)] +
                       [(k, sqq[k // 2][:, T * (k % 2):T * (k % 2) + T]) for k in range(4)],
                       [(5 + k, O[:, k, :], self.col("cgn"), O[:, k, :], None, gated(k)) for k in range(4)] +
                       [(k, DQ[:, k, :], self.col("dqn"), DQ[:, k, :], None, None) for k in range(4)],
                       1.0 / 64, sel, rs, None, m)
        m = A.do(lambda: s_.activation(flat(KY), flat(DK), ACT.Square))
        P_.wait(V.now())
        self.headnorms(N, [(5 + k, KY[:, k, :]) for k in range(4)],
                       [(5 + k, DK[:, k, :], self.col("dkn"), DK[:, k, :], None, None) for k in range(4)],
                       1.0 / 64, sel, rs, None, m)
        self.bounds()
        wk = Arena(self.arena, self.arena_size)
        qm, kn, vb, bi = wk(2, 2, T), wk(2, N), wk(2, 4, P), wk(4, 2, T)
        sc = (wk(2, N), wk(2, N), wk(2, 4), wk(2, N))
        V.do(lambda: tt(bias.rearrange("p a b c -> p a (b c)"), bias.rearrange("p a b c -> p a (b c)"),
                        bc(nm.rearrange("p b c -> p (b c)"), 8), ADD))
        V.wait(V.now())

        def heads(i):
            for q in (V, A):
                q.wait(ctl.last("pair_p"))
            for p in range(2):
                V.wait(ctl.last(f"pair{p}"))
            tile = lambda x, k: x[:, bass.ds(k, 1), :].rearrange("p a t -> p (a t)")
            units = []
            for p in range(2):
                for e in range(2):
                    V.do(lambda: v_.tensor_scalar(qm[:, p, e, :], tile(DQ, i * 2 + p), self.col("half", e),
                                                  None, MUL))
                V.do(lambda: v_.tensor_copy(kn[:, p, :], tile(DK, i * 2 + p)))
                V.do(lambda: v_.tensor_copy(vb[:, p, :, :], DV[:, :, bass.ds((i * 2 + p) * P, P)]))
                units += [((qm[:, p, e, P * qb:P * qb + P],), (kn[:, p, :],), N,
                           [vb[:, p, tb, 64 * e:64 * e + 64] for tb in range(4)],
                           bank[6 + p][64 * e:64 * e + 64, P * qb:P * qb + P], bi[:, 2 * p + e, qb, :],
                           {(0, 0): ("first", p), (1, 1): ("last", p)}.get((e, qb)))
                          for e in range(2) for qb in range(2)]
            V.do(lambda: v_.tensor_copy(bi[:, :, :, :], bias[:, bass.ds(i * 4, 4), :, :]))
            P_.wait(V.now())
            V.wait(V.now())

            def pair(p, m):
                out = att[:, bass.ds(i * 2 + 4 + p, 1), :].rearrange("p a t -> p (a t)")
                ctl.note(f"pair{p}", A.do(lambda: s_.copy(out, bank[6 + p][:, 0:T]), m))

            self.softmax_units(units, 64 ** -0.5, sc, pair)
            ctl.note("pair_p", P_.now())

        ctl.straight.clear()
        ctl.loop_over(2, [ENG.PE, ENG.DVE, ENG.Activation], heads)
        self.bounds()


def build(nc, t, parts, dumps=()):
    with ExitStack() as es:
        m = Machine(nc, t, es)
        g = m.G
        first = Load(m.ctl, m.sem("s_first"), "first")
        for dst, name in ((m.cols, "cols"), (m.ident, "ident"), (m.ones, "ones"), (m.blk64, "blk64")):
            got = first.start(g, dst[:, :], t[name][:, :])
        got = first.start(g, m.H[:, :, 0:T], t["x"])
        for q in (m.P, m.V, m.A, g):
            q.wait(got)
        names = [s for p in parts for s in PART_STAGES[p]]
        m.feed(names)
        for p in parts:
            kind, l = p[:-1], int(p[-1])
            if kind == "ffn":
                with m.scope(w_hi=(2, SLOT // 2), w_lo=(2, SLOT // 2), x_hi=(KT, 2 * T), x_lo=(KT, 2 * T),
                             u_hi=(FT, 2 * T), u_lo=(FT, 2 * T)):
                    m.ffn(l // 2, l % 2)
            elif kind == "conv":
                with m.scope(**m.BOXES):
                    m.conv_layer(l)
            else:
                room = {"ab": 22600, "cd": 23300}.get(kind)
                with m.scope(room):
                    {"ssm": lambda: m.ssm_layer(l), "rwkv": lambda: m.rwkv_layer(l), "ada": m.ada,
                     "ab": m.mixer_ab, "cd": m.mixer_cd}[kind]()
                if kind in ("ssm", "rwkv"):
                    with m.scope(**m.BOXES):
                        m.tail(l, "sc" if kind == "ssm" else None)
        m.bounds(m.S)
        s_out = m.sem("s_out")
        m.S.eng.dma_start(t["out"], m.H[:, :, 0:T]).then_inc(s_out, 16)
        m.S.eng.wait_ge(s_out, 16)
        for n, (name, ap) in enumerate(m.dumps if dumps else ()):
            m.S.eng.dma_start(t[name], ap).then_inc(s_out, 16)
            m.S.eng.wait_ge(s_out, 16 * (n + 2))


PART_STAGES = {
    "conv0": ["conv_in0", "out0", "ple0"], "ssm1": ["ssm_in", "ada_s", "glu", "out1", "ple1"],
    "rwkv2": ["lora", "rkvz", "ada_r", "out2", "ple2"], "conv3": ["conv_in3", "out3", "ple3"], "ada0": [],
    "ffn0": ["f00a", "f00b"], "ab0": ["ab_in", "ab_av", "ukv", "ab_out"], "ffn1": ["f01a", "f01b"],
    "ffn2": ["f10a", "f10b"], "cd0": ["cd_in", "cd_v", "cd_out"], "ffn3": ["f11a", "f11b"],
}
PARTS = ["conv0", "ssm1", "rwkv2", "conv3", "ada0", "ffn0", "ab0", "ffn1", "ffn2", "cd0", "ffn3"]


def tiles(w, order):
    return np.concatenate([w[k * P:(k + 1) * P, m * P:(m + 1) * P] for k, m in order], axis=1)


def whole(w, per=2):
    nk, nm = w.shape[0] // P, w.shape[1] // P
    return np.stack([tiles(w, [(k, m) for m in range(c, c + per) for k in range(nk)])
                     for c in range(0, nm, per)])


def fcol(v):
    return np.ascontiguousarray(v.reshape(-1, P).T)


def fmajor(a):
    return np.ascontiguousarray(a.T.reshape(-1, P, a.shape[0]).transpose(1, 0, 2))


def lay_out(inp):
    o = {}
    o["x"] = fmajor(inp["x"][0])
    o["p"] = np.stack([fmajor(inp["p"][l, 0]) for l in range(DEPTH1)])
    for l in (0, 3):
        w = inp["conv_w_in"][l // 3]
        bg, cg, h, z = (w[:, k * D:(k + 1) * D] for k in range(4))
        o[f"conv_in{l}"] = np.concatenate([
            np.stack([np.concatenate([tiles(a, [(k, m) for k in range(KT)]) for a in ab], axis=1)
                      for ab in ((cg, h), (bg, z))]) for m in range(KT)])
        o[f"out{l}"] = whole(inp["conv_w_out"][l // 3])
    for l in range(DEPTH1):
        o[f"ple{l}"] = np.stack([np.concatenate([
            tiles(inp["ple_gate"][l], [(k, m) for k in range(KT)]),
            tiles(inp["ple_proj"][l], [(k, m) for k in range(2)])], axis=1) for m in range(KT)])
    c = np.zeros((P, NCOL), np.float32)

    def put(name, a):
        c[:, COLS[name]:COLS[name] + a.shape[1]] = a

    put("conv_k", np.concatenate([fcol(inp["conv_k"][j, s]) for j in range(2) for s in range(3)], 1))
    put("ln_g", np.concatenate([fcol(inp["ln_g"][l]) for l in range(4)], 1))
    put("ln_b", np.concatenate([fcol(inp["ln_b"][l]) for l in range(4)], 1))
    lay_out_more(inp, o, put)
    o["cols"] = c
    o["ident"] = np.eye(P, dtype=np.float32)
    o["ones"] = np.ones((P, P), np.float32)
    o["blk64"] = np.kron(np.eye(2), np.ones((64, 64))).astype(np.float32)
    return o


def lay_out_more(inp, o, put):
    o["ssm_in"], o["glu"] = whole(inp["ssm_w_in"][0]), whole(inp["ssm_w_glu"][0])
    o["out1"] = whole(inp["ssm_w_out"][0])
    twice = lambda a: np.ascontiguousarray(np.concatenate([a.T, a.T]))
    o["s_lre"], o["s_lim"] = twice(inp["ssm_lam_re"][0]), twice(inp["ssm_lam_im"][0])
    o["s_ldt"] = np.ascontiguousarray(np.broadcast_to(inp["ssm_log_dt"][0][None], (P, G)))
    br, bi = (inp[n][0].transpose(1, 0, 2).reshape(NP_, G * GH) for n in ("ssm_b_re", "ssm_b_im"))
    cr, ci = (inp[n][0].transpose(2, 0, 1).reshape(NP_, G * GH) for n in ("ssm_c_re", "ssm_c_im"))
    o["s_b1"], o["s_b2"] = np.concatenate([br, bi]), np.concatenate([bi, br])
    o["s_c1"], o["s_c2"] = np.concatenate([cr, ci]), np.concatenate([ci, cr])
    put("ssm_d", fcol(inp["ssm_d"][0]))
    put("b_glu", fcol(inp["ssm_b_glu"][0]))
    put("sgn", np.concatenate([-np.ones((64, 1)), np.ones((64, 1))]))
    o["rkvz"] = np.concatenate([whole(inp["rwkv_w_rkvz"][0, n]) for n in range(4)])
    o["out2"] = whole(inp["rwkv_w_out"][0])
    low = lambda w: w.reshape(KT, P, 64).transpose(1, 0, 2).reshape(P, 512)
    o["lora"] = np.concatenate([low(inp["rwkv_w1"][0]), low(inp["rwkv_a1"][0]),
                                np.concatenate([inp["rwkv_w2"][0], inp["rwkv_a2"][0]])], axis=1)[None]
    put("mu", np.concatenate([fcol(inp["rwkv_mu"][0, n]) for n in range(6)], 1))
    for name in ("w0", "a0", "k_k", "k_a", "r_k", "lnx_g", "lnx_b"):
        put(name, fcol(inp["rwkv_" + name][0]))
    put("half", np.kron(np.eye(2), np.ones((64, 1))))
    s_, t_ = np.meshgrid(np.arange(P), np.arange(P), indexing="ij")
    chunk = s_ // 64 == t_ // 64

    def joins(lv):
        return (s_ >> (lv + 1) == t_ >> (lv + 1)) & ((t_ >> lv) % 2 == 1) & ((s_ >> lv) % 2 == 0)

    o["r_masks"] = np.concatenate(
        [chunk & (s_ < t_), chunk & (s_ <= t_), (chunk & (s_ < t_)).T, joins(0).T, joins(0)]
        + [joins(lv) for lv in range(1, 6)], axis=1).astype(np.float32)
    o["ctx"] = fmajor(inp["ctx_2"][0])
    c2 = np.stack([inp["c_2"][0].reshape(KT, P), inp["c_ctx_2"].reshape(KT, P)], axis=-1)
    put("c", c2.transpose(1, 0, 2).reshape(P, 2 * KT))
    ada = np.concatenate([inp["ada_w_2"][l].reshape(2, 4, P, -1, 512).transpose(3, 0, 2, 1, 4)
                          .reshape(-1, P, 2048) for l in range(DEPTH2)])
    o["ada_s"], o["ada_r"] = ada[:2 * ADA_SSM], ada[2 * ADA_SSM:]
    put("ada_b", np.concatenate([fcol(inp["ada_b_2"][l]) for l in range(DEPTH2)], 1))
    put("norm_g", np.concatenate([fcol(inp["norm_g_2"][l, s]) for l in range(2) for s in range(3)], 1))
    for l in range(DEPTH2):
        for s in range(2):
            w1, w3, w2 = (inp[n][l, s] for n in ("ffn_w1_2", "ffn_w3_2", "ffn_w2_2"))
            o[f"f{l}{s}a"] = np.concatenate([whole(w1, 1), whole(w3, 1)], axis=2)
            o[f"f{l}{s}b"] = whole(w2, 1).reshape(KT, P, 2, FT // 2 * P).transpose(0, 2, 1, 3).reshape(
                2 * KT, P, FT // 2 * P)
    w = inp["ab_w_in_2"][0]
    ab = {}
    at = 0
    for name, n in (("aq", 512), ("ak", 128), ("av", 128), ("bq", 768), ("bkv", 256), ("bkr", 32)):
        ab[name] = w[:, at:at + n]
        at += n
    perm = [h for i in range(4) for h in (i, i + 4)]
    aq = ab["aq"].reshape(D, 8, 64)[:, perm].reshape(D, 512)
    bq = ab["bq"].reshape(D, 8, 96)
    o["ab_in"] = whole(np.concatenate([aq, ab["ak"], bq[:, :, :64].reshape(D, 512),
                                       bq[:, :, 64:].reshape(D, 256), ab["bkv"],
                                       np.tile(ab["bkr"], (1, 4))], axis=1))
    o["ab_av"] = moving(ab["av"])[None]
    u = inp["ab_b_wukv_2"][0].reshape(256, 8, 128)
    o["ukv"] = np.concatenate([tiles(u[:, :, :64].reshape(256, 512), [(k, m) for m in range(4) for k in (0, 1)]),
                               moving(u[:, :, 64:].reshape(256, 512))], axis=1)[None]
    wo = inp["ab_w_out_2"][0]
    o["ab_out"] = whole(np.concatenate([wo[:512].reshape(8, 64, D)[perm].reshape(512, D), wo[512:]]))
    put("aqn", np.tile(inp["ab_a_qn_2"][0], 2)[:, None])
    put("akn", np.tile(inp["ab_a_kn_2"][0], 2)[:, None])
    for name, g in (("bq", inp["ab_b_qn_2"][0]), ("bk", inp["ab_b_kn_2"][0])):
        put(name + "n", np.tile(g[:64], 2)[:, None])
        put(name + "r", np.tile(g[64:], 4)[:, None])
    put("kvn", fcol(inp["ab_b_kvn_2"][0]))
    put("quart", np.kron(np.eye(4), np.ones((32, 1))))
    f = np.arange(P)

    def rotate(hb):
        r = np.zeros((P, P))
        for d in range(P):
            if d % hb < hb // 2:
                r[d + hb // 2, d] = -1
            else:
                r[d - hb // 2, d] = 1
        return r

    def rope(dim):
        inv = np.float32(10000.0) ** (-np.arange(0, dim // 2, 2, dtype=np.float32) / np.float32(dim // 2))
        pos = np.arange(T)
        ang = np.concatenate([np.concatenate([a, a], 1) for a in
                              ((pos // 64)[:, None] * inv[None], (pos % 64)[:, None] * inv[None])], 1)
        ang = np.tile(ang.astype(np.float32).T, (P // dim, 1))
        return [np.cos(ang), np.sin(ang)]

    o["ab_consts"] = np.concatenate(
        [rotate(32), rotate(16)] + rope(64) + rope(32), axis=1).astype(np.float32)
    first = [2 * k + f // 64 for k in range(5)]
    kind = [2 * k + f // 64 for k in range(4)] + [4 * k + f // 32 for k in range(2)]
    row = np.stack(first + [10 + r for r in kind] + [18 + r for r in kind])
    sel = (row[:, :, None] == np.arange(ROWS)).transpose(1, 0, 2)
    back = np.zeros((P, NSEL, P))
    back[:ROWS] = sel.transpose(2, 1, 0)
    per = np.where(np.arange(P) < 10, 1 / 64, 1 / 96)
    o["selectors"] = np.concatenate([sel.reshape(P, -1), back.reshape(P, -1), per[:, None]],
                                    axis=1).astype(np.float32)

    w = inp["cd_w_in_2"][0]
    q, zf, zb, iv, gate, dq, dk, dv = (w[:, 512 * k:512 * k + 512] for k in range(8))
    o["cd_in"] = whole(np.concatenate([zf, zb, dk, q, gate, dq], axis=1))
    o["cd_v"] = np.concatenate([moving(a).reshape(P, 2, 4 * 512).transpose(1, 0, 2) for a in (iv, dv)])
    o["cd_out"] = whole(inp["cd_w_out_2"][0])
    for n in range(2):
        put(f"lb{n}", np.concatenate([fcol(inp["hgrn_lb_2"][n, d]) for d in range(2)], 1))
    for name, key in (("cgn", "cd_c_gn_2"), ("dqn", "cd_d_qn_2"), ("dkn", "cd_d_kn_2")):
        put(name, np.tile(inp[key][0], 2)[:, None])
    none = np.zeros((P, P))
    o["h_masks"] = np.concatenate([joins(lv) for lv in range(7)] + [joins(lv).T for lv in range(7)]
                                  + [np.eye(P), none], axis=1).astype(np.float32)
    tok = np.arange(T)
    row, col = tok // 64, tok % 64
    start = np.clip(col - 8, 0, 48)
    inside = (col[None] >= start[:, None]) & (col[None] < start[:, None] + 16)
    dr = row[None] - row[:, None] + 7
    dc = np.where(inside, col[None] - col[:, None] + 15, 0)
    rpb = np.where(inside[None], inp["cd_d_rpb_2"][0][:, dr, dc], np.float32(0))
    o["d_bias"] = np.ascontiguousarray(rpb.reshape(8, 2, P, T).transpose(2, 0, 1, 3).reshape(P, -1))
    o["d_mask"] = np.where(inside, 0, NEG).astype(np.float32).reshape(2, P, T).transpose(
        1, 0, 2).reshape(P, -1)


def moving(w):
    return np.ascontiguousarray(w.reshape(-1, P, w.shape[1]).transpose(1, 0, 2).reshape(P, -1))


def kernel(**inputs):
    import concourse.bacc as bacc
    from concourse.bass_utils import run_bass_kernel_spmd

    arrays = lay_out({k: np.asarray(v) for k, v in inputs.items()})
    nc = bacc.Bacc("TRN2", target_bir_lowering=False, num_devices=1)
    t, send = {}, {}
    for name, a in arrays.items():
        send["in_" + name] = np.ascontiguousarray(a)
        t[name] = nc.dram_tensor("in_" + name, a.shape, F32, kind="ExternalInput").ap()
    for name in ("scratch_u", "scratch_y"):
        t[name] = nc.dram_tensor(name, (D * T,), F32, kind="Internal").ap()
    t["mods"] = nc.dram_tensor("mods", (2, DEPTH2 * 9 * D), F32, kind="Internal").ap()
    t["out"] = nc.dram_tensor("out_x", (P, KT, T), F32, kind="ExternalOutput").ap()
    build(nc, t, PARTS)
    got = run_bass_kernel_spmd(nc, [send], core_ids=[0]).results[0]["out_x"]
    return np.ascontiguousarray(got.transpose(1, 0, 2).reshape(D, T).T)[None]
```
